# Optimizing a Trainium2 kernel written in Bass

```python
import math
import jax, jax.numpy as jnp
from jax import lax
import numpy as np

D_MODEL = 2048
BATCH = 1
SEQ = 256
DEPTH = 1

S5_WIDTH = D_MODEL // 2
S5_GROUP = 16
S5_GROUPS = S5_WIDTH // S5_GROUP
S5_STATE = 64
S5_DT_MIN = 0.001
S5_DT_MAX = 0.1
DN_HEADS = 8
DN_DK = 128
DN_DV = 128
DN_QK_WIDTH = DN_HEADS * DN_DK
DN_V_WIDTH = DN_HEADS * DN_DV
DN_CONV = 4
DN_CHUNK = 64
DN_DT_MIN = 0.001
DN_DT_MAX = 0.1
FFN_DIM = 5632
FFN_CONV = 3
NORM_EPS = 1e-6

OFF_U = S5_WIDTH
OFF_QKV = OFF_U + 2 * DN_QK_WIDTH + DN_V_WIDTH
OFF_Z = OFF_QKV + DN_V_WIDTH
OFF_BETA = OFF_Z + DN_HEADS
OFF_ALPHA = OFF_BETA + DN_HEADS
OFF_GS = OFF_ALPHA + D_MODEL
N_IN = OFF_GS + D_MODEL
SPLITS = [OFF_U, OFF_QKV, OFF_Z, OFF_BETA, OFF_ALPHA, OFF_GS]


def rmsnorm(x, w):
    xf = x.astype(jnp.float32)
    y = xf * lax.rsqrt(jnp.mean(xf * xf, axis=-1, keepdims=True) + NORM_EPS) * w.astype(jnp.float32)
    return y.astype(x.dtype)

def l2norm(x):
    return x * lax.rsqrt(jnp.sum(x * x, axis=-1, keepdims=True) + NORM_EPS)

def causal_dwconv(x, w):
    K, C = w.shape
    return lax.conv_general_dilated(
        x, w[:, None, :].astype(x.dtype), window_strides=(1,), padding=[(K - 1, 0)],
        dimension_numbers=("NWC", "WIO", "NWC"), feature_group_count=C)

def s5_branch(u, log_dt, a_re, a_im, b_re, b_im, c_re, c_im, d):
    Bn, L, _ = u.shape
    f32 = jnp.float32
    uf = u.astype(f32)
    ug = uf.reshape(Bn, L, S5_GROUPS, S5_GROUP)
    lr, li = a_re.astype(f32), a_im.astype(f32)
    dt = jnp.exp(log_dt.astype(f32))[:, None]
    mag = jnp.exp(lr * dt)
    abar_re, abar_im = mag * jnp.cos(li * dt), mag * jnp.sin(li * dt)
    den = lr * lr + li * li
    nr, ni = abar_re - 1.0, abar_im
    coef_re = (nr * lr + ni * li) / den
    coef_im = (ni * lr - nr * li) / den
    br, bi = b_re.astype(f32), b_im.astype(f32)
    bbar_re = coef_re[..., None] * br - coef_im[..., None] * bi
    bbar_im = coef_re[..., None] * bi + coef_im[..., None] * br
    bu_re = jnp.einsum("gph,blgh->blgp", bbar_re, ug)
    bu_im = jnp.einsum("gph,blgh->blgp", bbar_im, ug)
    ar_t = jnp.broadcast_to(abar_re, bu_re.shape)
    ai_t = jnp.broadcast_to(abar_im, bu_re.shape)

    def combine(e1, e2):
        a1r, a1i, b1r, b1i = e1
        a2r, a2i, b2r, b2i = e2
        return (a2r * a1r - a2i * a1i,
                a2r * a1i + a2i * a1r,
                a2r * b1r - a2i * b1i + b2r,
                a2r * b1i + a2i * b1r + b2i)

    _, _, xr, xi = lax.associative_scan(combine, (ar_t, ai_t, bu_re, bu_im), axis=1)
    y = (jnp.einsum("ghp,blgp->blgh", c_re.astype(f32), xr)
         - jnp.einsum("ghp,blgp->blgh", c_im.astype(f32), xi))
    y = y.reshape(Bn, L, S5_WIDTH) + d.astype(f32) * uf
    return jax.nn.gelu(y, approximate=False).astype(u.dtype)

def chunk_gated_delta_rule(q, k, v, g, beta):
    Bn, L, H, DK = q.shape
    DV = v.shape[-1]
    N, C = L // DN_CHUNK, DN_CHUNK

    def chunks(t):
        return t.reshape(Bn, N, C, H, -1).transpose(1, 0, 3, 2, 4)

    qc, kc, vc = chunks(q), chunks(k), chunks(v)
    bc = beta.reshape(Bn, N, C, H).transpose(1, 0, 3, 2)
    gc = jnp.cumsum(g.reshape(Bn, N, C, H).transpose(1, 0, 3, 2), axis=-1)
    tril = jnp.tril(jnp.ones((C, C), dtype=bool))
    strict = jnp.tril(jnp.ones((C, C), dtype=bool), -1)
    decay = jnp.exp(jnp.where(tril, gc[..., :, None] - gc[..., None, :], -jnp.inf))
    k_beta = kc * bc[..., None]
    v_beta = vc * bc[..., None]
    lmat = jnp.where(strict, jnp.einsum("nbhcd,nbhsd->nbhcs", k_beta, kc) * decay, 0.0)
    eye = jnp.eye(C, dtype=q.dtype)
    rhs = jnp.concatenate([v_beta, k_beta * jnp.exp(gc)[..., None]], axis=-1)
    sol = lax.linalg.triangular_solve(eye + lmat, rhs, left_side=True, lower=True, unit_diagonal=True)
    u_c, w_c = sol[..., :DV], sol[..., DV:]
    attn = jnp.where(tril, jnp.einsum("nbhcd,nbhsd->nbhcs", qc, kc) * decay, 0.0)

    def step(S, inp):
        q_i, k_i, u_i, w_i, g_i, a_i = inp
        v_new = u_i - jnp.einsum("bhcd,bhdv->bhcv", w_i, S)
        o_i = (jnp.einsum("bhcd,bhdv->bhcv", q_i * jnp.exp(g_i)[..., None], S)
               + jnp.einsum("bhcs,bhsv->bhcv", a_i, v_new))
        g_last = g_i[..., -1]
        S = (S * jnp.exp(g_last)[..., None, None]
             + jnp.einsum("bhcd,bhcv->bhdv", k_i * jnp.exp(g_last[..., None] - g_i)[..., None], v_new))
        return S, o_i

    S0 = jnp.zeros((Bn, H, DK, DV), q.dtype)
    _, o = lax.scan(step, S0, (qc, kc, u_c, w_c, gc, attn))
    return o.transpose(1, 0, 3, 2, 4).reshape(Bn, L, H, DV)

def deltanet_branch(qkv, z, b_raw, a_raw, conv_w, a_log, dt_bias, norm_w):
    Bn, L, _ = qkv.shape
    f32 = jnp.float32
    qkv = jax.nn.silu(causal_dwconv(qkv, conv_w))
    q, k, v = jnp.split(qkv, [DN_QK_WIDTH, 2 * DN_QK_WIDTH], axis=-1)
    q = l2norm(q.reshape(Bn, L, DN_HEADS, DN_DK).astype(f32)) * (DN_DK ** -0.5)
    k = l2norm(k.reshape(Bn, L, DN_HEADS, DN_DK).astype(f32))
    v = v.reshape(Bn, L, DN_HEADS, DN_DV).astype(f32)
    beta = jax.nn.sigmoid(b_raw.astype(f32))
    g = -jnp.exp(a_log.astype(f32)) * jax.nn.softplus(a_raw.astype(f32) + dt_bias.astype(f32))
    o = chunk_gated_delta_rule(q, k, v, g, beta)
    o = rmsnorm(o, norm_w) * jax.nn.silu(z.reshape(Bn, L, DN_HEADS, DN_DV).astype(f32))
    return o.reshape(Bn, L, DN_V_WIDTH).astype(qkv.dtype)

def first_inputs(seed: int = 0) -> dict:
    key = jax.random.key(seed)
    ks = jax.random.split(key, 26)
    f32 = jnp.float32

    def nrm(k, shape, scale):
        return jax.random.normal(k, shape, f32) * scale

    G, P, HG = S5_GROUPS, S5_STATE, S5_GROUP
    x = nrm(ks[0], (BATCH, SEQ, D_MODEL), 1.0)
    mix_norm_w = 1.0 + nrm(ks[1], (DEPTH, D_MODEL), 0.02)
    w_in = nrm(ks[2], (DEPTH, D_MODEL, N_IN), D_MODEL ** -0.5)
    s5_log_dt = jax.random.uniform(ks[3], (DEPTH, G), f32, math.log(S5_DT_MIN), math.log(S5_DT_MAX))
    s5_a_re = -0.5 + nrm(ks[4], (DEPTH, G, P), 0.01)
    s5_a_im = math.pi * jnp.arange(P, dtype=f32) + nrm(ks[5], (DEPTH, G, P), 0.01)
    s5_b_re = nrm(ks[6], (DEPTH, G, P, HG), (2 * HG) ** -0.5)
    s5_b_im = nrm(ks[7], (DEPTH, G, P, HG), (2 * HG) ** -0.5)
    s5_c_re = nrm(ks[8], (DEPTH, G, HG, P), (2 * P) ** -0.5)
    s5_c_im = nrm(ks[9], (DEPTH, G, HG, P), (2 * P) ** -0.5)
    s5_d = nrm(ks[10], (DEPTH, S5_WIDTH), 1.0)
    s5_glu_w = nrm(ks[11], (DEPTH, S5_WIDTH, 2 * D_MODEL), S5_WIDTH ** -0.5)
    dn_conv_w = nrm(ks[12], (DEPTH, DN_CONV, 2 * DN_QK_WIDTH + DN_V_WIDTH), DN_CONV ** -0.5)
    dn_a_log = jnp.log(jax.random.uniform(ks[13], (DEPTH, DN_HEADS), f32, 1.0, 16.0))
    dn_dt = jnp.exp(jax.random.uniform(ks[14], (DEPTH, DN_HEADS), f32, math.log(DN_DT_MIN), math.log(DN_DT_MAX)))
    dn_dt_bias = dn_dt + jnp.log(-jnp.expm1(-dn_dt))
    dn_norm_w = 1.0 + nrm(ks[15], (DEPTH, DN_DV), 0.02)
    dn_proj_w = nrm(ks[16], (DEPTH, DN_V_WIDTH, D_MODEL), DN_V_WIDTH ** -0.5)
    w_out = nrm(ks[17], (DEPTH, D_MODEL, D_MODEL), D_MODEL ** -0.5)
    ffn_norm_w = 1.0 + nrm(ks[18], (DEPTH, D_MODEL), 0.02)
    ffn_up = nrm(ks[19], (DEPTH, D_MODEL, 2 * FFN_DIM), D_MODEL ** -0.5)
    ffn_conv_w = nrm(ks[20], (DEPTH, FFN_CONV, 2 * FFN_DIM), FFN_CONV ** -0.5)
    ffn_down = nrm(ks[21], (DEPTH, FFN_DIM, D_MODEL), FFN_DIM ** -0.5)
    final_norm_w = 1.0 + nrm(ks[22], (D_MODEL,), 0.02)
    return {"x": x, "mix_norm_w": mix_norm_w, "w_in": w_in, "s5_log_dt": s5_log_dt,
            "s5_a_re": s5_a_re, "s5_a_im": s5_a_im, "s5_b_re": s5_b_re, "s5_b_im": s5_b_im,
            "s5_c_re": s5_c_re, "s5_c_im": s5_c_im, "s5_d": s5_d, "s5_glu_w": s5_glu_w,
            "dn_conv_w": dn_conv_w, "dn_a_log": dn_a_log, "dn_dt_bias": dn_dt_bias,
            "dn_norm_w": dn_norm_w, "dn_proj_w": dn_proj_w, "w_out": w_out,
            "ffn_norm_w": ffn_norm_w, "ffn_up": ffn_up, "ffn_conv_w": ffn_conv_w,
            "ffn_down": ffn_down, "final_norm_w": final_norm_w}

def first_block(x, mix_norm_w, w_in, s5_log_dt, s5_a_re, s5_a_im, s5_b_re, s5_b_im,
              s5_c_re, s5_c_im, s5_d, s5_glu_w, dn_conv_w, dn_a_log, dn_dt_bias,
              dn_norm_w, dn_proj_w, w_out, ffn_norm_w, ffn_up, ffn_conv_w, ffn_down,
              final_norm_w):
    for l in range(DEPTH):
        h = rmsnorm(x, mix_norm_w[l])
        proj = jnp.einsum("bld,de->ble", h, w_in[l])
        u, qkv, z, b_raw, a_raw, g_s5, g_dn = jnp.split(proj, SPLITS, axis=-1)
        y_s5 = s5_branch(u, s5_log_dt[l], s5_a_re[l], s5_a_im[l], s5_b_re[l], s5_b_im[l],
                         s5_c_re[l], s5_c_im[l], s5_d[l])
        glu_a, glu_b = jnp.split(jnp.einsum("blc,ce->ble", y_s5, s5_glu_w[l]), 2, axis=-1)
        br_s5 = glu_a * jax.nn.sigmoid(glu_b)
        y_dn = deltanet_branch(qkv, z, b_raw, a_raw, dn_conv_w[l], dn_a_log[l], dn_dt_bias[l], dn_norm_w[l])
        br_dn = jnp.einsum("blc,cd->bld", y_dn, dn_proj_w[l])
        merged = jax.nn.sigmoid(g_s5) * br_s5 + jax.nn.sigmoid(g_dn) * br_dn
        x = x + jnp.einsum("bld,de->ble", merged, w_out[l])
        h = rmsnorm(x, ffn_norm_w[l])
        up = causal_dwconv(jnp.einsum("bld,df->blf", h, ffn_up[l]), ffn_conv_w[l])
        act, val = jnp.split(up, 2, axis=-1)
        x = x + jnp.einsum("blf,fd->bld", jax.nn.silu(act) * val, ffn_down[l])
    return rmsnorm(x, final_norm_w)


D_MIX = D_MODEL
D_POOL = D_MIX // 2
POOL_WINDOWS = (2, 4, 8, 16)
N_POOL_GROUPS = len(POOL_WINDOWS)
POOL_GROUP_DIM = D_POOL // N_POOL_GROUPS
D_GLA = D_MIX - D_POOL
GLA_HEADS = 4
GLA_DV = D_GLA // GLA_HEADS
GLA_DK_TOTAL = D_GLA // 2
GLA_DK = GLA_DK_TOTAL // GLA_HEADS
GLA_GATE_RANK = 16
GATE_LOGIT_NORMALIZER = 16.0
CHUNK = 64
D_IN = D_POOL + 2 * GLA_DK_TOTAL + 2 * D_GLA + GLA_GATE_RANK
D_FF = 5632
EPS = 1e-6


def rmsnorm_2(x, g):
    xf = x.astype(jnp.float32)
    y = xf * lax.rsqrt(jnp.mean(xf * xf, axis=-1, keepdims=True) + EPS)
    return (y * g.astype(jnp.float32)).astype(x.dtype)

def swiglu(h, w_in, w_out):
    gu = h @ w_in
    gate, up = gu[..., :D_FF], gu[..., D_FF:]
    return (jax.nn.silu(gate) * up) @ w_out

def pool_mixer(u, w_pool, pool_scale):
    B, S, _ = u.shape
    uf = u.astype(jnp.float32).reshape(B, S, N_POOL_GROUPS, POOL_GROUP_DIM)
    cs = jnp.cumsum(uf, axis=1)
    pos1 = jnp.arange(1, S + 1, dtype=jnp.int32)
    means = []
    for gi, w in enumerate(POOL_WINDOWS):
        c = cs[:, :, gi]
        shifted = jnp.pad(c, ((0, 0), (w, 0), (0, 0)))[:, :S]
        cnt = jnp.minimum(pos1, w).astype(jnp.float32)[None, :, None]
        means.append((c - shifted) / cnt)
    pooled = jnp.stack(means, axis=2) - uf
    y = jnp.einsum('bsgc,gcd->bsgd', pooled.astype(u.dtype), w_pool)
    return y.reshape(B, S, D_POOL) * pool_scale

def gla_mixer(q, k, v, g_out, gate_lr, w_alpha, b_alpha, gla_norm):
    B, S, _ = q.shape
    N = S // CHUNK
    log_alpha = jax.nn.log_sigmoid((gate_lr @ w_alpha + b_alpha).astype(jnp.float32)) / GATE_LOGIT_NORMALIZER

    def heads(t, d):
        return t.astype(jnp.float32).reshape(B, N, CHUNK, GLA_HEADS, d).transpose(0, 3, 1, 2, 4)

    qh = heads(q, GLA_DK) * (GLA_DK ** -0.5)
    kh = heads(k, GLA_DK)
    vh = heads(v, GLA_DV)
    bcum = jnp.cumsum(heads(log_alpha, GLA_DK), axis=3)
    b_last = bcum[:, :, :, -1:]
    q_dec = qh * jnp.exp(bcum)
    k_inv = kh * jnp.exp(-bcum)
    k_tail = kh * jnp.exp(b_last - bcum)

    mask = jnp.tril(jnp.ones((CHUNK, CHUNK), dtype=bool))
    scores = jnp.where(mask, jnp.einsum('bhnid,bhnjd->bhnij', q_dec, k_inv), 0.0)
    o_intra = jnp.einsum('bhnij,bhnjv->bhniv', scores, vh)

    kv_chunk = jnp.einsum('bhncd,bhncv->bhndv', k_tail, vh)
    decay_chunk = jnp.exp(b_last[:, :, :, 0])

    def step(state, inp):
        dec, kv = inp
        return state * dec[..., None] + kv, state

    init = jnp.zeros((B, GLA_HEADS, GLA_DK, GLA_DV), jnp.float32)
    _, states = lax.scan(step, init, (decay_chunk.transpose(2, 0, 1, 3), kv_chunk.transpose(2, 0, 1, 3, 4)))
    states = states.transpose(1, 2, 0, 3, 4)
    o = o_intra + jnp.einsum('bhncd,bhndv->bhncv', q_dec, states)

    o = o * lax.rsqrt(jnp.mean(o * o, axis=-1, keepdims=True) + EPS) * gla_norm.astype(jnp.float32)
    o = o.transpose(0, 2, 3, 1, 4).reshape(B, S, D_GLA)
    return (o * jax.nn.silu(g_out.astype(jnp.float32))).astype(q.dtype)

def second_inputs(seed: int = 0) -> dict:
    key = jax.random.key(seed)
    ks = jax.random.split(key, 16)
    f32 = jnp.float32

    def nrm(k, shape, fan_in):
        return jax.random.normal(k, shape, f32) * (fan_in ** -0.5)

    def gain(k, shape):
        return 1.0 + 0.02 * jax.random.normal(k, shape, f32)

    L = DEPTH
    return {
        "x": jax.random.normal(ks[0], (BATCH, SEQ, D_MODEL), f32),
        "ffn1_norm": gain(ks[1], (L, D_MODEL)),
        "ffn1_w_in": nrm(ks[2], (L, D_MODEL, 2 * D_FF), D_MODEL),
        "ffn1_w_out": nrm(ks[3], (L, D_FF, D_MODEL), D_FF),
        "mix_norm": gain(ks[4], (L, D_MODEL)),
        "w_in_mix": nrm(ks[5], (L, D_MODEL, D_IN), D_MODEL),
        "w_pool": nrm(ks[6], (L, N_POOL_GROUPS, POOL_GROUP_DIM, POOL_GROUP_DIM), POOL_GROUP_DIM),
        "pool_scale": 1.0 + 0.1 * jax.random.normal(ks[7], (L, D_POOL), f32),
        "w_alpha": nrm(ks[8], (L, GLA_GATE_RANK, GLA_DK_TOTAL), GLA_GATE_RANK),
        "b_alpha": 0.01 * jax.random.normal(ks[9], (L, GLA_DK_TOTAL), f32),
        "gla_norm": gain(ks[10], (L, GLA_DV)),
        "w_out_mix": nrm(ks[11], (L, D_MIX, D_MODEL), D_MIX),
        "ffn2_norm": gain(ks[12], (L, D_MODEL)),
        "ffn2_w_in": nrm(ks[13], (L, D_MODEL, 2 * D_FF), D_MODEL),
        "ffn2_w_out": nrm(ks[14], (L, D_FF, D_MODEL), D_FF),
        "final_norm": gain(ks[15], (D_MODEL,)),
    }

def second_block(x, ffn1_norm, ffn1_w_in, ffn1_w_out, mix_norm, w_in_mix, w_pool, pool_scale,
              w_alpha, b_alpha, gla_norm, w_out_mix, ffn2_norm, ffn2_w_in, ffn2_w_out, final_norm):
    h = x
    o_q = D_POOL
    o_k = o_q + GLA_DK_TOTAL
    o_v = o_k + GLA_DK_TOTAL
    o_g = o_v + D_GLA
    o_r = o_g + D_GLA
    for l in range(DEPTH):
        h = h + 0.5 * swiglu(rmsnorm_2(h, ffn1_norm[l]), ffn1_w_in[l], ffn1_w_out[l])
        u = rmsnorm_2(h, mix_norm[l]) @ w_in_mix[l]
        y_pool = pool_mixer(u[..., :o_q], w_pool[l], pool_scale[l])
        y_gla = gla_mixer(u[..., o_q:o_k], u[..., o_k:o_v], u[..., o_v:o_g], u[..., o_g:o_r],
                          u[..., o_r:], w_alpha[l], b_alpha[l], gla_norm[l])
        h = h + jnp.concatenate([y_pool.astype(h.dtype), y_gla.astype(h.dtype)], axis=-1) @ w_out_mix[l]
        h = h + 0.5 * swiglu(rmsnorm_2(h, ffn2_norm[l]), ffn2_w_in[l], ffn2_w_out[l])
    return rmsnorm_2(h, final_norm)


def setup_inputs(seed=0):
    out = dict(first_inputs(seed))
    for name, value in second_inputs(seed + 1).items():
        if name != "x":
            out[name + "_2"] = value
    return out


def reference(
    x, mix_norm_w, w_in, s5_log_dt, s5_a_re, s5_a_im, s5_b_re, s5_b_im, s5_c_re, s5_c_im, s5_d,
    s5_glu_w, dn_conv_w, dn_a_log, dn_dt_bias, dn_norm_w, dn_proj_w, w_out, ffn_norm_w, ffn_up,
    ffn_conv_w, ffn_down, final_norm_w, ffn1_norm_2, ffn1_w_in_2, ffn1_w_out_2, mix_norm_2,
    w_in_mix_2, w_pool_2, pool_scale_2, w_alpha_2, b_alpha_2, gla_norm_2, w_out_mix_2,
    ffn2_norm_2, ffn2_w_in_2, ffn2_w_out_2, final_norm_2,
):
    x = first_block(
        x, mix_norm_w, w_in, s5_log_dt, s5_a_re, s5_a_im, s5_b_re, s5_b_im, s5_c_re, s5_c_im,
        s5_d, s5_glu_w, dn_conv_w, dn_a_log, dn_dt_bias, dn_norm_w, dn_proj_w, w_out,
        ffn_norm_w, ffn_up, ffn_conv_w, ffn_down, final_norm_w,
    )
    return second_block(
        x, ffn1_norm_2, ffn1_w_in_2, ffn1_w_out_2, mix_norm_2, w_in_mix_2, w_pool_2,
        pool_scale_2, w_alpha_2, b_alpha_2, gla_norm_2, w_out_mix_2, ffn2_norm_2, ffn2_w_in_2,
        ffn2_w_out_2, final_norm_2,
    )


_drawn_inputs = setup_inputs


def setup_inputs(seed=0):
    import zlib

    import numpy as np

    out = dict(_drawn_inputs(seed))
    spreads = {}
    factors = {'mix_norm_w': 3.553,
     's5_log_dt': 32.184,
     's5_a_re': 64.0,
     's5_a_im': 32.008,
     's5_b_re': 44.0,
     's5_b_im': 46.04,
     's5_c_re': 44.688,
     's5_c_im': 45.016,
     'dn_norm_w': 7.213,
     'ffn_norm_w': 3.218,
     'ffn1_norm_2': 3.116,
     'b_alpha_2': 8.0,
     'gla_norm_2': 22.491,
     'ffn2_norm_2': 8.0,
     'final_norm_2': 8.491,
     'pool_scale_2': 3.169}
    for name, (base, spread) in spreads.items():
        noise = np.random.default_rng([zlib.crc32(name.encode()), seed]).standard_normal(out[name].shape)
        drawn = base * np.exp(spread * noise) if base else spread * noise
        out[name] = __import__('jax').numpy.asarray(drawn.astype(out[name].dtype))
    for name, factor in factors.items():
        out[name] = (out[name] * factor).astype(out[name].dtype)
    return out
```

```python
import math
import concourse.bass as bass
from concourse import mybir
from contextlib import ExitStack


def two_block_kernel(nc, a, out, phases=None):
    F32, F32R, BF16, I32 = mybir.dt.float32, mybir.dt.float32r, mybir.dt.bfloat16, mybir.dt.int32
    ALU, ACT, AX = mybir.AluOpType, mybir.ActivationFunctionType, mybir.AxisListType

    P = 128
    T, D = a["x"].shape[1], a["x"].shape[2]
    M = T // P
    KD = D // P
    NW = 512
    KW = NW // P
    XC = D // NW
    KG = 2
    RING = 4
    FF = a["ffn_down"].shape[1]
    FT = 2 * FF // P
    PAIRS = FF // NW
    PARTS = [4, 4, 3]
    GC = KD // KG
    GH = GC // 2
    CU = a["s5_d"].shape[1]
    CT = CU // P
    H = a["dn_a_log"].shape[1]
    QT = a["dn_conv_w"].shape[2] // P
    DTAPS = a["dn_conv_w"].shape[1]
    SG, SP_, SH = a["s5_b_re"].shape[1:]
    ST = SG * SP_ // P
    SJ = ST // CT
    SW = P // SJ
    OFF_QKV, OFF_Z = CU, CU + QT * P
    OFF_BA = OFF_Z + H * P
    OFF_GS = OFF_BA + 2 * H
    OFF_GD = OFF_GS + D
    LEVELS = P.bit_length() - 1
    W_IN = ([("u", c * NW) for c in range(CU // NW)] + [("qkv", OFF_QKV + c * NW) for c in range(QT // KW)]
            + [("z", OFF_Z + c * NW) for c in range(H * P // NW)] + [("gs", OFF_GS + c * NW) for c in range(XC)]
            + [("gd", OFF_GD + c * NW) for c in range(XC)])
    NU, NQ, NZ = CU // NW, QT // KW, H * P // NW
    PG, PD = a["w_pool_2"].shape[1:3]
    GR, GK = a["w_alpha_2"].shape[1:]
    GHD = GK // P
    GV = a["gla_norm_2"].shape[1]
    LC = 64
    LN = T // LC
    OFF2 = dict(u=0, q=PG * PD, k=PG * PD + GK, v=PG * PD + 2 * GK, g=PG * PD + 2 * GK + GHD * GV,
                lr=PG * PD + 2 * GK + 2 * GHD * GV)
    W_IN2 = ([("u", c * NW) for c in range(PG * PD // NW)] + [("q", OFF2["q"]), ("k", OFF2["k"])]
             + [("v", OFF2["v"] + c * NW) for c in range(GHD * GV // NW)]
             + [("g", OFF2["g"] + c * NW) for c in range(GHD * GV // NW)])
    VC = GHD * GV // NW
    assert sum(PARTS) == PAIRS
    EPS = 1e-6
    EVAC, SPLIT = 3, 5
    LEAD = 3
    MAGIC = 1.5 * 2.0 ** 23
    TURN = 6.283185
    TURN_1, TURN_2, TURN_3 = 6.28125, 0.0019350051879882812, 3.0199159819e-07
    IN_TURNS = 0.15915494309189535
    GATE_NORM = 16.0
    Q_LOG = -0.5 * math.log(a["dn_conv_w"].shape[2] // 3 // a["dn_a_log"].shape[1])
    ATT_WARM = 6
    S5_SLOT = 22
    ATT_SLOT = 44

    FFN_GROUPS = sum(3 * GC * n for n in PARTS)
    phases = phases or ["init", "mix1", "ffn1", "ffn2", "mix2", "ffn3"]
    NEXT = dict(zip(phases, phases[1:]))
    ends = lambda ph: XC if ph in NEXT else 0
    MIX1_GROUPS = GC * len(W_IN) + GH * 3 * XC + GC * XC
    MIX2_GROUPS = GC * len(W_IN2) + GC * XC
    size = {
        "mix1": dict(g=MIX1_GROUPS, ev=NU + NQ + NU + NZ + XC + ends("mix1"), op=NU + NZ + XC + ends("mix1"), x=XC),
        "mix2": dict(g=MIX2_GROUPS, ev=2 + 3 * VC + ends("mix2"), op=2 * VC + ends("mix2"), x=XC),
        "init": dict(ev=XC, op=XC),
        "ffn1": dict(g=FFN_GROUPS, ev=2 * PAIRS + ends("ffn1"), op=PAIRS + ends("ffn1"), src=2 * PAIRS,
                     x=len(PARTS) * XC, gate=PAIRS, conv=2 * PAIRS, prod=PAIRS),
        "ffn2": dict(g=FFN_GROUPS, ev=PAIRS + ends("ffn2"), op=PAIRS + ends("ffn2"), src=PAIRS,
                     x=len(PARTS) * XC, gate=PAIRS),
        "ffn3": dict(g=FFN_GROUPS, ev=PAIRS + ends("ffn3"), op=PAIRS + ends("ffn3"), src=PAIRS,
                     x=len(PARTS) * XC, gate=PAIRS),
    }
    COUNTS = ["g", "ev", "op", "src", "x", "gate", "conv", "prod"]
    at, total = {}, dict.fromkeys(COUNTS, 0)
    for ph in phases:
        at[ph] = dict(total)
        total = {c: total[c] + size[ph].get(c, 0) for c in COUNTS}

    norm_order = []
    for ph in phases:
        if ph == "ffn1" and ph in NEXT:
            norm_order.append("block end")
        norm_order.append(NEXT.get(ph, "result"))
    NORM = {n: k for k, n in enumerate(norm_order)}
    NORMS = len(norm_order)
    NORM_W = {"mix1": "mix_norm_w", "ffn1": "ffn_norm_w", "ffn2": "ffn1_norm_2", "mix2": "mix_norm_2",
              "ffn3": "ffn2_norm_2"}
    two_norms = "ffn1" in NEXT

    def wview(w):
        return w.rearrange("o (k p) n -> p (o k) n", p=P)

    def n_at(n, i, per):
        return n if i is None else i * per + n

    def cols(c):
        return slice(c * NW, (c + 1) * NW)

    ctx = ExitStack()
    with ctx:
        def sem(name):
            return ctx.enter_context(nc.semaphore(name))

        def over(*spans):
            spans = [list(span) for span in spans]

            def put(name, shape, dt=F32):
                n = 4 if dt in (F32, F32R, I32) else 2
                for d in shape[1:]:
                    n *= d
                n = -(-n // 32) * 32
                for span in spans:
                    if span[1] >= n:
                        span[0], span[1] = span[0] + n, span[1] - n
                        return nc.alloc_sbuf_tensor_at(name, shape, dt, offset=span[0] - n)
                raise ValueError(f"no room for {name}")
            return put

        first = -(-nc.sbuf_base // 32) * 32
        sb = over((first, nc.sbuf_usable_end - first))

        def spot(name, shape, dt=F32):
            t = sb(name, shape, dt)
            return t, t.manual_sbuf_range[0]

        stage = sb("stage", [P, RING, KG, NW])
        w_hi = sb("w_hi", [P, RING, KG, NW], F32R)
        w_lo = sb("w_lo", [P, RING, KG, NW], F32R)
        a_hi, A_HI = spot("a_hi", [P, KD, T], F32R)
        a_lo, A_LO = spot("a_lo", [P, KD, T], F32R)
        b_hi, B_HI = spot("b_hi", [P, KD, T], F32R)
        b_lo, B_LO = spot("b_lo", [P, KD, T], F32R)
        A, B = (a_hi, a_lo), (b_hi, b_lo)
        x, X = spot("x", [P, M, D])
        XB = 4 * M * D
        HB = 4 * KD * T // 2
        evac = sb("evac", [P, M, NW])
        ident = sb("ident", [P, P])
        half = sb("half", [P, 8])
        ssq = sb("ssq", [P, M, XC])
        sumsq = sb("sumsq", [P, NORMS, M])
        mean = sb("mean", [P, NORMS, M])
        rstd = sb("rstd", [P, NORMS, M])
        row_scale = sb("row_scale", [P, M])
        junk = sb("junk", [P, M, NW], BF16)
        VECS = ["mix_norm_w", "ffn_norm_w", "final_norm_w", "ffn1_norm_2", "mix_norm_2", "ffn2_norm_2",
                "pool_scale_2", "b_alpha_2", "gla_norm_2", "dn_norm_w"]
        vec_at, VEC_ROWS = {}, 0
        for name in VECS:
            vec_at[name] = VEC_ROWS
            VEC_ROWS += a[name].shape[-1] // P
        vecT = sb("vecT", [P, VEC_ROWS])
        blk_w = sb("blk_w", [P, KD])
        TAPS = a["ffn_conv_w"].shape[1]
        taps = sb("taps", [P, TAPS, FT])
        dtaps = sb("dtaps", [P, DTAPS, QT])
        s5p = sb("s5p", [P, 6, ST])
        expo_mask = sb("expo_mask", [P, 2, P])
        lev_mask = sb("lev_mask", [P, LEVELS, P], BF16)
        triu = sb("triu", [P, P])
        ones = sb("ones", [P, P])
        score_mask = sb("score_mask", [P, P], I32)
        dv = {n: sb("dn_" + n, [P, M, H]) for n in (
            "cum", "beta", "rowk", "wk", "nwk", "wq", "colk", "colq", "lnb")}
        dn_tail = sb("dn_tail_scale", [P, H])
        dn_ssq = sb("dn_ssq", [P, 4])
        dn_mean = sb("dn_mean", [P, 4])
        dn_rstd = sb("dn_rstd", [P, 4])
        g_ssq = sb("gla_ssq", [P, M, GHD])
        g_mean = sb("gla_mean", [P, M, GHD])
        g_rstd = sb("gla_rstd", [P, M, GHD])

        ARENA = 64 * 1024
        arena, AR = spot("arena", [P, ARENA // 4])
        put = over((AR, ARENA))
        sgate = put("sgate", [P, M, NW])
        conv_g = put("conv_g", [P, KW, T])
        conv_v = put("conv_v", [P, KW, T])
        fnorm = put("fnorm", [P, D])
        put = over((AR, ARENA))
        uT, UT = put("uT", [P, CT, T]), AR
        qkvT = put("qkvT", [P, QT, T])
        QK = UT + 4 * CT * T
        zs = put("zs", [P, M, H * P])
        ZS = QK + 4 * QT * T
        gs = put("gs", [P, M, D])
        ud = put("ud", [P, M, CU])
        UD = ZS + 4 * M * H * P + 4 * M * D
        put = over((X, XB))
        s5_B = put("s5_B", [P, CT, 2, P])
        s5_C = put("s5_C", [P, CT, 2, P])
        gd = over((X, XB))("gd", [P, M, D])
        put = over((ZS, UD - ZS))
        b_wide = put("b_wide", [P, 2, ST, P // SP_, SH])
        c_wide = put("c_wide", [P, 2, CT, P // SP_, SP_])
        b_nat = put("b_nat", [P, 2, ST, SH])
        c_nat = put("c_nat", [P, 2, CT, SP_])
        put = over((QK, ZS - QK))
        d_row = put("d_row", [P, CU])
        b_t = put("b_t", [P, 2, ST, SH])
        par = put("par", [P, P // SP_])
        ba_w = put("ba_w", [P, KD, 2 * H])
        ba_hi = put("ba_hi", [P, KD, 2 * H], F32R)
        ba_lo = put("ba_lo", [P, KD, 2 * H], F32R)
        ba = put("ba", [P, M, 2 * H])
        ba_abs = put("ba_abs", [P, M, 2 * H])
        ba_ln = put("ba_ln", [P, M, 2 * H])
        dt_row = put("dt_row", [P, H])
        alog_row = put("alog_row", [P, H])
        ea_row = put("ea_row", [P, H])
        dn_g = put("dn_g", [P, M, H])
        log_dt = put("log_dt", [ST, P // SP_])
        s5_dt = put("s5_dt", [ST, P // SP_])
        vecs = put("vecs", [VEC_ROWS, P])
        tap_rows = put("tap_rows", [FT, TAPS, P])
        dtap_rows = put("dtap_rows", [DTAPS * QT, P])
        row = {n: put("row_" + n, [ST, P]) for n in (
            "lr", "li", "lrdt", "th", "k", "mag", "f", "sn", "sh", "cs", "ar", "ai", "den", "t1", "t2", "cr", "ci",
            "flo")}
        row_fhi = put("row_fhi", [ST, P], F32R)
        put = over((B_HI, 2 * HB), (B_LO, 2 * HB))
        tok_i = put("tok_i", [P, T], I32)
        tok = put("tok", [P, T])
        turn = put("turn", [P, 2, T])
        frac = put("frac", [P, 2, T])
        sin_h = put("sin_h", [P, 2, T])
        sn = put("sn", [P, 2, T])
        cs = put("cs", [P, 2, T])
        p_c = put("p_c", [P, 2, T])
        p_s = put("p_s", [P, 2, T])
        rot = put("rot", [P, 2, 2, T])
        scn = put("scn", [P, 2, T])
        put = over((UT, QK - UT), (UD, 4 * M * CU))
        vb = put("vb", [P, 4, P])
        ktail = put("ktail", [P, 2, P])
        vnew = put("vnew", [P, 4, P])
        dn_S = put("dn_S", [P, 2, P])
        rhs1 = put("rhs1", [P, 2, P])
        qS = put("qS", [P, 2, P])
        dn_o = put("dn_o", [P, 4, P])
        dn_junk = put("dn_junk", [P, P], BF16)
        dn_ss = put("dn_ss", [P, M, 2 * H])
        put = over((B_HI + HB, HB), (B_LO + HB, HB))
        dec = put("dec", [P, 2, 4, P])
        LT = put("LT", [P, 4, P])
        AT = put("AT", [P, 4, P])
        DT = put("DT", [P, 4, P])
        DD = put("DD", [P, 4, P])
        PP = put("PP", [P, 4, P])
        LK = put("LK", [P, 4, P])
        sq4 = over((B_HI + HB, HB))("sq4", [P, KW, T])
        put = over((AR, ARENA))
        u2T = put("u2T", [P, 8, T])
        vv = put("vv", [P, M, GHD * GV])
        sg = put("sg", [P, M, GHD * GV])
        qd = put("qd", [P, GHD, T])
        ki = put("ki", [P, GHD, T])
        kt = put("kt", [P, GHD, T])
        la = put("la", [P, GHD, T])
        lt = put("lt", [P, GHD, T])
        ktT = put("ktT", [P, M, GHD, P])
        sc = put("sc", [P, M, GHD, P])
        SA = AR + 4 * (2 * M * GHD * GV + 8 * T + 5 * GHD * T + 2 * M * GHD * P)
        SBYTES = 4 * (LN - 1) * GHD * GV
        Sg = put("Sg", [P, LN - 1, GHD, GV])
        put = over((SA, SBYTES))
        lr2 = put("lr2", [P, M, GR])
        lrT = put("lrT", [GR, T])
        wal = put("wal", [GR, GK])
        put = over((A_HI + HB, HB), (A_LO + HB, HB))
        lr_w = put("lr_w", [P, KD, GR])
        lr_hi = put("lr_hi", [P, KD, GR], F32R)
        lr_lo = put("lr_lo", [P, KD, GR], F32R)
        put = over((A_HI + HB, HB), (A_LO + HB, HB))
        pool_a = put("pool_a", [P, 8, T])
        pool_b = put("pool_b", [P, 8, T])
        wp = [over((A_HI + HB // 2, HB // 2))("wp0", [P, 2, 2, PD]), over((A_LO + HB // 2, HB // 2))("wp1", [P, 2, 2, PD])]
        rcnt = sb("rcnt", [P, PG, 16])
        gdec = sb("gdec", [P, GHD, LN])

        acc = ctx.enter_context(nc.psum_tensor("acc", [P, 2, M, NW], F32))
        tp = ctx.enter_context(nc.psum_tensor("tp", [P, KW, T], F32))
        side = ctx.enter_context(nc.psum_tensor("side", [P, 2, NW], F32))

        stage_full = [sem(f"stage_full{s}") for s in range(RING)]
        hi_done = sem("hi_done")
        lo_done = sem("lo_done")
        used = sem("used")
        x_full = [sem(f"x_full{m}") for m in range(M)]
        vec_full = sem("vec_full")
        taps_full = sem("taps_full")
        fnorm_full = sem("fnorm_full")
        consts = sem("consts")
        vec_T = sem("vec_T")
        vec_in = sem("vec_in")
        src = sem("src")
        tp_full = sem("tp_full")
        hi_T = sem("hi_T")
        op_T = sem("op_T")
        gated = sem("gated")
        tap_step = sem("tap_step")
        conved = sem("conved")
        prod = sem("prod")
        x_new = sem("x_new")
        sq = sem("sq")
        sums = sem("sums")
        ms = sem("ms")
        rs = sem("rs")
        blk_ready = sem("blk_ready")
        scaled = sem("scaled")
        rescaled = sem("rescaled")
        out_done = sem("out_done")
        masks = sem("masks")
        left = sem("left")
        copied = sem("copied")
        step_d = sem("step_d")
        step_a = sem("step_a")
        x_again = sem("x_again")
        dtap_full = sem("dtap_full")
        s5_full = sem("s5_full")
        s5_bc_full = sem("s5_bc_full")
        d_full = sem("d_full")
        ba_full = sem("ba_full")
        dnp_full = sem("dnp_full")
        skip_done = sem("skip_done")
        par_dt = sem("par_dt")
        par_th = sem("par_th")
        par_trig = sem("par_trig")
        par_done = sem("par_done")
        par_T = sem("par_T")
        par_in = sem("par_in")
        wide_b = sem("wide_b")
        wide_T = sem("wide_T")
        wide_in = sem("wide_in")
        tok_done = sem("tok_done")
        s5_turn = sem("s5_turn")
        s5_frac = sem("s5_frac")
        s5_sin = sem("s5_sin")
        s5_bu = sem("s5_bu")
        s5_rot = sem("s5_rot")
        s5_x = sem("s5_x")
        s5_y = sem("s5_y")
        s5_res = sem("s5_res")
        s5_gelu = sem("s5_gelu")
        ba_split = sem("ba_split")
        ba_mm = sem("ba_mm")
        ba_in = sem("ba_in")
        ba_neg = sem("ba_neg")
        ba_log = sem("ba_log")
        dn_gate = sem("dn_gate")
        dn_cum = sem("dn_cum")
        dn_conved = sem("dn_conved")
        qkv_act = sem("qkv_act")
        qk_sq = sem("qk_sq")
        qk_ss = sem("qk_ss")
        dn_ssin = sem("dn_ssin")
        dn_lns = sem("dn_lns")
        dn_rows = sem("dn_rows")
        dn_fac = sem("dn_fac")
        dn_nwk = sem("dn_nwk")
        dn_expo = sem("dn_expo")
        dn_masked = sem("dn_masked")
        dn_decay = sem("dn_decay")
        dn_kk = sem("dn_kk")
        dn_LA = sem("dn_LA")
        dn_D = sem("dn_D")
        dn_DT = sem("dn_DT")
        dn_lev = sem("dn_lev")
        dn_P = sem("dn_P")
        dn_Pin = sem("dn_Pin")
        dn_X = sem("dn_X")
        dn_vk = sem("dn_vk")
        dn_vb = sem("dn_vb")
        dn_new = sem("dn_new")
        dn_newin = sem("dn_newin")
        dn_St = sem("dn_St")
        dn_Sin = sem("dn_Sin")
        dn_o0 = sem("dn_o0")
        dn_kS = sem("dn_kS")
        dn_rhs = sem("dn_rhs")
        dn_out = sem("dn_out")
        dn_ofull = sem("dn_ofull")
        dn_sq = sem("dn_sq")
        dn_ms = sem("dn_ms")
        dn_rs = sem("dn_rs")
        dn_y = sem("dn_y")
        gate_sig = sem("gate_sig")
        glu_sig = sem("glu_sig")
        glu_a = sem("glu_a")
        s5_part = sem("s5_part")
        merged = sem("merged")
        lr_full = sem("lr_full")
        wal_full = sem("wal_full")
        wp_full = sem("wp_full")
        lr_split = sem("lr_split")
        lr_mm = sem("lr_mm")
        lr_in = sem("lr_in")
        lr_T = sem("lr_T")
        lr_Tin = sem("lr_Tin")
        al_mm = sem("al_mm")
        al_in = sem("al_in")
        al_abs = sem("al_abs")
        al_exp = sem("al_exp")
        al_one = sem("al_one")
        al_ln = sem("al_ln")
        al_cum = sem("al_cum")
        al_dec = sem("al_dec")
        qk_dec = sem("qk_dec")
        gk_T = sem("gk_T")
        gk_in = sem("gk_in")
        g_sc = sem("g_sc")
        g_scin = sem("g_scin")
        g_kv = sem("g_kv")
        g_S = sem("g_S")
        g_o = sem("g_o")
        g_oin = sem("g_oin")
        g_ms = sem("g_ms")
        g_rs = sem("g_rs")
        g_y = sem("g_y")
        pooled = sem("pooled")

        block = ctx.enter_context(nc.Block())

        def weight_of(ph):
            if ph == "ffn2" and two_norms:
                return blk_w[:, :]
            o = vec_at[NORM_W[ph]]
            return vecT[:, o:o + KD]

        first_x = A if phases[1] == "mix1" else B
        left0 = len(W_IN) if "mix1" in phases else 0
        copied0 = NU if "mix1" in phases else 0
        sq_count = {}
        for k, n in enumerate(norm_order):
            sq_count[n] = M * XC * (k + 1)

        @block.sync
        def _(sp):
            def load(g, w, k0, col, i=None, per=0):
                s = g % RING
                if g >= RING or i is not None:
                    sp.wait_ge(lo_done, n_at(g - RING + 1, i, per))
                sp.dma_start(stage[:, s], wview(w)[:, k0:k0 + KG, bass.ds(col, NW)]).then_inc(stage_full[s], 16)

            def ffn(ph, up, down):
                g0, pair0 = at[ph]["g"], 0
                for n in PARTS:
                    for pos in range(2 * GC):
                        load(g0 + pos, up, KG * (pos % GC), pair0 * NW + FF * (pos // GC))
                    if not pair0 and (ph == "ffn1" or ph not in NEXT):
                        v = a["final_norm_2" if ph != "ffn1" and "ffn1" in phases else "final_norm_w"]
                        v = v.rearrange("(o c) -> o c", o=1) if len(v.shape) == 1 else v
                        sp.dma_start(fnorm[:], v[0, :].partition_broadcast(P)).then_inc(fnorm_full, 16)
                    with sp.Fori(1, n) as i:
                        for pos in range(2 * GC):
                            load(g0 + pos, up, KG * (pos % GC), i * NW + (pair0 * NW + FF * (pos // GC)), i, 2 * GC)
                    g0 += 2 * GC * n
                    for c in range(XC):
                        for pos in range(KW * n // KG):
                            load(g0, down, KW * pair0 + KG * pos, c * NW)
                            g0 += 1
                    pair0 += n

            def mix(ph, chunks, w_out):
                g = at[ph]["g"]
                for w, col, n in chunks + [(w_out, c * NW, GC) for c in range(XC)]:
                    for pos in range(n):
                        load(g, w, KG * pos, col)
                        g += 1
                    if ph == "mix1" and w is w_out and col == 0:
                        sp.wait_ge(merged, XC)
                        for m in range(M):
                            sp.dma_start(x[:, m], a["x"][0, m * P:(m + 1) * P, :]).then_inc(x_again, 16)

            for m in range(M):
                sp.dma_start(x[:, m], a["x"][0, m * P:(m + 1) * P, :]).then_inc(x_full[m], 16)
            for name in VECS:
                v = a[name]
                v = v.rearrange("(r c) -> r c", c=P) if len(v.shape) == 1 else v.rearrange("o (r c) -> (o r) c", c=P)
                sp.dma_start(vecs[vec_at[name]:vec_at[name] + v.shape[0], :], v).then_inc(vec_full, 16)
            sp.dma_start(tap_rows[:], a["ffn_conv_w"].rearrange("o t (r c) -> r (o t) c", c=P)).then_inc(taps_full, 16)
            sp.dma_start(dtap_rows[:], a["dn_conv_w"].rearrange("o t (r c) -> (o t r) c", c=P)).then_inc(dtap_full, 16)
            for ph in phases:
                if ph == "mix1":
                    mix(ph, [(a["w_in"], col, GC) for _, col in W_IN]
                        + [(a["s5_glu_w"], half_ * D + c * NW, GH) for c in range(XC) for half_ in range(2)]
                        + [(a["dn_proj_w"], c * NW, GH) for c in range(XC)], a["w_out"])
                elif ph == "mix2":
                    mix(ph, [(a["w_in_mix_2"], col, GC) for _, col in W_IN2], a["w_out_mix_2"])
                elif ph == "ffn1":
                    ffn(ph, a["ffn_up"], a["ffn_down"])
                elif ph == "ffn2":
                    ffn(ph, a["ffn1_w_in_2"], a["ffn1_w_out_2"])
                elif ph == "ffn3":
                    ffn(ph, a["ffn2_w_in_2"], a["ffn2_w_out_2"])
            if two_norms and phases[-1] == "ffn1":
                sp.wait_ge(scaled, M)
            for m in range(M):
                sp.wait_ge(scaled, (M if two_norms else 0) + m + 1)
                sp.dma_start(out[0, m * P:(m + 1) * P, :], x[:, m]).then_inc(out_done, 16)
            sp.wait_ge(out_done, 16 * M)

        counts = {consts: 0, masks: 0}

        @block.gpsimd
        def _(gp):
            def const(op, which):
                op.then_inc(which, 1)
                counts[which] += 1

            def keep(t, which, op, base, pattern, cm, fill):
                gp.wait_ge(which, counts[which])
                const(nc.gpsimd.affine_select(out=t, in_=t, compare_op=op, fill=fill, base=base, pattern=pattern,
                                              channel_multiplier=cm), which)

            const(nc.gpsimd.memset(ident[:], 0.0), consts)
            keep(ident[:], consts, ALU.not_equal, 0, [[-1, P]], 1, 1.0)
            const(nc.gpsimd.memset(half[:], -0.5), consts)
            const(nc.gpsimd.memset(ones[:], 1.0), consts)
            if "mix1" in phases:
                g2 = P // SP_
                for dst, view, full in (
                        (log_dt[:], a["s5_log_dt"].rearrange("o (t g) -> (o t) g", g=g2), s5_full),
                        (row["lr"][:], a["s5_a_re"].rearrange("o (t g) p -> (o t) (g p)", g=g2), s5_full),
                        (row["li"][:], a["s5_a_im"].rearrange("o (t g) p -> (o t) (g p)", g=g2), s5_full),
                        (b_nat[:, 0], a["s5_b_re"].rearrange("o (t g) p h -> (o g p) t h", g=g2), s5_bc_full),
                        (b_nat[:, 1], a["s5_b_im"].rearrange("o (t g) p h -> (o g p) t h", g=g2), s5_bc_full),
                        (c_nat[:, 0], a["s5_c_re"].rearrange("o (c g) h p -> (o g h) c p", c=CT), s5_bc_full),
                        (c_nat[:, 1], a["s5_c_im"].rearrange("o (c g) h p -> (o g h) c p", c=CT), s5_bc_full),
                        (ba_w[:], a["w_in"][:, :, OFF_BA:OFF_BA + 2 * H].rearrange("o (k p) n -> p (o k) n", p=P), ba_full),
                        (d_row[:], a["s5_d"][0, :].partition_broadcast(P), d_full),
                        (dt_row[:], a["dn_dt_bias"][0, :].partition_broadcast(P), dnp_full),
                        (alog_row[:], a["dn_a_log"][0, :].partition_broadcast(P), dnp_full)):
                    gp.dma_start(dst, view).then_inc(full, 16)
                const(nc.gpsimd.memset(b_wide[:], 0.0), consts)
                const(nc.gpsimd.iota(tok_i[:], pattern=[[1, T]], base=0, channel_multiplier=0), consts)
                const(nc.gpsimd.memset(triu[:], 1.0), masks)
                keep(triu[:], masks, ALU.is_ge, 0, [[1, P]], -1, 0.0)
                const(nc.gpsimd.memset(expo_mask[:], 0.0), masks)
                keep(expo_mask[:, 0], masks, ALU.is_gt, 0, [[1, P]], -1, -1e30)
                keep(expo_mask[:, 1], masks, ALU.is_ge, 0, [[1, P]], -1, -1e30)
                for l in range(LEVELS):
                    n = 1 << l
                    odd = lev_mask[:, l].rearrange("p (j h c) -> p j h c", h=2, c=n)[:, :, 1]
                    const(nc.gpsimd.memset(lev_mask[:, l], 0.0), masks)
                    gp.wait_ge(masks, counts[masks])
                    const(nc.gpsimd.memset(odd, 1.0), masks)
                    keep(odd, masks, ALU.is_ge, 0, [[-2 * n, P // (2 * n)], [0, n]], 1, 0.0)
                    keep(odd, masks, ALU.is_ge, n - 1, [[2 * n, P // (2 * n)], [0, n]], -1, 0.0)
            if "mix2" in phases:
                view = score_mask[:].rearrange("p (n i) -> p n i", i=LC)
                const(nc.gpsimd.memset(score_mask[:], 1), masks)
                keep(view, masks, ALU.is_ge, 0, [[LC, P // LC], [1, LC]], -1, 0)
                keep(view, masks, ALU.is_ge, 0, [[-LC, P // LC], [0, LC]], 1, 0)
                for t in range(16):
                    const(nc.gpsimd.memset(rcnt[:, :, t:t + 1], 1.0 / (t + 1)), masks)
                gp.wait_ge(masks, counts[masks])
                for gi in range(PG - 1):
                    w = 2 << gi
                    const(nc.gpsimd.memset(rcnt[:, gi, w:16], 1.0 / w), masks)
            gp.wait_ge(consts, counts[consts])
            for n in norm_order:
                if n == "mix2":
                    gp.wait_ge(x_new, at[n]["x"])
                    gp.dma_start(lr_w[:], a["w_in_mix_2"][:, :, OFF2["lr"]:OFF2["lr"] + GR].rearrange(
                        "o (k p) n -> p (o k) n", p=P)).then_inc(lr_full, 16)
                    gp.dma_start(wal[:], a["w_alpha_2"][0]).then_inc(wal_full, 16)
                    for g2 in range(PG):
                        gp.dma_start(wp[g2 // 2][:, g2 % 2], a["w_pool_2"][0, g2].rearrange("(k p) n -> p k n", p=P)
                                     ).then_inc(wp_full, 16)
                gp.wait_ge(ms, NORM[n] + 1)
                nc.gpsimd.tensor_tensor(rstd[:, NORM[n]], mean[:, NORM[n]], half[:, 0:M], ALU.pow).then_inc(rs, 1)
                if n == "mix1":
                    for b in range(H // 2):
                        gp.wait_ge(dn_ms, b + 1)
                        if b:
                            gp.wait_ge(dn_y, b)
                        nc.gpsimd.tensor_tensor(dn_rstd[:], dn_mean[:], half[:, 0:4], ALU.pow).then_inc(dn_rs, 1)
                if n == "mix2":
                    gp.wait_ge(g_ms, 1)
                    nc.gpsimd.tensor_tensor(g_rstd[:].rearrange("p m h -> p (m h)"), g_mean[:].rearrange("p m h -> p (m h)"),
                                            half[:, 0:M * GHD], ALU.pow).then_inc(g_rs, 1)

        const_total, mask_total = counts[consts], counts[masks]

        @block.scalar
        def _(act):
            def hi(g, i=None, per=0):
                s = g % RING
                act.wait_ge(stage_full[s], n_at(16 * (g // RING + 1), i, 16 * per // RING))
                if g >= RING or i is not None:
                    act.wait_ge(used, n_at(g - RING + 1, i, per))
                nc.scalar.activation(w_hi[:, s], stage[:, s], ACT.Copy).then_inc(hi_done, 1)

            def chunk_hi(ev, dst, k0, weight=None, i=None, w0=None, w_period=KD):
                act.wait_ge(tp_full, n_at(ev + 1, i, 1))
                if w0 is not None:
                    for k in range(KW):
                        w = w0 + k % w_period
                        op = nc.scalar.activation(dst[:, k0 + k], tp[:, k], ACT.Copy, scale=vecT[:, w:w + 1])
                    op.then_inc(hi_T, 1)
                elif weight is None:
                    nc.scalar.activation(dst[:, bass.ds(k0, KW)], tp[:], ACT.Copy).then_inc(hi_T, 1)
                else:
                    for k in range(KW):
                        op = nc.scalar.activation(dst[:, k0 + k], tp[:, k], ACT.Copy,
                                                  scale=weight[:, k0 + k:k0 + k + 1])
                    op.then_inc(hi_T, 1)

            n_squares = [0]

            def squares(c):
                for m in range(M):
                    if n_squares[0] >= M:
                        act.wait_ge(sq, n_squares[0] - M + 1)
                    nc.scalar.activation(junk[:, m], x[:, m, cols(c)], ACT.Square,
                                         accum_out=ssq[:, m, c:c + 1]).then_inc(sq, 1)
                    n_squares[0] += 1

            def no_tail(pos):
                pass

            def x_tail(ev, xc, c, dst, weight):
                def tail(pos):
                    if pos == EVAC + 1:
                        act.wait_ge(x_new, xc + 1)
                        squares(c)
                    if pos == SPLIT and dst is not None:
                        chunk_hi(ev, dst[0], KW * c, weight)
                return tail

            def block_end_tail(before):
                def tail(pos):
                    before(pos)
                    if pos == SPLIT + 4:
                        act.wait_ge(scaled, M)
                        for c in range(XC):
                            squares(c)
                return tail

            def ffn(ph, conv, xdst, adst, tail):
                at_ph = at[ph]
                g0, ev, sr, xc, q0, cv = (at_ph[k] for k in ("g", "ev", "src", "x", "gate", "conv"))
                weight = weight_of(NEXT[ph]) if ph in NEXT else None
                both = ph == "ffn2" and two_norms
                scale = row_scale[:, :] if both else rstd[:, NORM[ph]]
                per = 2 if conv else 1

                def leave_psum(g, sr, e, s, i=None):
                    act.wait_ge(used, n_at(g, i, 2 * GC))
                    act.wait_ge(tp_full, n_at(e, i, 2))
                    for m in range(M):
                        op = nc.scalar.activation(evac[:, m], acc[:, s, m], ACT.Copy, scale=scale[:, m:m + 1])
                    op.then_inc(src, 1)

                def gate_silu(g, sr, i=None):
                    act.wait_ge(used, n_at(g, i, 2 * GC))
                    act.wait_ge(src, n_at(sr, i, 1))
                    for m in range(M):
                        op = nc.scalar.activation(sgate[:, m], acc[:, 0, m], ACT.Silu, scale=scale[:, m:m + 1])
                    op.then_inc(gated, 1)

                def pair(g, sr, e, cv, before, i=None):
                    for pos in range(2 * GC):
                        hi(g + pos, i, 2 * GC)
                        before(pos)
                        if pos == GC + EVAC and conv:
                            leave_psum(g + GC, sr, e, 0, i)
                        if pos == GC + EVAC and not conv:
                            gate_silu(g + GC, sr, i)
                        if pos == GC + SPLIT and conv:
                            act.wait_ge(conved, n_at(cv + 1, i, 2))
                            nc.scalar.activation(conv_g[:], conv_g[:], ACT.Silu).then_inc(gated, 1)

                def pair_tail(g, sr, e, pr, k0, i=None):
                    def tail(pos):
                        if pos == EVAC and conv:
                            leave_psum(g, sr, e, 1, i)
                        if pos == SPLIT and conv:
                            act.wait_ge(prod, n_at(pr + 1, i, 1))
                            nc.scalar.activation(adst[0][:, bass.ds(k0, KW)], conv_v[:], ACT.Copy).then_inc(hi_T, 1)
                        if pos == SPLIT and not conv:
                            chunk_hi(e, adst[0], k0, None, i)
                    return tail

                pr = at_ph["prod"]
                for p, n in enumerate(PARTS):
                    if p == 0:
                        x_end = tail

                        def tail(pos):
                            x_end(pos)
                            if pos == GC + EVAC - 1:
                                if both:
                                    act.wait_ge(rescaled, 1)
                                else:
                                    act.wait_ge(rs, NORM[ph] + 1)
                    pair(g0, sr, ev, cv, tail)
                    with act.Fori(1, n) as i:
                        last = pair_tail(g0, sr - 1, ev - 1, pr - 1, i * KW - KW, i)
                        pair(g0, sr, ev, cv, last, i)
                    g0, sr, ev, cv, pr = g0 + 2 * GC * n, sr + per * n, ev + per * n, cv + 2 * n, pr + n
                    tail = pair_tail(g0, sr - 1, ev - 1, pr - 1, KW * (n - 1))
                    for c in range(XC):
                        for pos in range(KW * n // KG):
                            hi(g0)
                            g0 += 1
                            tail(pos)
                        tail = no_tail
                        if p == len(PARTS) - 1:
                            tail = x_tail(ev, xc + c, c, xdst, weight)
                            ev += xdst is not None
                    xc += XC
                if ph == "ffn1" and two_norms:
                    tail = block_end_tail(tail)
                return tail

            steps = [0]

            def link(op):
                op.then_inc(step_a, 1)
                steps[0] += 1
                act.wait_ge(step_a, steps[0])

            def s5_and_delta(e0):
                def sines(t):
                    b = t % 2
                    act.wait_ge(s5_frac, t + 1)
                    if t >= 2:
                        act.wait_ge(s5_x, t - 1)
                    nc.scalar.activation(sn[:, b], frac[:, b], ACT.Sin, scale=TURN)
                    link(nc.scalar.activation(sin_h[:, b], frac[:, b], ACT.Sin, scale=TURN / 2))
                    nc.scalar.activation(sin_h[:, b], sin_h[:, b], ACT.Square).then_inc(s5_sin, 1)

                def turns(t):
                    b = t % 2
                    if t >= 2:
                        act.wait_ge(s5_frac, t - 1)
                    link(nc.scalar.activation(turn[:, b], tok[:], ACT.Copy, scale=s5p[:, 1, t:t + 1], bias=MAGIC))
                    nc.scalar.activation(turn[:, b], turn[:, b], ACT.Copy, bias=-MAGIC).then_inc(s5_turn, 1)

                act.wait_ge(s5_full, 48)
                nc.scalar.activation(s5_dt[:], log_dt[:], ACT.Exp).then_inc(par_dt, 1)
                act.wait_ge(ba_full, 16)
                nc.scalar.activation(ba_hi[:], ba_w[:], ACT.Copy).then_inc(ba_split, 1)
                act.wait_ge(par_th, 1)
                nc.scalar.activation(row["mag"][:], row["lrdt"][:], ACT.Exp)
                nc.scalar.activation(row["sn"][:], row["f"][:], ACT.Sin, scale=TURN)
                link(nc.scalar.activation(row["sh"][:], row["f"][:], ACT.Sin, scale=TURN / 2))
                nc.scalar.activation(row["sh"][:], row["sh"][:], ACT.Square).then_inc(par_trig, 1)
                yield
                act.wait_ge(par_T, 1)
                nc.scalar.activation(s5p[:], side[:, 0, 0:6 * ST].rearrange("p (n t) -> p n t", t=ST), ACT.Copy).then_inc(par_in, 1)
                act.wait_ge(ba_mm, 1)
                act.wait_ge(rs, NORM["mix1"] + 1)
                for m in range(M):
                    op = nc.scalar.activation(ba[:, m], side[:, 1, m * 2 * H:(m + 1) * 2 * H], ACT.Copy,
                                              scale=rstd[:, NORM["mix1"], m:m + 1])
                op.then_inc(ba_in, 1)
                act.wait_ge(ba_neg, 1)
                nc.scalar.activation(ba_ln[:], ba_abs[:], ACT.Exp, scale=-1.0).then_inc(ba_log, 1)
                act.wait_ge(dnp_full, 32)
                nc.scalar.activation(ea_row[:], alog_row[:], ACT.Exp).then_inc(ba_log, 1)
                act.wait_ge(ba_neg, 2)
                nc.scalar.activation(ba_ln[:], ba_ln[:], ACT.Ln).then_inc(ba_log, 1)
                yield
                for q in range(4):
                    for b in range(2):
                        act.wait_ge(wide_T, 2 * q + b + 1)
                        dst = s5_B if q < 2 else s5_C
                        nc.scalar.activation(dst[:, 4 * b:4 * b + 4, q % 2], side[:, b].rearrange("p (c s) -> p c s", s=P),
                                             ACT.Copy, scale=-1.0 if q == 3 else 1.0).then_inc(wide_in, 1)
                    yield
                yield
                act.wait_ge(tok_done, 1)
                turns(0)
                sines(0)
                n = 7
                while n < S5_SLOT:
                    n += 1
                    yield
                for t in range(ST):
                    if t + 1 < ST:
                        turns(t + 1)
                    yield
                    if t + 1 < ST:
                        sines(t + 1)
                    yield
                act.wait_ge(s5_res, CT)
                for m in range(M):
                    op = nc.scalar.activation(ud[:, m], ud[:, m], ACT.Gelu)
                op.then_inc(s5_gelu, 1)
                yield
                for c in range(NU):
                    chunk_hi(e0 + c, B[0], KW * c)
                    yield
                yield "s5"
                for j in range(2 * H // KW):
                    act.wait_ge(qkv_act, j + 1)
                    if j:
                        act.wait_ge(qk_ss, j)
                    nc.scalar.activation(sq4[:], qkvT[:, KW * j:KW * (j + 1)], ACT.Square).then_inc(qk_sq, 1)
                    yield
                act.wait_ge(dn_ssin, 1)
                nc.scalar.activation(dn_ss[:], dn_ss[:], ACT.Ln).then_inc(dn_lns, 1)
                act.wait_ge(dn_rows, 1)
                nc.scalar.activation(dv["wk"][:], dv["colk"][:], ACT.Exp)
                nc.scalar.activation(dv["wq"][:], dv["colq"][:], ACT.Exp)
                nc.scalar.activation(dv["beta"][:], dv["lnb"][:], ACT.Exp)
                nc.scalar.activation(dn_tail[:], dn_tail[:], ACT.Exp).then_inc(dn_fac, 1)
                yield
                for b in range(H // 2):
                    unit = [(h, m) for h in (2 * b, 2 * b + 1) for m in range(M)]
                    act.wait_ge(dn_masked, b + 1)
                    for w in range(2):
                        for u, (h, m) in enumerate(unit):
                            op = nc.scalar.activation(dec[:, w, u], dec[:, w, u], ACT.Exp, bias=dv["rowk"][:, m, h:h + 1])
                    op.then_inc(dn_decay, 1)
                    yield
                    act.wait_ge(dn_vk, b + 1)
                    for u, (h, m) in enumerate(unit):
                        nc.scalar.activation(vb[:, u], side[:, 0, u * P:(u + 1) * P], ACT.Copy, scale=dv["beta"][:, m, h:h + 1])
                    for e in range(2):
                        op = nc.scalar.activation(ktail[:, e], side[:, 1, e * P:(e + 1) * P], ACT.Copy,
                                                  scale=dn_tail[:, 2 * b + e:2 * b + e + 1])
                    op.then_inc(dn_vb, 1)
                    yield
                    yield
                    yield
                    for l in range(1, LEVELS):
                        act.wait_ge(dn_P, (LEVELS - 1) * b + l)
                        nc.scalar.activation(PP[:].rearrange("p u c -> p (u c)"), side[:, 0], ACT.Copy).then_inc(dn_Pin, 1)
                        yield
                        yield
                    act.wait_ge(dn_new, 2 * b + 1)
                    nc.scalar.activation(vnew[:, 0:2], side[:, 0, 0:2 * P].rearrange("p (e c) -> p e c", c=P),
                                         ACT.Copy).then_inc(dn_newin, 1)
                    yield
                    act.wait_ge(dn_St, b + 1)
                    nc.scalar.activation(dn_S[:], side[:, 0, 0:2 * P].rearrange("p (e c) -> p e c", c=P),
                                         ACT.Copy).then_inc(dn_Sin, 1)
                    yield
                    yield
                    act.wait_ge(dn_new, 2 * b + 2)
                    nc.scalar.activation(vnew[:, 2:4], side[:, 0, 0:2 * P].rearrange("p (e c) -> p e c", c=P),
                                         ACT.Copy).then_inc(dn_newin, 1)
                    yield
                    act.wait_ge(dn_ofull, b + 1)
                    if b:
                        act.wait_ge(dn_ms, b)
                    for u in range(4):
                        if u or b:
                            act.wait_ge(dn_sq, 4 * b + u)
                        nc.scalar.activation(dn_junk[:], dn_o[:, u], ACT.Square,
                                             accum_out=dn_ssq[:, u:u + 1]).then_inc(dn_sq, 1)
                    yield
                yield
                for c in range(NZ):
                    chunk_hi(e0 + NU + c, B[0], KW * (NU + c), None, None, vec_at["dn_norm_w"], 1)
                    yield

            def mix1(xdst, tail):
                g0, e0, xc = (at["mix1"][k] for k in ("g", "ev", "x"))
                g = g0
                scale = rstd[:, NORM["mix1"]]
                e_y = e0 + NU + NQ
                e_m = e_y + NU + NZ
                e_x = e_m + XC
                side_work = s5_and_delta(e_y)

                def leave(c, kind):
                    def tail(pos):
                        if pos == EVAC:
                            act.wait_ge(used, g0 + GC * (c + 1))
                            dst = {"z": zs, "gs": gs, "gd": gd}.get(kind)
                            if dst is None:
                                act.wait_ge(tp_full, e0 + c)
                                if 1 <= c <= NU:
                                    act.wait_ge(skip_done, c)
                            if kind == "gd":
                                act.wait_ge(tp_full, e_y + NU)
                            o = dict(z=NU + NQ, gs=NU + NQ + NZ, gd=NU + NQ + NZ + XC).get(kind, c)
                            for m in range(M):
                                to = evac[:, m] if dst is None else dst[:, m, cols(c - o)]
                                op = nc.scalar.activation(to, acc[:, c % 2, m], ACT.Silu if kind == "z" else ACT.Copy,
                                                          scale=scale[:, m:m + 1])
                            op.then_inc(left, 1)
                        if pos == SPLIT and kind == "u":
                            act.wait_ge(tp_full, e0 + c + 1)
                            nc.scalar.activation(uT[:, KW * c:KW * (c + 1)], tp[:], ACT.Copy).then_inc(copied, 1)
                        if pos == SPLIT + 2 and kind == "qkv":
                            act.wait_ge(dn_conved, c - NU + 1)
                            q = qkvT[:, KW * (c - NU):KW * (c - NU + 1)]
                            nc.scalar.activation(q, q, ACT.Silu).then_inc(qkv_act, 1)
                    return tail

                def advance():
                    if g - g0 >= LEAD:
                        return next(side_work, "end")

                for c, (kind, _) in enumerate(W_IN):
                    for pos in range(GC):
                        hi(g)
                        if c == 0 and pos == GC - 1:
                            act.wait_ge(rs, NORM["mix1"] + 1)
                        tail(pos)
                        seen.add(advance())
                        g += 1
                    tail = leave(c, kind)
                while "s5" not in seen and "end" not in seen:
                    seen.add(next(side_work, "end"))
                older = no_tail
                c0 = len(W_IN)

                def glu(j):
                    def tail(pos):
                        if pos == EVAC:
                            act.wait_ge(used, g0 + GC * c0 + GH * (2 * j + 2))
                            if j:
                                act.wait_ge(s5_part, j)
                            op = nc.scalar.activation(evac[:], acc[:, 1], ACT.Sigmoid).then_inc(glu_sig, 1)
                    return tail

                def both(j):
                    def tail(pos):
                        if pos == SPLIT:
                            chunk_hi(e_m + j, A[0], KW * j)
                    return tail

                def sigmoid(t, c, j):
                    act.wait_ge(left, c + 1)
                    nc.scalar.activation(t[:, :, cols(j)], t[:, :, cols(j)], ACT.Sigmoid).then_inc(gate_sig, 1)

                for c in range(3 * XC):
                    if c == 2 * XC:
                        for mark in side_work:
                            pass
                    for pos in range(GH):
                        hi(g)
                        tail(pos)
                        older(pos + GH)
                        if pos == 1 and c < 2 * XC and c % 2 == 0:
                            sigmoid(gs, NU + NQ + NZ + c // 2, c // 2)
                        if pos == 1 and c >= 2 * XC:
                            sigmoid(gd, NU + NQ + NZ + XC + c - 2 * XC, c - 2 * XC)
                        if c < 2 * XC:
                            next(side_work, None)
                        g += 1
                    older = tail if c else no_tail
                    tail = (glu(c // 2) if c % 2 else no_tail) if c < 2 * XC else both(c - 2 * XC)
                for c in range(XC):
                    for pos in range(GC):
                        hi(g)
                        tail(pos)
                        if c == 0 and pos < GH:
                            older(pos + GH)
                        g += 1
                    tail = x_tail(e_x + c, xc + c, c, xdst, weight_of(NEXT["mix1"]))
                return tail

            def attention():
                n, n_junk = ATT_WARM + 4, False
                for _ in range(ATT_WARM):
                    yield
                act.wait_ge(lr_full, 16)
                nc.scalar.activation(lr_hi[:], lr_w[:], ACT.Copy).then_inc(lr_split, 1)
                yield
                act.wait_ge(lr_mm, 1)
                act.wait_ge(rs, NORM["mix2"] + 1)
                for m in range(M):
                    op = nc.scalar.activation(lr2[:, m], side[:, 0, m * GR:(m + 1) * GR], ACT.Copy,
                                              scale=rstd[:, NORM["mix2"], m:m + 1])
                op.then_inc(lr_in, 1)
                yield
                act.wait_ge(lr_T, 1)
                nc.scalar.activation(lrT[:], side[0:GR, 0, 0:T], ACT.Copy).then_inc(lr_Tin, 1)
                yield
                act.wait_ge(al_mm, 1)
                for h in range(GHD):
                    w = vec_at["b_alpha_2"] + h
                    op = nc.scalar.activation(la[:, h], side[:, h // 2, (h % 2) * T:(h % 2 + 1) * T], ACT.Identity,
                                              bias=vecT[:, w:w + 1])
                op.then_inc(al_in, 1)
                act.wait_ge(al_abs, 1)
                nc.scalar.activation(lt[:], lt[:], ACT.Exp, scale=-1.0).then_inc(al_exp, 1)
                act.wait_ge(al_one, 1)
                nc.scalar.activation(lt[:], lt[:], ACT.Ln).then_inc(al_ln, 1)
                yield
                while n < ATT_SLOT:
                    n += 1
                    yield
                act.wait_ge(al_cum, 1)
                nc.scalar.activation(gdec[:], lt[:].rearrange("p h (n t) -> p h n t", t=LC)[:, :, :, LC - 1], ACT.Exp,
                                     scale=1.0 / GATE_NORM)
                nc.scalar.activation(la[:], lt[:], ACT.Exp, scale=1.0 / GATE_NORM).then_inc(al_dec, 1)
                act.wait_ge(qk_dec, 1)
                nc.scalar.activation(la[:], lt[:], ACT.Exp, scale=-1.0 / GATE_NORM).then_inc(al_dec, 1)
                yield
                act.wait_ge(qk_dec, 3)
                nc.scalar.activation(la[:], la[:], ACT.Exp, scale=1.0 / GATE_NORM).then_inc(al_dec, 1)
                yield
                act.wait_ge(gk_T, 1)
                nc.scalar.activation(ktT[:].rearrange("p m h d -> p m (h d)"), side[:], ACT.Copy).then_inc(gk_in, 1)
                yield
                yield
                for n in range(LN - 1):
                    yield
                for m in range(M):
                    act.wait_ge(g_o, m + 1)
                    for h in range(GHD):
                        o = side[:, h // 2, (h % 2) * GV:(h % 2 + 1) * GV]
                        if n_junk:
                            act.wait_ge(step_a, steps[0])
                        op = nc.scalar.activation(junk[:, 0, 0:GV], o, ACT.Square, accum_out=g_ssq[:, m, h:h + 1])
                        op.then_inc(step_a, 1)
                        steps[0] += 1
                        n_junk = True
                    act.wait_ge(step_a, steps[0])
                    nc.scalar.activation(vv[:, m], side[:].rearrange("p b n -> p (b n)"), ACT.Copy).then_inc(g_oin, 1)
                    yield

            def mix2(xdst, tail):
                g0, e0, xc = (at["mix2"][k] for k in ("g", "ev", "x"))
                g = g0
                scale = rstd[:, NORM["mix2"]]
                event = dict(u0=0, p0=1, u1=2, p1=3, q=4, k=5, y0=6, y1=7)
                e_x = e0 + len(event)
                side_work = attention()
                c_of = {}

                def leave(c, kind, n):
                    def tail(pos):
                        e = e0 + event.get(kind, event.get(f"{kind}{n}", 0))
                        if pos == EVAC:
                            act.wait_ge(used, g0 + GC * (c + 1))
                            to = evac[:]
                            if kind in ("v", "g"):
                                to = (vv if kind == "v" else sg)[:, :, cols(n)]
                            else:
                                act.wait_ge(tp_full, e)
                            for m in range(M):
                                op = nc.scalar.activation(to[:, m], acc[:, c % 2, m], ACT.Silu if kind == "g" else ACT.Copy,
                                                          scale=scale[:, m:m + 1])
                            op.then_inc(left, 1)
                        if pos == SPLIT and kind in ("u", "q", "k"):
                            act.wait_ge(tp_full, e + 1)
                            to = u2T[:, KW * n:KW * (n + 1)] if kind == "u" else (qd if kind == "q" else kt)[:]
                            nc.scalar.activation(to, tp[:], ACT.Copy, scale=P ** -0.5 if kind == "q" else 1.0).then_inc(copied, 1)
                        if pos == GC + 2 and kind == "u":
                            chunk_hi(e0 + event[f"p{n}"], A[0], KW * n, None, None, vec_at["pool_scale_2"] + KW * n)
                        if pos == SPLIT + 1 and kind == "g":
                            chunk_hi(e0 + event[f"y{n}"], A[0], KW * (VC + n), None, None, vec_at["gla_norm_2"], GV // P)
                    return tail

                older, n = no_tail, {}
                for c, (kind, _) in enumerate(W_IN2):
                    for pos in range(GC):
                        hi(g)
                        if c == 0 and pos == GC - 1:
                            act.wait_ge(rs, NORM["mix2"] + 1)
                        tail(pos)
                        older(pos + GC)
                        if g - g0 >= LEAD:
                            next(side_work, None)
                        g += 1
                    older = tail if c else no_tail
                    tail = leave(c, kind, n.get(kind, 0))
                    n[kind] = n.get(kind, 0) + 1
                for _ in side_work:
                    pass
                for c in range(XC):
                    for pos in range(GC):
                        hi(g)
                        tail(pos)
                        g += 1
                    tail = x_tail(e_x + c, xc + c, c, xdst, weight_of(NEXT["mix2"]))
                return tail

            act.wait_ge(vec_T, 2 + TAPS)
            nc.scalar.activation(vecT[:], side[:, 0, 0:VEC_ROWS], ACT.Copy).then_inc(vec_in, 1)
            for t in range(TAPS):
                nc.scalar.activation(taps[:, t], side[:, 0, P * (t + 1):P * (t + 1) + FT], ACT.Copy).then_inc(vec_in, 1)
            nc.scalar.activation(dtaps[:], side[:, 1, 0:DTAPS * QT].rearrange("p (t r) -> p t r", r=QT), ACT.Copy).then_inc(vec_in, 1)
            for m in range(M):
                act.wait_ge(x_full[m], 16)
            act.wait_ge(vec_in, 1)
            for c in range(XC):
                squares(c)
                chunk_hi(c, first_x[0], KW * c, weight_of(phases[1]))
            tail = no_tail
            seen = set()
            for ph in phases[1:]:
                if ph in ("ffn1", "ffn2", "ffn3"):
                    tail = ffn(ph, ph == "ffn1", B if ph in NEXT else None, A, tail)
                elif ph == "mix1":
                    tail = mix1(B if ph in NEXT else None, tail)
                elif ph == "mix2":
                    tail = mix2(B if ph in NEXT else None, tail)
            for pos in range(GC):
                tail(pos)

        @block.vector
        def _(dve):
            def lo(g, i=None, per=0):
                dve.wait_ge(hi_done, n_at(g + 1, i, per))
                s = g % RING
                nc.vector.tensor_tensor(w_lo[:, s], stage[:, s], w_hi[:, s].bitcast(F32), ALU.subtract).then_inc(lo_done, 1)

            def chunk_lo(op, dst, k0, weight=None, i=None, w0=None, w_period=KD):
                dve.wait_ge(hi_T, n_at(op + 1, i, 1))
                if w0 is not None:
                    for k in range(KW):
                        w = w0 + k % w_period
                        o = nc.vector.scalar_tensor_tensor(
                            out=dst[1][:, k0 + k], in0=tp[:, k], scalar=vecT[:, w:w + 1],
                            in1=dst[0][:, k0 + k].bitcast(F32), op0=ALU.mult, op1=ALU.subtract)
                    o.then_inc(op_T, 1)
                elif weight is None:
                    k = bass.ds(k0, KW)
                    nc.vector.tensor_tensor(dst[1][:, k], tp[:], dst[0][:, k].bitcast(F32), ALU.subtract).then_inc(op_T, 1)
                else:
                    for k in range(k0, k0 + KW):
                        o = nc.vector.scalar_tensor_tensor(
                            out=dst[1][:, k], in0=tp[:, k - k0], scalar=weight[:, k:k + 1],
                            in1=dst[0][:, k].bitcast(F32), op0=ALU.mult, op1=ALU.subtract)
                    o.then_inc(op_T, 1)

            def norm(n):
                k = NORM[n]
                dve.wait_ge(sq, sq_count[n])
                nc.vector.tensor_reduce(out=sumsq[:, k], in_=ssq[:], axis=AX.X, op=ALU.add).then_inc(sums, 1)
                dve.wait_ge(sums, k + 1)
                nc.vector.tensor_scalar(mean[:, k], sumsq[:, k], 1.0 / D, EPS, ALU.mult, ALU.add).then_inc(ms, 1)

            def no_tail(pos):
                pass

            def x_tail(g, op, xc, c, alpha, dst, weight, after):
                def tail(pos):
                    if pos == EVAC:
                        dve.wait_ge(used, g)
                        dve.wait_ge(*after)
                        nc.vector.scalar_tensor_tensor(out=x[:, :, cols(c)], in0=acc[:, c % 2], scalar=alpha,
                                                       in1=x[:, :, cols(c)], op0=ALU.mult, op1=ALU.add).then_inc(x_new, 1)
                    if pos == SPLIT and dst is not None:
                        chunk_lo(op, dst, KW * c, weight)
                return tail

            def norm_tail(n, before):
                def tail(pos):
                    before(pos)
                    if pos == SPLIT + 1:
                        norm(n)
                return tail

            def apply_norm(n, m):
                nc.vector.scalar_tensor_tensor(out=x[:, m], in0=x[:, m], scalar=rstd[:, NORM[n], m:m + 1],
                                               in1=fnorm[:], op0=ALU.mult, op1=ALU.mult).then_inc(scaled, 1)

            def block_end_tail(nxt, op, before):
                def tail(pos):
                    before(pos)
                    if pos == SPLIT + 1:
                        norm("block end")
                    if pos in (SPLIT + 2, SPLIT + 3):
                        if pos == SPLIT + 2:
                            dve.wait_ge(rs, NORM["block end"] + 1)
                            dve.wait_ge(fnorm_full, 16)
                            dve.wait_ge(op_T, op)
                        apply_norm("block end", pos - SPLIT - 2)
                    if pos == SPLIT + 5:
                        norm(nxt)
                        dve.wait_ge(rs, NORM[nxt] + 1)
                        nc.vector.tensor_tensor(row_scale[:], rstd[:, NORM[nxt]], rstd[:, NORM["block end"]],
                                                ALU.mult).then_inc(rescaled, 1)
                return tail

            def ffn(ph, conv, alpha, xdst, adst, tail, x_after):
                at_ph = at[ph]
                g0, ev, op, sr, xc, q0, cv, pr = (at_ph[k] for k in ("g", "ev", "op", "src", "x", "gate", "conv", "prod"))
                weight = weight_of(NEXT[ph]) if ph in NEXT else None
                both = ph == "ffn2" and two_norms
                scale = row_scale[:, :] if both else rstd[:, NORM[ph]]
                per = 2 if conv else 1

                def convolve(cv, e, ft, dst, free, i=None):
                    dve.wait_ge(tp_full, n_at(e + 1, i, 2))
                    dve.wait_ge(*free)
                    steps = 2 * KW
                    for k in range(KW):
                        w = taps[:, TAPS - 1, bass.ds(ft + k, 1)]
                        nc.vector.tensor_scalar(dst[:, k], tp[:, k], w, None, ALU.mult).then_inc(tap_step, 1)
                    for back in range(1, TAPS):
                        for k in range(KW):
                            dve.wait_ge(tap_step, n_at(steps * cv + KW * (back - 1) + k + 1, i, 2 * steps))
                            w = taps[:, TAPS - 1 - back, bass.ds(ft + k, 1)]
                            o = nc.vector.scalar_tensor_tensor(
                                out=dst[:, k, back:T], in0=tp[:, k, 0:T - back], scalar=w, in1=dst[:, k, back:T],
                                op0=ALU.mult, op1=ALU.add)
                            if back < TAPS - 1:
                                o.then_inc(tap_step, 1)
                    o.then_inc(conved, 1)

                def pair(g, e, cv, ft, op, before, i=None):
                    for pos in range(2 * GC):
                        lo(g + pos, i, 2 * GC)
                        before(pos)
                        if pos == GC + SPLIT and conv:
                            convolve(cv, e, ft, conv_g, (prod, n_at(op, i, 1)), i)

                def pair_tail(g, e, q, sr, cv, op, pr, ft, k0, i=None):
                    def tail(pos):
                        if pos == EVAC and not conv:
                            dve.wait_ge(used, n_at(g, i, 2 * GC))
                            dve.wait_ge(gated, n_at(q + 1, i, 1))
                            dve.wait_ge(tp_full, n_at(e, i, 1))
                            for m in range(M):
                                o = nc.vector.scalar_tensor_tensor(
                                    out=evac[:, m], in0=acc[:, 1, m], scalar=scale[:, m:m + 1], in1=sgate[:, m],
                                    op0=ALU.mult, op1=ALU.mult)
                            o.then_inc(src, 1)
                        if pos == SPLIT and not conv:
                            chunk_lo(op, adst, k0, None, i)
                        if pos == SPLIT and conv:
                            convolve(cv, e, ft, conv_v, (op_T, n_at(op, i, 1)), i)
                            dve.wait_ge(gated, n_at(q + 1, i, 1))
                            dve.wait_ge(conved, n_at(cv + 1, i, 2))
                            nc.vector.tensor_tensor(conv_v[:], conv_v[:], conv_g[:], ALU.mult).then_inc(prod, 1)
                            dve.wait_ge(hi_T, n_at(op + 1, i, 1))
                            k = bass.ds(k0, KW)
                            nc.vector.tensor_tensor(adst[1][:, k], conv_v[:], adst[0][:, k].bitcast(F32),
                                                    ALU.subtract).then_inc(op_T, 1)
                    return tail

                ft = 0
                for p, n in enumerate(PARTS):
                    pair(g0, ev, cv, ft, pr, tail)
                    with dve.Fori(1, n) as i:
                        last = pair_tail(g0, ev - 1, q0 - 1, sr - 1, cv - 1, op - 1, pr - 1,
                                         i * KW + (FT // 2 + ft - KW), i * KW - KW, i)
                        pair(g0, ev, cv, i * KW + ft, pr, last, i)
                    g0, sr, ev, cv = g0 + 2 * GC * n, sr + per * n, ev + per * n, cv + 2 * n
                    pr, q0, op, ft = pr + n, q0 + n, op + n, ft + KW * n
                    tail = pair_tail(g0, ev - 1, q0 - 1, sr - 1, cv - 1, op - 1, pr - 1, FT // 2 + ft - KW, KW * (n - 1))
                    for c in range(XC):
                        for pos in range(KW * n // KG):
                            lo(g0)
                            g0 += 1
                            tail(pos)
                        end = p == len(PARTS) - 1 and xdst is not None
                        tail = x_tail(g0, op, xc + c, c, alpha, xdst if end else None, weight, x_after)
                        op += end
                        x_after = (x_new, xc + c + 2 - XC) if p or c == XC - 1 else x_after
                        x_after = (x_new, xc + c + 2 - XC) if xc + c + 2 - XC > at_ph["x"] else x_after
                    xc += XC
                if ph == "ffn1" and two_norms:
                    return block_end_tail(NEXT[ph], op, tail)
                return norm_tail(NEXT.get(ph, "result"), tail)

            if two_norms:
                dve.wait_ge(vec_in, 1)
                f, n1 = vec_at["final_norm_w"], vec_at[NORM_W["ffn2"]]
                nc.vector.tensor_tensor(blk_w[:], vecT[:, f:f + KD], vecT[:, n1:n1 + KD], ALU.mult).then_inc(blk_ready, 1)
            steps = [0]

            def link(op):
                op.then_inc(step_d, 1)
                steps[0] += 1
                dve.wait_ge(step_d, steps[0])

            def free_wide(t, n):
                return t.unsqueeze(len(t.shape)).to_broadcast(list(t.shape) + [n])

            TT, TS, STT = nc.vector.tensor_tensor, nc.vector.tensor_scalar, nc.vector.scalar_tensor_tensor

            def s5_and_delta(o0):
                def fractions(t):
                    b = t % 2
                    dve.wait_ge(s5_turn, t + 1)
                    if t >= 2:
                        dve.wait_ge(s5_sin, t - 1)
                    link(STT(out=frac[:, b], in0=tok[:], scalar=s5p[:, 2, t:t + 1], in1=turn[:, b],
                             op0=ALU.mult, op1=ALU.subtract))
                    link(STT(out=frac[:, b], in0=tok[:], scalar=s5p[:, 3, t:t + 1], in1=frac[:, b],
                             op0=ALU.mult, op1=ALU.add))
                    TS(frac[:, b], frac[:, b], 0.5, -0.5, ALU.min, ALU.max).then_inc(s5_frac, 1)

                def cosines(t):
                    b = t % 2
                    dve.wait_ge(s5_sin, t + 1)
                    link(TS(cs[:, b], sin_h[:, b], -2.0, 1.0, ALU.mult, ALU.add))

                r = {n: t[:] for n, t in row.items()}
                g2 = P // SP_
                dve.wait_ge(par_dt, 1)
                dt = free_wide(s5_dt[:], SP_)
                lr, li = (r[n].rearrange("t (g p) -> t g p", g=g2) for n in ("lr", "li"))
                TT(r["lrdt"].rearrange("t (g p) -> t g p", g=g2), lr, dt, ALU.mult)
                link(TT(r["th"].rearrange("t (g p) -> t g p", g=g2), li, dt, ALU.mult))
                link(TS(r["k"], r["th"], IN_TURNS, MAGIC, ALU.mult, ALU.add))
                link(TS(r["k"], r["k"], MAGIC, None, ALU.subtract))
                for c in (TURN_1, TURN_2, TURN_3):
                    link(STT(out=r["th"], in0=r["k"], scalar=-c, in1=r["th"], op0=ALU.mult, op1=ALU.add))
                link(TS(r["f"], r["th"], IN_TURNS, None, ALU.mult))
                TS(r["f"], r["f"], 0.5, -0.5, ALU.min, ALU.max).then_inc(par_th, 1)
                dve.wait_ge(ba_split, 1)
                TT(ba_lo[:], ba_w[:], ba_hi[:].bitcast(F32), ALU.subtract).then_inc(ba_split, 1)
                dve.wait_ge(par_trig, 1)
                TS(row_fhi[:], r["f"], 1.0, None, ALU.mult)
                TT(r["t1"], r["lr"], r["lr"], ALU.mult)
                TT(r["t2"], r["li"], r["li"], ALU.mult)
                TT(r["ai"], r["mag"], r["sn"], ALU.mult)
                link(TS(r["cs"], r["sh"], -2.0, 1.0, ALU.mult, ALU.add))
                link(TT(r["ar"], r["mag"], r["cs"], ALU.mult))
                TT(r["flo"], r["f"], row_fhi[:].bitcast(F32), ALU.subtract)
                TT(r["den"], r["t1"], r["t2"], ALU.add)
                link(TS(r["ar"], r["ar"], 1.0, None, ALU.subtract))
                TT(r["t1"], r["ar"], r["lr"], ALU.mult)
                link(TT(r["t2"], r["ai"], r["li"], ALU.mult))
                link(TT(r["cr"], r["t1"], r["t2"], ALU.add))
                TT(r["t1"], r["ai"], r["lr"], ALU.mult)
                link(TT(r["t2"], r["ar"], r["li"], ALU.mult))
                TT(r["ci"], r["t1"], r["t2"], ALU.subtract)
                link(nc.vector.reciprocal(r["den"], r["den"]))
                TT(r["cr"], r["cr"], r["den"], ALU.mult)
                TT(r["ci"], r["ci"], r["den"], ALU.mult).then_inc(par_done, 1)
                yield
                dve.wait_ge(par_in, 1)
                dve.wait_ge(s5_bc_full, 64)
                dve.wait_ge(consts, const_total)
                cr, ci = (free_wide(s5p[:, 4 + n], SH) for n in range(2))
                for n, (p, q, op) in enumerate(((cr, ci, ALU.subtract), (ci, cr, ALU.add))):
                    if n:
                        dve.wait_ge(step_d, steps[0])
                    TT(b_t[:, 0], b_nat[:, 0], p, ALU.mult)
                    link(TT(b_t[:, 1], b_nat[:, 1], q, ALU.mult))
                    for e in range(g2):
                        s = slice(e * SP_, (e + 1) * SP_)
                        o = TT(b_wide[s, n, :, e], b_t[s, 0], b_t[s, 1], op)
                    link(o)
                link(nc.vector.tensor_reduce(out=par[:], in_=ident[:].rearrange("p (j g h) -> p g j h", g=g2, h=SH),
                                             axis=AX.XY, op=ALU.add))
                for n in range(2):
                    for e in range(g2):
                        o = TS(c_wide[:, n, :, e], c_nat[:, n], par[:, e:e + 1], None, ALU.mult)
                o.then_inc(wide_b, 1)
                nc.vector.tensor_copy(tok[:], tok_i[:]).then_inc(tok_done, 1)
                dve.wait_ge(ba_in, 1)
                dve.wait_ge(dnp_full, 32)
                TS(ba[:, :, 0:H], ba[:, :, 0:H], -1.0, None, ALU.mult)
                link(TT(ba[:, :, H:2 * H], ba[:, :, H:2 * H], dt_row[:].unsqueeze(1).to_broadcast([P, M, H]), ALU.add))
                STT(out=ba_abs[:], in0=ba[:], scalar=-1.0, in1=ba[:], op0=ALU.mult, op1=ALU.max).then_inc(ba_neg, 1)
                dve.wait_ge(ba_log, 1)
                TS(ba_ln[:], ba_ln[:], 1.0, None, ALU.add).then_inc(ba_neg, 1)
                dve.wait_ge(ba_log, 3)
                link(STT(out=ba_ln[:], in0=ba[:], scalar=0.0, in1=ba_ln[:], op0=ALU.max, op1=ALU.add))
                TS(dv["lnb"][:], ba_ln[:, :, 0:H], -1.0, None, ALU.mult)
                STT(out=dn_g[:], in0=ba_ln[:, :, H:2 * H], scalar=-1.0,
                    in1=ea_row[:].unsqueeze(1).to_broadcast([P, M, H]), op0=ALU.mult, op1=ALU.mult).then_inc(dn_gate, 1)
                yield
                for q in range(4):
                    yield
                dve.wait_ge(dn_cum, 1)
                nc.vector.tensor_copy(dv["cum"][:], side[:, 0, 0:M * H].rearrange("p (m h) -> p m h", h=H))
                nc.vector.tensor_copy(dn_tail[:], side[:, 0, M * H:M * H + H]).then_inc(dn_gate, 1)
                yield
                fractions(0)
                cosines(0)
                n = 7
                while n < S5_SLOT:
                    n += 1
                    yield
                for t in range(ST):
                    b, c, j = t % 2, t // SJ, t % SJ
                    two = lambda v: v.unsqueeze(1).to_broadcast([P, 2, T])
                    dve.wait_ge(s5_bu, t + 1)
                    if t >= 2:
                        dve.wait_ge(s5_y, t - 1)
                    bu = side[:, 0].rearrange("p (n t) -> p n t", t=T)
                    TT(p_c[:], bu, two(cs[:, b]), ALU.mult)
                    TT(p_s[:], bu, two(sn[:, b]), ALU.mult).then_inc(s5_rot, 1)
                    dve.wait_ge(s5_rot, t + 1)
                    TT(rot[:, b, 0], p_c[:, 0], p_s[:, 1], ALU.add)
                    link(TT(rot[:, b, 1], p_c[:, 1], p_s[:, 0], ALU.subtract))
                    if t + 1 < ST:
                        fractions(t + 1)
                    yield
                    for n in range(2):
                        o = nc.vector.tensor_tensor_scan(scn[:, n], s5p[:, 0, t:t + 1].to_broadcast([P, T]), rot[:, b, n],
                                                         0.0, ALU.mult, ALU.add)
                    link(o)
                    TT(p_c[:], scn[:], two(cs[:, b]), ALU.mult)
                    link(TT(p_s[:], scn[:], two(sn[:, b]), ALU.mult))
                    TT(rot[:, b, 0], p_c[:, 0], p_s[:, 1], ALU.subtract)
                    TT(rot[:, b, 1], p_c[:, 1], p_s[:, 0], ALU.add).then_inc(s5_x, 1)
                    dve.wait_ge(s5_x, t + 1)
                    if t + 1 < ST:
                        cosines(t + 1)
                    if t and j == 0:
                        outputs(c - 1)
                    yield
                outputs(CT - 1)
                yield
                for c in range(NU):
                    chunk_lo(o0 + c, B, KW * c)
                    yield
                yield "s5"
                for j in range(2 * H // KW):
                    yield
                dve.wait_ge(qk_ss, 2 * H // KW)
                TS(dn_ss[:], side[:, 0, 0:M * 2 * H].rearrange("p (m n) -> p m n", m=M), EPS, None, ALU.add).then_inc(dn_ssin, 1)
                dve.wait_ge(dn_lns, 1)
                lq, lk = dn_ss[:, :, 0:H], dn_ss[:, :, H:2 * H]
                dve.wait_ge(dn_gate, 2)
                STT(out=dv["colq"][:], in0=lq, scalar=-0.5, in1=dv["cum"][:], op0=ALU.mult, op1=ALU.add)
                STT(out=dv["colk"][:], in0=lk, scalar=-0.5, in1=dv["cum"][:], op0=ALU.mult, op1=ALU.add)
                link(STT(out=dv["rowk"][:], in0=lk, scalar=-0.5, in1=dv["cum"][:], op0=ALU.mult, op1=ALU.subtract))
                TS(dv["colq"][:], dv["colq"][:], Q_LOG, None, ALU.add)
                TT(dv["colk"][:], dv["colk"][:], dv["lnb"][:], ALU.add)
                TT(dn_tail[:], dn_tail[:], dv["rowk"][:, 0], ALU.add).then_inc(dn_rows, 1)
                dve.wait_ge(dn_fac, 1)
                TS(dv["nwk"][:], dv["wk"][:], -1.0, None, ALU.mult).then_inc(dn_nwk, 1)
                yield
                four = lambda v: v.unsqueeze(1).to_broadcast([P, 4, P])
                bank = lambda b: side[:, b].rearrange("p (u c) -> p u c", c=P)

                def results(b):
                    dve.wait_ge(dn_rs, b + 1)
                    for u in range(4):
                        z = zs[:, u % 2, (2 * b + u // 2) * P:(2 * b + u // 2 + 1) * P]
                        o = STT(out=z, in0=dn_o[:, u], scalar=dn_rstd[:, u:u + 1], in1=z, op0=ALU.mult, op1=ALU.mult)
                    o.then_inc(dn_y, 1)

                dve.wait_ge(masks, mask_total)
                dve.wait_ge(left, NU + NQ + NZ)
                for b in range(H // 2):
                    dve.wait_ge(dn_expo, b + 1)
                    if b:
                        dve.wait_ge(dn_LA, b)
                    TT(dec[:, 0], bank(0), four(expo_mask[:, 0]), ALU.add)
                    TT(dec[:, 1], bank(1), four(expo_mask[:, 1]), ALU.add).then_inc(dn_masked, 1)
                    if b:
                        results(b - 1)
                    yield
                    yield
                    dve.wait_ge(dn_kk, b + 1)
                    dve.wait_ge(dn_decay, b + 1)
                    TT(LT[:], bank(0), dec[:, 0], ALU.mult)
                    TT(AT[:], bank(1), dec[:, 1], ALU.mult).then_inc(dn_LA, 1)
                    dve.wait_ge(dn_LA, b + 1)
                    link(TT(LK[:], LT[:], four(lev_mask[:, 0]), ALU.mult))
                    TT(DT[:], four(ident[:]), LK[:], ALU.subtract).then_inc(dn_D, 1)
                    yield
                    dve.wait_ge(dn_DT, b + 1)
                    nc.vector.tensor_copy(DD[:], bank(0))
                    TT(LK[:], LT[:], four(lev_mask[:, 1]), ALU.mult).then_inc(dn_lev, 1)
                    yield
                    for l in range(1, LEVELS):
                        yield
                        dve.wait_ge(dn_X, (LEVELS - 1) * b + l)
                        dve.wait_ge(dn_lev, LEVELS * b + l)
                        o = TT(DT[:], DT[:], bank(1), ALU.subtract)
                        if l + 1 < LEVELS:
                            TT(DD[:], DD[:], bank(0), ALU.subtract)
                            o = TT(LK[:], LT[:], four(lev_mask[:, l + 1]), ALU.mult)
                        o.then_inc(dn_lev, 1)
                        yield
                    yield
                    dve.wait_ge(dn_St, b + 1)
                    nc.vector.tensor_copy(dn_o[:].rearrange("p (e m) c -> p m e c", m=M)[:, 0],
                                          side[:, 1, 0:2 * P].rearrange("p (e c) -> p e c", c=P)).then_inc(dn_o0, 1)
                    yield
                    dve.wait_ge(dn_kS, b + 1)
                    for e in range(2):
                        h = 2 * b + e
                        STT(out=rhs1[:, e], in0=side[:, 0, e * P:(e + 1) * P], scalar=dv["nwk"][:, 1, h:h + 1],
                            in1=vb[:, 2 * e + 1], op0=ALU.mult, op1=ALU.add)
                        o = TS(qS[:, e], side[:, 0, (2 + e) * P:(3 + e) * P], dv["wq"][:, 1, h:h + 1], None, ALU.mult)
                    o.then_inc(dn_rhs, 1)
                    yield
                    yield
                    dve.wait_ge(dn_out, b + 1)
                    dve.wait_ge(dn_rhs, b + 1)
                    TT(dn_o[:].rearrange("p (e m) c -> p m e c", m=M)[:, 1],
                       side[:, 1, 0:2 * P].rearrange("p (e c) -> p e c", c=P), qS[:], ALU.add).then_inc(dn_ofull, 1)
                    dve.wait_ge(dn_sq, 4 * (b + 1))
                    if b:
                        dve.wait_ge(dn_rs, b)
                    TS(dn_mean[:], dn_ssq[:], 1.0 / P, EPS, ALU.mult, ALU.add).then_inc(dn_ms, 1)
                    yield
                results(H // 2 - 1)
                yield
                for c in range(NZ):
                    chunk_lo(o0 + NU + c, B, KW * (NU + c), None, None, vec_at["dn_norm_w"], 1)
                    yield

            def outputs(c):
                dve.wait_ge(s5_y, SJ * (c + 1))
                if c % KW == 0:
                    dve.wait_ge(skip_done, c // KW + 1)
                u = ud[:, :, c * P:(c + 1) * P]
                TT(u, side[:, 1, 0:M * P].rearrange("p (m c) -> p m c", m=M), u, ALU.add).then_inc(s5_res, 1)

            def mix1(xdst, tail):
                g0, e0, o0, xc = (at["mix1"][k] for k in ("g", "ev", "op", "x"))
                g = g0
                o_m = o0 + NU + NZ
                side_work = s5_and_delta(o0)

                def convolve(q):
                    def tiles(ks):
                        for k in ks:
                            link(TS(qkvT[:, KW * q + k], tp[:, k], dtaps[:, DTAPS - 1, KW * q + k:KW * q + k + 1], None, ALU.mult))
                        for back in range(1, DTAPS):
                            for k in ks:
                                n = KW * q + k
                                o = STT(out=qkvT[:, n, back:T], in0=tp[:, k, 0:T - back],
                                        scalar=dtaps[:, DTAPS - 1 - back, n:n + 1], in1=qkvT[:, n, back:T],
                                        op0=ALU.mult, op1=ALU.add)
                                if back < DTAPS - 1:
                                    link(o)
                        return o
                    return tiles

                def leave(c, kind):
                    def tail(pos):
                        if pos == EVAC + 1 and kind == "u":
                            dve.wait_ge(left, c + 1)
                            dve.wait_ge(d_full, 16)
                            TT(ud[:, :, cols(c)], evac[:], d_row[:, cols(c)].unsqueeze(1).to_broadcast([P, M, NW]),
                               ALU.mult).then_inc(skip_done, 1)
                        if kind == "qkv" and pos in (SPLIT, SPLIT + 1):
                            if pos == SPLIT:
                                dve.wait_ge(tp_full, e0 + c + 1)
                            o = convolve(c - NU)(range(KW // 2) if pos == SPLIT else range(KW // 2, KW))
                            if pos == SPLIT + 1:
                                o.then_inc(dn_conved, 1)
                    return tail

                for c, (kind, _) in enumerate(W_IN):
                    for pos in range(GC):
                        lo(g)
                        tail(pos)
                        if g - g0 >= LEAD:
                            seen.add(next(side_work, "end"))
                        g += 1
                    tail = leave(c, kind)
                while "s5" not in seen and "end" not in seen:
                    seen.add(next(side_work, "end"))
                older = no_tail
                gg = g0 + GC * len(W_IN)

                def linear(j):
                    def tail(pos):
                        if pos == EVAC:
                            dve.wait_ge(used, gg + GH * (2 * j + 1))
                            dve.wait_ge(gate_sig, j + 1)
                            TT(gs[:, :, cols(j)], acc[:, 0], gs[:, :, cols(j)], ALU.mult).then_inc(glu_a, 1)
                    return tail

                def glu(j):
                    def tail(pos):
                        if pos == EVAC + 1:
                            dve.wait_ge(glu_sig, j + 1)
                            dve.wait_ge(glu_a, j + 1)
                            TT(gs[:, :, cols(j)], gs[:, :, cols(j)], evac[:], ALU.mult).then_inc(s5_part, 1)
                    return tail

                def both(j):
                    def tail(pos):
                        if pos == EVAC:
                            dve.wait_ge(used, gg + GH * (2 * XC + j + 1))
                            dve.wait_ge(gate_sig, XC + j + 1)
                            link(TT(gd[:, :, cols(j)], acc[:, j % 2], gd[:, :, cols(j)], ALU.mult))
                            dve.wait_ge(s5_part, j + 1)
                            TT(gs[:, :, cols(j)], gs[:, :, cols(j)], gd[:, :, cols(j)], ALU.add).then_inc(merged, 1)
                        if pos == SPLIT:
                            chunk_lo(o_m + j, A, KW * j)
                    return tail

                tail = no_tail
                for c in range(3 * XC):
                    if c == 2 * XC:
                        for _ in side_work:
                            pass
                    for pos in range(GH):
                        lo(g)
                        tail(pos)
                        older(pos + GH)
                        if c < 2 * XC:
                            next(side_work, None)
                        g += 1
                    older = tail
                    tail = both(c - 2 * XC) if c >= 2 * XC else glu(c // 2) if c % 2 else linear(c // 2)
                for c in range(XC):
                    for pos in range(GC):
                        lo(g)
                        tail(pos)
                        if c == 0 and pos < GH:
                            older(pos + GH)
                        g += 1
                    tail = x_tail(g, o_m + XC + c, xc + c, c, 1.0, xdst, weight_of(NEXT["mix1"]), (x_again, 16 * M))
                return norm_tail(NEXT["mix1"], tail)

            def attention():
                for _ in range(ATT_WARM):
                    yield
                dve.wait_ge(lr_split, 1)
                TT(lr_lo[:], lr_w[:], lr_hi[:].bitcast(F32), ALU.subtract).then_inc(lr_split, 1)
                nc.vector.memset(sc[:], 0.0).then_inc(g_scin, 1)
                yield
                yield
                yield
                dve.wait_ge(al_in, 1)
                STT(out=lt[:], in0=la[:], scalar=-1.0, in1=la[:], op0=ALU.mult, op1=ALU.max).then_inc(al_abs, 1)
                dve.wait_ge(al_exp, 1)
                TS(lt[:], lt[:], 1.0, None, ALU.add).then_inc(al_one, 1)
                yield
                dve.wait_ge(al_ln, 1)
                link(STT(out=la[:], in0=la[:], scalar=0.0, in1=lt[:], op0=ALU.min, op1=ALU.subtract))
                for h in range(GHD):
                    for n in range(LN):
                        t = slice(n * LC, (n + 1) * LC)
                        o = nc.vector.tensor_tensor_scan(lt[:, h, t], ones[:, 0:1].to_broadcast([P, LC]), la[:, h, t],
                                                         0.0, ALU.mult, ALU.add)
                o.then_inc(al_cum, 1)
                n = ATT_WARM + 4
                while n < ATT_SLOT:
                    n += 1
                    yield
                dve.wait_ge(al_dec, 1)
                dve.wait_ge(copied, copied0 + 4)
                TT(qd[:], qd[:], la[:], ALU.mult).then_inc(qk_dec, 1)
                dve.wait_ge(al_dec, 2)
                TT(ki[:], kt[:], la[:], ALU.mult).then_inc(qk_dec, 1)
                dve.wait_ge(qk_dec, 2)
                by_chunk = lt[:].rearrange("p h (n t) -> p (h n) t", t=LC)
                dve.wait_ge(al_cum, 1)
                TT(la[:].rearrange("p h (n t) -> p (h n) t", t=LC), by_chunk[:, :, LC - 1:LC].to_broadcast([P, GHD * LN, LC]),
                   by_chunk, ALU.subtract).then_inc(qk_dec, 1)
                yield
                dve.wait_ge(al_dec, 3)
                TT(kt[:], kt[:], la[:], ALU.mult).then_inc(qk_dec, 1)
                yield
                yield
                dve.wait_ge(g_sc, 1)
                dve.wait_ge(g_scin, 1)
                for m in range(M):
                    o = nc.vector.copy_predicated(sc[:, m], score_mask[:].unsqueeze(1).to_broadcast([P, GHD, P]),
                                                  side[:, m].rearrange("p (h i) -> p h i", i=P))
                o.then_inc(g_scin, 1)
                yield
                for n in range(LN - 1):
                    dve.wait_ge(g_kv, n + 1)
                    kv = lambda h: side[:, h // 2, (h % 2) * GV:(h % 2 + 1) * GV]
                    if n:
                        dve.wait_ge(g_S, n)
                    for h in range(GHD):
                        if n:
                            o = STT(out=Sg[:, n, h], in0=Sg[:, n - 1, h], scalar=gdec[:, h, n:n + 1], in1=kv(h),
                                    op0=ALU.mult, op1=ALU.add)
                        else:
                            o = nc.vector.tensor_copy(Sg[:, n, h], kv(h))
                    o.then_inc(g_S, 1)
                    yield
                yield
                dve.wait_ge(g_oin, M)
                TS(g_mean[:], g_ssq[:], 1.0 / GV, EPS, ALU.mult, ALU.add).then_inc(g_ms, 1)
                yield

            def mix2(xdst, tail):
                g0, e0, o0, xc = (at["mix2"][k] for k in ("g", "ev", "op", "x"))
                g = g0
                side_work = attention()

                def pool(n, half_):
                    ks = slice(KW * n, KW * (n + 1))
                    u, s, t = u2T[:, ks], pool_a[:, ks], pool_b[:, ks]
                    src_ = u
                    lv = range(0, 2 * n + 1) if half_ == 0 else range(2 * n + 1, 2 * n + 2)
                    k0 = 0 if half_ == 0 else KW // 2
                    for l in lv:
                        d = 1 << l
                        if l:
                            src_ = (s, t)[(l - 1) % 2]
                        dst = (s, t)[l % 2]
                        nc.vector.tensor_copy(dst[:, k0:, 0:d], src_[:, k0:, 0:d])
                        link(TT(dst[:, k0:, d:T], src_[:, k0:, d:T], src_[:, k0:, 0:T - d], ALU.add))
                    l = lv[-1]
                    w = 2 << l
                    k = slice(k0, k0 + KW // 2)
                    sm, o = (s, t)[l % 2][:, k], (t, s)[l % 2][:, k]
                    link(STT(out=o, in0=sm, scalar=1.0 / w, in1=u[:, k], op0=ALU.mult, op1=ALU.subtract))
                    c = rcnt[:, l].unsqueeze(1).to_broadcast([P, KW // 2, 16])
                    link(TT(o[:, :, 0:16], sm[:, :, 0:16], c, ALU.mult))
                    return TT(o[:, :, 0:16], o[:, :, 0:16], u[:, k, 0:16], ALU.subtract)

                def leave(c, kind, n):
                    def tail(pos):
                        if kind == "u" and pos == SPLIT + 1:
                            dve.wait_ge(copied, copied0 + n + 1)
                            dve.wait_ge(lr_mm, 1)
                            dve.wait_ge(masks, mask_total)
                            link(pool(n, 0))
                        if kind == "u" and pos == SPLIT + 2:
                            pool(n, 1).then_inc(pooled, 1)
                        if kind == "u" and pos == GC + 2:
                            chunk_lo(o0 + n, A, KW * n, None, None, vec_at["pool_scale_2"] + KW * n)
                        if kind == "g" and pos == EVAC + 1:
                            dve.wait_ge(g_rs, 1)
                            dve.wait_ge(left, left0 + c + 1)
                            for m in range(M):
                                for h in range(NW // GV * n, NW // GV * (n + 1)):
                                    v = slice(h * GV, (h + 1) * GV)
                                    o = STT(out=vv[:, m, v], in0=vv[:, m, v], scalar=g_rstd[:, m, h:h + 1], in1=sg[:, m, v],
                                            op0=ALU.mult, op1=ALU.mult)
                            o.then_inc(g_y, 1)
                        if kind == "g" and pos == SPLIT + 1:
                            chunk_lo(o0 + VC + n, A, KW * (VC + n), None, None, vec_at["gla_norm_2"], GV // P)
                    return tail

                older, n = no_tail, {}
                for c, (kind, _) in enumerate(W_IN2):
                    for pos in range(GC):
                        lo(g)
                        tail(pos)
                        older(pos + GC)
                        if g - g0 >= LEAD:
                            next(side_work, None)
                        g += 1
                    older = tail if c else no_tail
                    tail = leave(c, kind, n.get(kind, 0))
                    n[kind] = n.get(kind, 0) + 1
                for _ in side_work:
                    pass
                for c in range(XC):
                    for pos in range(GC):
                        lo(g)
                        tail(pos)
                        g += 1
                    tail = x_tail(g, o0 + 2 * VC + c, xc + c, c, 1.0, xdst, weight_of(NEXT["mix2"]), x_after)
                return norm_tail(NEXT["mix2"], tail)

            dve.wait_ge(vec_in, 2 + TAPS)
            for c in range(XC):
                chunk_lo(c, first_x, KW * c, weight_of(phases[1]))
            seen = set()
            norm(phases[1])
            tail = no_tail
            x_after = (x_full[M - 1], 16)
            for ph in phases[1:]:
                if ph in ("ffn1", "ffn2", "ffn3"):
                    tail = ffn(ph, ph == "ffn1", 1.0 if ph == "ffn1" else 0.5, B if ph in NEXT else None, A, tail, x_after)
                elif ph == "mix1":
                    tail = mix1(B if ph in NEXT else None, tail)
                elif ph == "mix2":
                    tail = mix2(B if ph in NEXT else None, tail)
                x_after = (scaled, M) if ph == "ffn1" and two_norms else (x_new, at[ph]["x"] + size[ph]["x"])
            for pos in range(GC):
                tail(pos)
            dve.wait_ge(rs, NORMS)
            dve.wait_ge(fnorm_full, 32 if two_norms and phases[-1] != "ffn1" else 16)
            dve.wait_ge(sq, sq_count["result"])
            for m in range(M):
                apply_norm("result", m)

        @block.tensor
        def _(pe):
            def products(g, xT, k0, s, first, last, i=None, per=0):
                pe.wait_ge(lo_done, n_at(g + 1, i, per))
                r = g % RING
                for kk in range(KG):
                    for m in range(M):
                        xh, xl = (xT[h][:, k0 + kk, m * P:(m + 1) * P] for h in (0, 1))
                        st, en = first and kk == 0, last and kk == KG - 1
                        nc.tensor.matmul(acc[:, s, m], xh, w_hi[:, r, kk], start=st, stop=False)
                        nc.tensor.matmul(acc[:, s, m], xh, w_lo[:, r, kk], start=False, stop=False)
                        op = nc.tensor.matmul(acc[:, s, m], xl, w_hi[:, r, kk], start=False, stop=en)
                op.then_inc(used, 1)

            def transpose_chunk(source, ready, tp_read):
                pe.wait_ge(*ready)
                if tp_read is not None:
                    pe.wait_ge(*tp_read)
                for k in range(KW):
                    for m in range(M):
                        op = nc.tensor.transpose(tp[:, k, m * P:(m + 1) * P], source[:, m, k * P:(k + 1) * P], ident[:])
                op.then_inc(tp_full, 1)

            def no_tail(pos):
                pass

            def x_tail(xc, c, tp_read):
                def tail(pos):
                    if pos == EVAC:
                        transpose_chunk(x[:, :, cols(c)], (x_new, xc + 1), tp_read)
                return tail

            def ffn(ph, conv, end, xT, xdst_op, aT, tail, free, tp_read):
                at_ph = at[ph]
                g0, op, sr, xc, q0, cv = (at_ph[k] for k in ("g", "op", "src", "x", "gate", "conv"))

                def pair(g, free, before, operand=None, gate_step=None, i=None):
                    for pos in range(2 * GC):
                        s, k = pos // GC, pos % GC
                        if k == 0 and free[s] is not None:
                            pe.wait_ge(*free[s])
                        if operand is not None and s == 0 and k % 2 == 0:
                            pe.wait_ge(op_T, operand + k // 2 + 1)
                        products(g + pos, xT, KG * k, s, k == 0, k == GC - 1, i, 2 * GC)
                        before(pos)
                        if pos == GC + EVAC and conv:
                            transpose_chunk(evac[:], *gate_step)

                def pair_tail(sr, op, cv, i=None):
                    def tail(pos):
                        if pos == EVAC:
                            if conv:
                                transpose_chunk(evac[:], (src, n_at(sr, i, 2)), (conved, n_at(cv, i, 2)))
                            else:
                                transpose_chunk(evac[:], (src, n_at(sr, i, 1)), (op_T, n_at(op, i, 1)))
                    return tail

                per = 2 if conv else 1
                for p, n in enumerate(PARTS):
                    gate_step = ((src, sr + 1), tp_read)
                    pair(g0, free, tail, xdst_op if p == 0 else None, gate_step)
                    with pe.Fori(1, n) as i:
                        if conv:
                            busy = [(src, i * 2 + (sr - 1)), (src, i * 2 + sr)]
                            step = ((src, i * 2 + (sr + 1)), (op_T, i + op))
                            last = pair_tail(sr, None, cv - 1, i)
                        else:
                            busy = [(gated, i + q0), (src, i + sr)]
                            step = None
                            last = pair_tail(sr, op - 1, None, i)
                        pair(g0, busy, last, None, step, i)
                    g0, sr, op, q0, cv = g0 + 2 * GC * n, sr + per * n, op + n, q0 + n, cv + 2 * n
                    tail = pair_tail(sr, op - 1, cv - 1)
                    free = [(src, sr - 1) if conv else (gated, q0), (src, sr)]
                    tp_read = (op_T, op)
                    GP = KW * n // KG
                    for c in range(XC):
                        if free[c % 2] is not None:
                            pe.wait_ge(*free[c % 2])
                        for pos in range(GP):
                            if c == 0 and pos % 2 == 0:
                                pe.wait_ge(op_T, op - n + pos // 2 + 1)
                            products(g0, aT, KG * pos, c % 2, pos == 0, pos == GP - 1)
                            g0 += 1
                            tail(pos)
                        free[c % 2] = (x_new, xc + c + 1)
                        tail = no_tail
                        if p == len(PARTS) - 1 and end:
                            tail = x_tail(xc + c, c, tp_read)
                            op += 1
                            tp_read = (op_T, op)
                    xc += XC
                return tail, free, tp_read, op - XC

            MM, TR = nc.tensor.matmul, nc.tensor.transpose

            def small(out_col, bank, xT, hi_, lo_, n):
                for m in range(M):
                    o = side[:, bank, out_col + m * n:out_col + (m + 1) * n]
                    for k in range(KD):
                        xh, xl = (xT[h][:, k, m * P:(m + 1) * P] for h in (0, 1))
                        MM(o, xh, hi_[:, k], start=k == 0, stop=False)
                        MM(o, xh, lo_[:, k], start=False, stop=False)
                        op = MM(o, xl, hi_[:, k], start=False, stop=k == KD - 1)
                return op

            def s5_and_delta(xT, x_op, readers, e_y):
                yield
                pe.wait_ge(vec_in, 2 + TAPS)
                pe.wait_ge(par_done, 1)
                for i, t in enumerate((row["mag"], row["f"], row_fhi[:].bitcast(F32), row["flo"], row["cr"], row["ci"])):
                    op = TR(side[:, 0, i * ST:(i + 1) * ST], t if i == 2 else t[:], ident[0:ST, 0:ST])
                op.then_inc(par_T, 1)
                pe.wait_ge(ba_split, 2)
                pe.wait_ge(op_T, x_op + XC)
                small(0, 1, xT, ba_hi, ba_lo, 2 * H).then_inc(ba_mm, 1)
                yield
                pe.wait_ge(wide_b, 1)
                for q in range(4):
                    for b in range(2):
                        if q:
                            pe.wait_ge(wide_in, 2 * (q - 1) + b + 1)
                        else:
                            pe.wait_ge(*((par_in, 1), (ba_in, 1))[b])
                        for k in range(4):
                            c = 4 * b + k
                            t = (b_wide[:, q, SJ * c:SJ * (c + 1)].rearrange("p t g h -> p (t g h)") if q < 2 else
                                 c_wide[:, q - 2, c].rearrange("p g s -> p (g s)"))
                            op = TR(side[:, b, k * P:(k + 1) * P], t, ident[:])
                        op.then_inc(wide_T, 1)
                    yield
                pe.wait_ge(dn_gate, 1)
                pe.wait_ge(masks, mask_total)
                pe.wait_ge(wide_in, 8)
                for m in range(M):
                    MM(side[:, 0, m * H:(m + 1) * H], triu[:], dn_g[:, m], start=True, stop=True)
                MM(side[:, 0, M * H:(M + 1) * H], ones[:], dn_g[:, 0], start=True, stop=True).then_inc(dn_cum, 1)
                yield
                n = 7
                while n < S5_SLOT:
                    n += 1
                    yield
                pe.wait_ge(dn_gate, 2)

                def y(t):
                    c, j = t // SJ, t % SJ
                    pe.wait_ge(s5_x, t + 1)
                    if c and j == 0:
                        pe.wait_ge(s5_res, c)
                    for m in range(M):
                        for n in range(2):
                            op = MM(side[:, 1, m * P + j * SW:m * P + (j + 1) * SW], rot[:, t % 2, n, m * P:(m + 1) * P],
                                    s5_C[:, c, n, j * SW:(j + 1) * SW], start=n == 0, stop=n == 1)
                    op.then_inc(s5_y, 1)

                for t in range(ST):
                    c, j = t // SJ, t % SJ
                    if t % (SJ * KW) == 0:
                        pe.wait_ge(copied, c // KW + 1)
                    if t:
                        pe.wait_ge(s5_rot, t)
                    s = slice(j * SW, (j + 1) * SW)
                    for n in range(2):
                        op = MM(side[:, 0, n * T:(n + 1) * T], s5_B[s, c, n], uT[s, c], start=True, stop=True)
                    op.then_inc(s5_bu, 1)
                    yield
                    if t:
                        y(t - 1)
                    yield
                y(ST - 1)
                yield
                for c in range(NU):
                    transpose_chunk(ud[:, :, cols(c)], (s5_gelu, 1), readers[e_y + c - 1])
                    yield
                yield "s5"
                pe.wait_ge(s5_rot, ST)
                pe.wait_ge(s5_res, CT)
                for j in range(2 * H // KW):
                    pe.wait_ge(qk_sq, j + 1)
                    for k in range(KW):
                        for m in range(M):
                            o = m * 2 * H + KW * j + k
                            op = MM(side[:, 0, o:o + 1], sq4[:, k, m * P:(m + 1) * P], ones[:, 0:1], start=True, stop=True)
                    op.then_inc(qk_ss, 1)
                    yield
                yield
                pe.wait_ge(dn_rows, 1)
                pe.wait_ge(qkv_act, NQ)
                tok_of = lambda m: slice(m * P, (m + 1) * P)
                unit_of = lambda u: slice(u * P, (u + 1) * P)
                for b in range(H // 2):
                    unit = [(h, m) for h in (2 * b, 2 * b + 1) for m in range(M)]
                    if b:
                        pe.wait_ge(dn_newin, 2 * b)
                        pe.wait_ge(dn_ofull, b)
                    for w, name in enumerate(("colk", "colq")):
                        for u, (h, m) in enumerate(unit):
                            op = MM(side[:, w, unit_of(u)], dv[name][:, m, h:h + 1].to_broadcast([P, P]), ident[:],
                                    start=True, stop=True)
                    op.then_inc(dn_expo, 1)
                    yield
                    pe.wait_ge(dn_masked, b + 1)
                    for u, (h, m) in enumerate(unit):
                        TR(side[:, 0, unit_of(u)], qkvT[:, 2 * H + h, tok_of(m)], ident[:])
                    for e in range(2):
                        op = TR(side[:, 1, unit_of(e)], qkvT[:, H + 2 * b + e, tok_of(0)], ident[:])
                    op.then_inc(dn_vk, 1)
                    yield
                    pe.wait_ge(dn_vb, b + 1)
                    for w in range(2):
                        for u, (h, m) in enumerate(unit):
                            op = MM(side[:, w, unit_of(u)], qkvT[:, H + h, tok_of(m)], qkvT[:, (1 - w) * H + h, tok_of(m)],
                                    start=True, stop=True)
                    op.then_inc(dn_kk, 1)
                    yield
                    pe.wait_ge(dn_D, b + 1)
                    for u in range(4):
                        op = TR(side[:, 0, unit_of(u)], DT[:, u], ident[:])
                    op.then_inc(dn_DT, 1)
                    yield
                    for l in range(1, LEVELS):
                        pe.wait_ge(dn_lev, LEVELS * b + l)
                        for u in range(4):
                            op = MM(side[:, 0, unit_of(u)], LK[:, u], DD[:, u], start=True, stop=True)
                        op.then_inc(dn_P, 1)
                        yield
                        pe.wait_ge(dn_Pin, (LEVELS - 1) * b + l)
                        for u in range(4):
                            op = MM(side[:, 1, unit_of(u)], PP[:, u], DT[:, u], start=True, stop=True)
                        if l + 1 < LEVELS:
                            for u in range(4):
                                op = MM(side[:, 0, unit_of(u)], DT[:, u], PP[:, u], start=True, stop=True)
                        op.then_inc(dn_X, 1)
                        yield
                    pe.wait_ge(dn_lev, LEVELS * (b + 1))
                    for e in range(2):
                        op = MM(side[:, 0, unit_of(e)], DT[:, 2 * e], vb[:, 2 * e], start=True, stop=True)
                    op.then_inc(dn_new, 1)
                    yield
                    pe.wait_ge(dn_newin, 2 * b + 1)
                    for e in range(2):
                        MM(side[:, 0, unit_of(e)], ktail[:, e], vnew[:, e], start=True, stop=True)
                    for e in range(2):
                        op = MM(side[:, 1, unit_of(e)], AT[:, 2 * e], vnew[:, e], start=True, stop=True)
                    op.then_inc(dn_St, 1)
                    yield
                    pe.wait_ge(dn_Sin, b + 1)
                    pe.wait_ge(dn_o0, b + 1)
                    for w in range(2):
                        for e in range(2):
                            op = MM(side[:, 0, unit_of(2 * w + e)], qkvT[:, (1 - w) * H + 2 * b + e, tok_of(1)], dn_S[:, e],
                                    start=True, stop=True)
                    op.then_inc(dn_kS, 1)
                    yield
                    pe.wait_ge(dn_rhs, b + 1)
                    for e in range(2):
                        op = MM(side[:, 0, unit_of(e)], DT[:, 2 * e + 1], rhs1[:, e], start=True, stop=True)
                    op.then_inc(dn_new, 1)
                    yield
                    pe.wait_ge(dn_newin, 2 * b + 2)
                    for e in range(2):
                        op = MM(side[:, 1, unit_of(e)], AT[:, 2 * e + 1], vnew[:, 2 + e], start=True, stop=True)
                    op.then_inc(dn_out, 1)
                    yield
                yield
                for c in range(NZ):
                    transpose_chunk(zs[:, :, cols(c)], (dn_y, H // 4 * (c + 1)), readers[e_y + NU + c - 1])
                    yield

            def mix1(end, xT, x_op, yT, tail, free, tp_read):
                g, o0, xc = (at["mix1"][k] for k in ("g", "op", "x"))
                readers = ([(copied, c + 1) for c in range(NU)] + [(dn_conved, q + 1) for q in range(NQ)]
                           + [(op_T, o0 + i + 1) for i in range(NU + NZ + 2 * XC)])
                e_y = NU + NQ
                e_m = e_y + NU + NZ
                side_work = s5_and_delta(xT, x_op, readers, e_y)
                seen = set()

                def leave(c, kind):
                    def tail(pos):
                        if pos == EVAC and kind in ("u", "qkv"):
                            transpose_chunk(evac[:], (left, c + 1), readers[c - 1] if c else tp_read)
                    return tail

                for c, (kind, _) in enumerate(W_IN):
                    for pos in range(GC):
                        if pos == 0 and (c >= 2 or free[c % 2] is not None):
                            pe.wait_ge(*((left, c - 1) if c >= 2 else free[c % 2]))
                        if c == 0 and pos % 2 == 0:
                            pe.wait_ge(op_T, x_op + pos // 2 + 1)
                        products(g, xT, KG * pos, c % 2, pos == 0, pos == GC - 1)
                        tail(pos)
                        seen.add(next(side_work, "end"))
                        g += 1
                    tail = leave(c, kind)
                while "s5" not in seen and "end" not in seen:
                    seen.add(next(side_work, "end"))
                C = len(W_IN)
                older = no_tail

                def both(j):
                    def tail(pos):
                        if pos == EVAC:
                            transpose_chunk(gs[:, :, cols(j)], (merged, j + 1), readers[e_m + j - 1])
                    return tail

                for c in range(3 * XC):
                    j = c // 2 if c < 2 * XC else c - 2 * XC
                    if c == 2 * XC:
                        for _ in side_work:
                            pass
                    if c < 2 * XC:
                        busy = ((glu_a, glu_sig)[c % 2], j) if j else (left, C - 1 + c)
                        k0, op0 = 0, o0
                    else:
                        busy = (merged, j - 1) if j >= 2 else ((glu_a, glu_sig)[j], XC)
                        k0, op0 = KD // 2, o0 + NU
                    pe.wait_ge(*busy)
                    for pos in range(GH):
                        if c in (0, 2 * XC) and pos % 2 == 0:
                            pe.wait_ge(op_T, op0 + pos // 2 + 1)
                        products(g, yT, k0 + KG * pos, c % 2, pos == 0, pos == GH - 1)
                        tail(pos)
                        if c < 2 * XC:
                            next(side_work, None)
                        g += 1
                    tail = both(j) if c >= 2 * XC else no_tail
                for c in range(XC):
                    pe.wait_ge(*((merged, XC - 1 + c) if c < 2 else (x_new, xc + c - 1)))
                    for pos in range(GC):
                        if c == 0 and pos % 2 == 0:
                            pe.wait_ge(op_T, o0 + NU + NZ + pos // 2 + 1)
                        products(g, xT, KG * pos, c % 2, pos == 0, pos == GC - 1)
                        tail(pos)
                        g += 1
                    tail = x_tail(xc + c, c, readers[e_m + XC + c - 1])
                return tail, [(x_new, xc + XC - 1), (x_new, xc + XC)], readers[-1], o0 + NU + NZ + XC

            def attention(xT, x_op):
                for _ in range(ATT_WARM):
                    yield
                yield
                pe.wait_ge(lr_split, 2)
                pe.wait_ge(op_T, x_op + XC)
                small(0, 0, xT, lr_hi, lr_lo, GR).then_inc(lr_mm, 1)
                yield
                pe.wait_ge(lr_in, 1)
                for m in range(M):
                    op = TR(side[0:GR, 0, m * P:(m + 1) * P], lr2[:, m], ident[:])
                op.then_inc(lr_T, 1)
                yield
                pe.wait_ge(lr_Tin, 1)
                pe.wait_ge(wal_full, 16)
                for h in range(GHD):
                    op = MM(side[:, h // 2, (h % 2) * T:(h % 2 + 1) * T], wal[:, h * P:(h + 1) * P], lrT[:], start=True, stop=True)
                op.then_inc(al_mm, 1)
                yield
                n = ATT_WARM + 4
                while n < ATT_SLOT:
                    n += 1
                    yield
                yield
                yield
                pe.wait_ge(qk_dec, 4)
                for m in range(M):
                    for h in range(GHD):
                        op = TR(side[:, m, h * P:(h + 1) * P], kt[:, h, m * P:(m + 1) * P], ident[:])
                op.then_inc(gk_T, 1)
                yield
                pe.wait_ge(gk_in, 1)
                for m in range(M):
                    for h in range(GHD):
                        op = MM(side[:, m, h * P:(h + 1) * P], ki[:, h, m * P:(m + 1) * P], qd[:, h, m * P:(m + 1) * P],
                                start=True, stop=True)
                op.then_inc(g_sc, 1)
                yield
                pe.wait_ge(left, left0 + VC + 2 + VC)
                out_of = lambda h: (h // 2, slice((h % 2) * GV, (h % 2 + 1) * GV))
                for n in range(LN - 1):
                    pe.wait_ge(*((g_S, n) if n else (g_scin, 2)))
                    t = slice(n % 2 * LC, (n % 2 + 1) * LC)
                    for h in range(GHD):
                        b, w = out_of(h)
                        op = MM(side[:, b, w], ktT[t, n // 2, h], vv[t, n // 2, h * GV:(h + 1) * GV], start=True, stop=True)
                    op.then_inc(g_kv, 1)
                    yield
                pe.wait_ge(g_S, LN - 1)
                for m in range(M):
                    if m:
                        pe.wait_ge(g_oin, m)
                    for h in range(GHD):
                        b, w = out_of(h)
                        v = vv[:, m, h * GV:(h + 1) * GV]
                        if m:
                            MM(side[:, b, w], sc[:, m, h], v, start=True, stop=False)
                        for e in range(P // LC):
                            n = P // LC * m + e
                            rows = slice(e * LC, (e + 1) * LC)
                            if not m:
                                MM(side[rows, b, w], sc[:, m, h, rows], v, start=True, stop=n == 0)
                            if n:
                                op = MM(side[rows, b, w], qd[:, h, n * LC:(n + 1) * LC], Sg[:, n - 1, h], start=False, stop=True)
                    op.then_inc(g_o, 1)
                    yield

            def mix2(end, xT, x_op, yT, tail, free, tp_read):
                g, o0, xc = (at["mix2"][k] for k in ("g", "op", "x"))
                order = ["u0", "p0", "u1", "p1", "q0", "k0", "y0", "y1"]
                reader = dict(u0=(copied, copied0 + 1), p0=(op_T, o0 + 1), u1=(copied, copied0 + 2), p1=(op_T, o0 + 2),
                              q0=(copied, copied0 + 3), k0=(copied, copied0 + 4), y0=(op_T, o0 + 3), y1=(op_T, o0 + 4))
                before = lambda e: reader[order[order.index(e) - 1]] if e != order[0] else tp_read
                side_work = attention(xT, x_op)

                def leave(c, kind, n):
                    def tail(pos):
                        if pos == EVAC and kind in ("u", "q", "k"):
                            transpose_chunk(evac[:], (left, left0 + c + 1), before(f"{kind}{n}"))
                        if pos == GC and kind == "u":
                            pe.wait_ge(pooled, n + 1)
                            pe.wait_ge(wp_full, 16 * PG)
                            pe.wait_ge(*before(f"p{n}"))
                            for e in range(2):
                                t = (pool_b, pool_a)[e]
                                for d in range(PD // P):
                                    for k in range(PD // P):
                                        op = MM(tp[:, 2 * e + d], wp[n][:, e, k, d * P:(d + 1) * P], t[:, KW * n + 2 * e + k],
                                                start=k == 0, stop=k == PD // P - 1)
                            op.then_inc(tp_full, 1)
                        if pos == EVAC + 1 and kind == "g":
                            transpose_chunk(vv[:, :, cols(n)], (g_y, n + 1), before(f"y{n}"))
                    return tail

                older, n = no_tail, {}
                for c, (kind, _) in enumerate(W_IN2):
                    for pos in range(GC):
                        if pos == 0 and (c >= 2 or free[c % 2] is not None):
                            pe.wait_ge(*((left, left0 + c - 1) if c >= 2 else free[c % 2]))
                        if c == 0 and pos % 2 == 0:
                            pe.wait_ge(op_T, x_op + pos // 2 + 1)
                        products(g, xT, KG * pos, c % 2, pos == 0, pos == GC - 1)
                        tail(pos)
                        older(pos + GC)
                        next(side_work, None)
                        g += 1
                    older = tail if c else no_tail
                    tail = leave(c, kind, n.get(kind, 0))
                    n[kind] = n.get(kind, 0) + 1
                for _ in side_work:
                    pass
                C = len(W_IN2)
                for c in range(XC):
                    pe.wait_ge(*((left, left0 + C - 1 + c) if c < 2 else (x_new, xc + c - 1)))
                    for pos in range(GC):
                        if c == 0 and pos % 2 == 0:
                            pe.wait_ge(op_T, o0 + pos // 2 + 1)
                        products(g, yT, KG * pos, c % 2, pos == 0, pos == GC - 1)
                        tail(pos)
                        g += 1
                    tail = x_tail(xc + c, c, (op_T, o0 + 2 * VC + c))
                return tail, [(x_new, xc + XC - 1), (x_new, xc + XC)], (op_T, o0 + 2 * VC + XC), o0 + 2 * VC

            pe.wait_ge(consts, 2)
            pe.wait_ge(vec_full, 16 * len(VECS))
            nc.tensor.transpose(side[:, 0, 0:VEC_ROWS], vecs[:], ident[0:VEC_ROWS, 0:VEC_ROWS]).then_inc(vec_T, 1)
            pe.wait_ge(taps_full, 16)
            for t in range(TAPS):
                nc.tensor.transpose(side[:, 0, P * (t + 1):P * (t + 1) + FT], tap_rows[:, t], ident[0:FT, 0:FT]).then_inc(vec_T, 1)
            pe.wait_ge(dtap_full, 16)
            nc.tensor.transpose(side[:, 1, 0:DTAPS * QT], dtap_rows[:], ident[0:DTAPS * QT, 0:DTAPS * QT]).then_inc(vec_T, 1)
            for m in range(M):
                pe.wait_ge(x_full[m], 16)
            for c in range(XC):
                transpose_chunk(x[:, :, cols(c)], (x_full[M - 1], 16), (op_T, c) if c else None)
            tail, free, tp_read, operand = no_tail, [None, None], (op_T, XC), 0
            for ph in phases[1:]:
                if ph in ("ffn1", "ffn2", "ffn3"):
                    tail, free, tp_read, operand = ffn(ph, ph == "ffn1", ph in NEXT, B, operand, A, tail, free, tp_read)
                elif ph == "mix1":
                    tail, free, tp_read, operand = mix1(True, A, operand, B, tail, free, tp_read)
                elif ph == "mix2":
                    tail, free, tp_read, operand = mix2(True, B, operand, A, tail, free, tp_read)


_INS = ["x", "mix_norm_w", "w_in", "s5_log_dt", "s5_a_re", "s5_a_im", "s5_b_re", "s5_b_im", "s5_c_re", "s5_c_im", "s5_d",
        "s5_glu_w", "dn_conv_w", "dn_a_log", "dn_dt_bias", "dn_norm_w", "dn_proj_w", "w_out", "ffn_norm_w", "ffn_up",
        "ffn_conv_w", "ffn_down", "final_norm_w", "ffn1_norm_2", "ffn1_w_in_2", "ffn1_w_out_2", "mix_norm_2", "w_in_mix_2",
        "w_pool_2", "pool_scale_2", "w_alpha_2", "b_alpha_2", "gla_norm_2", "w_out_mix_2", "ffn2_norm_2", "ffn2_w_in_2",
        "ffn2_w_out_2", "final_norm_2"]


def kernel(**inputs):
    import numpy as _np
    import concourse.bacc as _bacc
    from concourse import mybir as _mybir
    from concourse.bass_utils import run_bass_kernel_spmd as _run

    nc = _bacc.Bacc("TRN2", target_bir_lowering=False, num_devices=1)
    arrays, aps = {}, {}
    for name in _INS:
        v = _np.ascontiguousarray(inputs[name])
        arrays[f"in_{name}_dram"] = v
        aps[name] = nc.dram_tensor(f"in_{name}_dram", v.shape, _mybir.dt.from_np(v.dtype), kind="ExternalInput").ap()
    out = nc.dram_tensor("out_0_dram", inputs["x"].shape, _mybir.dt.float32, kind="ExternalOutput").ap()
    two_block_kernel(nc, aps, out)
    return _run(nc, [arrays], core_ids=[0]).results[0]["out_0_dram"]
```

```python
import math
import concourse.bass as bass
from concourse import mybir
from contextlib import ExitStack


def two_block_kernel(nc, a, out, phases=None):
    F32, F32R, BF16, I32 = mybir.dt.float32, mybir.dt.float32r, mybir.dt.bfloat16, mybir.dt.int32
    ALU, ACT, AX = mybir.AluOpType, mybir.ActivationFunctionType, mybir.AxisListType

    P = 128
    T, D = a["x"].shape[1], a["x"].shape[2]
    M = T // P
    KD = D // P
    NW = 512
    KW = NW // P
    XC = D // NW
    KG = 2
    RING = 4
    FF = a["ffn_down"].shape[1]
    FT = 2 * FF // P
    PAIRS = FF // NW
    PARTS = [4, 4, 3]
    GC = KD // KG
    GH = GC // 2
    CU = a["s5_d"].shape[1]
    CT = CU // P
    H = a["dn_a_log"].shape[1]
    QT = a["dn_conv_w"].shape[2] // P
    DTAPS = a["dn_conv_w"].shape[1]
    SG, SP_, SH = a["s5_b_re"].shape[1:]
    ST = SG * SP_ // P
    SJ = ST // CT
    SW = P // SJ
    OFF_QKV, OFF_Z = CU, CU + QT * P
    OFF_BA = OFF_Z + H * P
    OFF_GS = OFF_BA + 2 * H
    OFF_GD = OFF_GS + D
    LEVELS = P.bit_length() - 1
    W_IN = ([("u", c * NW) for c in range(CU // NW)] + [("qkv", OFF_QKV + c * NW) for c in range(QT // KW)]
            + [("z", OFF_Z + c * NW) for c in range(H * P // NW)] + [("gs", OFF_GS + c * NW) for c in range(XC)]
            + [("gd", OFF_GD + c * NW) for c in range(XC)])
    NU, NQ, NZ = CU // NW, QT // KW, H * P // NW
    PG, PD = a["w_pool_2"].shape[1:3]
    GR, GK = a["w_alpha_2"].shape[1:]
    GHD = GK // P
    GV = a["gla_norm_2"].shape[1]
    LC = 64
    LN = T // LC
    OFF2 = dict(u=0, q=PG * PD, k=PG * PD + GK, v=PG * PD + 2 * GK, g=PG * PD + 2 * GK + GHD * GV,
                lr=PG * PD + 2 * GK + 2 * GHD * GV)
    W_IN2 = ([("u", c * NW) for c in range(PG * PD // NW)] + [("q", OFF2["q"]), ("k", OFF2["k"])]
             + [("v", OFF2["v"] + c * NW) for c in range(GHD * GV // NW)]
             + [("g", OFF2["g"] + c * NW) for c in range(GHD * GV // NW)])
    VC = GHD * GV // NW
    assert sum(PARTS) == PAIRS
    EPS = 1e-6
    EVAC, FLIP, SPLIT = 3, 2, 5
    LEAD = 2
    MAGIC = 1.5 * 2.0 ** 23
    TURN = 6.283185
    TURN_1, TURN_2, TURN_3 = 6.28125, 0.0019350051879882812, 3.0199159819e-07
    IN_TURNS = 0.15915494309189535
    GATE_NORM = 16.0
    Q_LOG = -0.5 * math.log(a["dn_conv_w"].shape[2] // 3 // a["dn_a_log"].shape[1])
    ATT_WARM = 6
    S5_SLOT = 16
    S5_REST = 1
    DN_SLOT = 70
    ATT_SLOT = 44

    FFN_GROUPS = sum(3 * GC * n for n in PARTS)
    phases = phases or ["init", "mix1", "ffn1", "ffn2", "mix2", "ffn3"]
    NEXT = dict(zip(phases, phases[1:]))
    ends = lambda ph: XC if ph in NEXT else 0
    MIX1_GROUPS = GC * len(W_IN) + GH * 3 * XC + GC * XC
    MIX2_GROUPS = GC * len(W_IN2) + GC * XC
    size = {
        "mix1": dict(g=MIX1_GROUPS, ev=NU + NQ + NZ + XC + ends("mix1"), op=NU + NZ + XC + ends("mix1"), x=XC),
        "mix2": dict(g=MIX2_GROUPS, ev=2 + 3 * VC + ends("mix2"), op=2 * VC + ends("mix2"), x=XC),
        "init": dict(ev=XC, op=XC),
        "ffn1": dict(g=FFN_GROUPS, ev=2 * PAIRS + ends("ffn1"), op=PAIRS + ends("ffn1"), src=2 * PAIRS,
                     x=len(PARTS) * XC, gate=PAIRS, conv=2 * PAIRS, prod=PAIRS),
        "ffn2": dict(g=FFN_GROUPS, ev=PAIRS + ends("ffn2"), op=PAIRS + ends("ffn2"), src=PAIRS,
                     x=len(PARTS) * XC, gate=PAIRS),
        "ffn3": dict(g=FFN_GROUPS, ev=PAIRS + ends("ffn3"), op=PAIRS + ends("ffn3"), src=PAIRS,
                     x=len(PARTS) * XC, gate=PAIRS),
    }
    COUNTS = ["g", "ev", "op", "src", "x", "gate", "conv", "prod"]
    at, total = {}, dict.fromkeys(COUNTS, 0)
    for ph in phases:
        at[ph] = dict(total)
        total = {c: total[c] + size[ph].get(c, 0) for c in COUNTS}

    norm_order = []
    for ph in phases:
        if ph == "ffn1" and ph in NEXT:
            norm_order.append("block end")
        norm_order.append(NEXT.get(ph, "result"))
    NORM = {n: k for k, n in enumerate(norm_order)}
    NORMS = len(norm_order)
    NORM_W = {"mix1": "mix_norm_w", "ffn1": "ffn_norm_w", "ffn2": "ffn1_norm_2", "mix2": "mix_norm_2",
              "ffn3": "ffn2_norm_2"}
    two_norms = "ffn1" in NEXT

    def wview(w):
        return w.rearrange("o (k p) n -> p (o k) n", p=P)

    def n_at(n, i, per):
        return n if i is None else i * per + n

    def cols(c):
        return slice(c * NW, (c + 1) * NW)

    ctx = ExitStack()
    with ctx:
        def sem(name):
            return ctx.enter_context(nc.semaphore(name))

        def over(*spans):
            spans = [list(span) for span in spans]

            def put(name, shape, dt=F32):
                n = 4 if dt in (F32, F32R, I32) else 2
                for d in shape[1:]:
                    n *= d
                n = -(-n // 32) * 32
                for span in spans:
                    if span[1] >= n:
                        span[0], span[1] = span[0] + n, span[1] - n
                        return nc.alloc_sbuf_tensor_at(name, shape, dt, offset=span[0] - n)
                raise ValueError(f"no room for {name}")
            return put

        first = -(-nc.sbuf_base // 32) * 32
        sb = over((first, nc.sbuf_usable_end - first))

        def spot(name, shape, dt=F32):
            t = sb(name, shape, dt)
            return t, t.manual_sbuf_range[0]

        stage = sb("stage", [P, RING, KG, NW])
        w_hi = sb("w_hi", [P, RING, KG, NW], F32R)
        w_lo = sb("w_lo", [P, RING, KG, NW], F32R)
        a_hi, A_HI = spot("a_hi", [P, KD, T], F32R)
        a_lo, A_LO = spot("a_lo", [P, KD, T], F32R)
        b_hi, B_HI = spot("b_hi", [P, KD, T], F32R)
        b_lo, B_LO = spot("b_lo", [P, KD, T], F32R)
        A, B = (a_hi, a_lo), (b_hi, b_lo)
        x, X = spot("x", [P, M, D])
        XB = 4 * M * D
        HB = 4 * KD * T // 2
        evac = sb("evac", [P, M, NW])
        ident = sb("ident", [P, P])
        half = sb("half", [P, 8])
        ssq = sb("ssq", [P, M, XC])
        sumsq = sb("sumsq", [P, NORMS, M])
        mean = sb("mean", [P, NORMS, M])
        rstd = sb("rstd", [P, NORMS, M])
        row_scale = sb("row_scale", [P, M])
        junk, JUNK = spot("junk", [P, M, NW], BF16)
        VECS = ["mix_norm_w", "ffn_norm_w", "final_norm_w", "ffn1_norm_2", "mix_norm_2", "ffn2_norm_2",
                "pool_scale_2", "b_alpha_2", "gla_norm_2", "dn_norm_w"]
        vec_at, VEC_ROWS = {}, 0
        for name in VECS:
            vec_at[name] = VEC_ROWS
            VEC_ROWS += a[name].shape[-1] // P
        vecT = sb("vecT", [P, VEC_ROWS])
        blk_w = sb("blk_w", [P, KD])
        TAPS = a["ffn_conv_w"].shape[1]
        taps = sb("taps", [P, TAPS, FT])
        dtaps = sb("dtaps", [P, DTAPS, QT])
        s5p = sb("s5p", [P, 6, ST])
        expo_mask = sb("expo_mask", [P, 2, P])
        lev_mask = sb("lev_mask", [P, LEVELS, P], BF16)
        triu = sb("triu", [P, P])
        ones = sb("ones", [P, P])
        score_mask = sb("score_mask", [P, P], I32)
        dv = {n: sb("dn_" + n, [P, M, H]) for n in (
            "cum", "beta", "rowk", "wk", "nwk", "wq", "colk", "colq", "lnb")}
        dn_tail = sb("dn_tail_scale", [P, H])
        dn_ss = sb("dn_ss", [P, M, 2 * H])
        dn_ssq = sb("dn_ssq", [P, 4])
        dn_mean = sb("dn_mean", [P, 4])
        dn_rstd = sb("dn_rstd", [P, 4])
        g_ssq = sb("gla_ssq", [P, M, GHD])
        g_mean = sb("gla_mean", [P, M, GHD])
        g_rstd = sb("gla_rstd", [P, M, GHD])

        ARENA = 64 * 1024
        AR = spot("arena", [P, ARENA // 4])[1]
        put = over((AR, ARENA))
        sgate = put("sgate", [P, M, NW])
        conv_g = put("conv_g", [P, KW, T])
        conv_v = put("conv_v", [P, KW, T])
        fnorm = put("fnorm", [P, D])
        put = over((AR, ARENA))
        uT, UT = put("uT", [P, CT, T]), AR
        qkvT = put("qkvT", [P, QT, T])
        QK = UT + 4 * CT * T
        zs = put("zs", [P, M, H * P])
        ZS = QK + 4 * QT * T
        gs = put("gs", [P, M, D])
        ud = put("ud", [P, M, CU])
        UD = ZS + 4 * M * H * P + 4 * M * D
        put = over((X, XB))
        s5_B = put("s5_B", [P, CT, 2, P])
        s5_C = put("s5_C", [P, CT, 2, P])
        gd = over((X, XB))("gd", [P, M, D])
        put = over((ZS, UD - ZS))
        b_wide = put("b_wide", [P, 2, ST, P // SP_, SH])
        c_wide = put("c_wide", [P, 2, CT, P // SP_, SP_])
        b_nat = put("b_nat", [P, 2, ST, SH])
        c_nat = put("c_nat", [P, 2, CT, SP_])
        put = over((QK, ZS - QK))
        d_row = put("d_row", [P, CU])
        b_t = put("b_t", [P, 2, ST, SH])
        par = put("par", [P, P // SP_])
        ba_w = put("ba_w", [P, KD, 2 * H])
        ba_hi = put("ba_hi", [P, KD, 2 * H], F32R)
        ba_lo = put("ba_lo", [P, KD, 2 * H], F32R)
        ba = put("ba", [P, M, 2 * H])
        ba_abs = put("ba_abs", [P, M, 2 * H])
        ba_ln = put("ba_ln", [P, M, 2 * H])
        dt_row = put("dt_row", [P, H])
        alog_row = put("alog_row", [P, H])
        ea_row = put("ea_row", [P, H])
        dn_g = put("dn_g", [P, M, H])
        log_dt = put("log_dt", [ST, P // SP_])
        s5_dt = put("s5_dt", [ST, P // SP_])
        vecs = put("vecs", [VEC_ROWS, P])
        tap_rows = put("tap_rows", [FT, TAPS, P])
        dtap_rows = put("dtap_rows", [DTAPS * QT, P])
        row = {n: put("row_" + n, [ST, P]) for n in (
            "lr", "li", "lrdt", "th", "k", "mag", "f", "sn", "sh", "cs", "ar", "ai", "den", "t1", "t2", "cr", "ci",
            "flo")}
        row_fhi = put("row_fhi", [ST, P], F32R)
        tok_i = over((B_HI + HB, HB))("tok_i", [P, T], I32)
        put = over((B_HI, HB), (B_LO, HB))
        tok = put("tok", [P, T])
        angle = put("angle", [P, 2, T])
        sn = put("sn", [P, 2, T])
        rot = put("rot", [P, 2, T])
        p_c = put("p_c", [P, 2, T])
        p_s = put("p_s", [P, 2, T])
        state = put("state", [P, 2, 2, T])
        put = over((B_HI + HB, HB), (B_LO + HB, HB))
        dec = put("dec", [P, 2, 4, P])
        LT = put("LT", [P, 4, P])
        AT, AT_AT = put("AT", [P, 4, P]), B_HI + HB + 4 * 12 * P
        DT = put("DT", [P, 4, P])
        DD = put("DD", [P, 4, P])
        LK = put("LK", [P, 4, P])
        ktail = put("ktail", [P, 2, P])
        dn_S = put("dn_S", [P, 2, P])
        sq4 = over((B_HI + HB, HB))("sq4", [P, KW, T])
        PP = over((B_HI + HB, HB))("PP", [P, 4, P])
        dn_o = over((B_HI + HB + 16 * P, HB))("dn_o", [P, 4, P])
        dn_junk = over((AT_AT, 8 * P))("dn_junk", [P, P], BF16)
        vnew = over((B_LO + HB + 16 * P, HB))("vnew", [P, 4, P])
        put = over((B_LO + HB + 32 * P, 16 * P))
        rhs1 = put("rhs1", [P, 2, P])
        qS = put("qS", [P, 2, P])
        vb = over((JUNK, 16 * P))("vb", [P, 4, P])
        put = over((AR, ARENA))
        u2T = put("u2T", [P, 8, T])
        vv = put("vv", [P, M, GHD * GV])
        sg = put("sg", [P, M, GHD * GV])
        qd = put("qd", [P, GHD, T])
        ki = put("ki", [P, GHD, T])
        kt = put("kt", [P, GHD, T])
        la = put("la", [P, GHD, T])
        lt = put("lt", [P, GHD, T])
        ktT = put("ktT", [P, M, GHD, P])
        sc = put("sc", [P, M, GHD, P])
        SA = AR + 4 * (2 * M * GHD * GV + 8 * T + 5 * GHD * T + 2 * M * GHD * P)
        SBYTES = 4 * (LN - 1) * GHD * GV
        Sg = put("Sg", [P, LN - 1, GHD, GV])
        put = over((SA, SBYTES))
        lr2 = put("lr2", [P, M, GR])
        lrT = put("lrT", [GR, T])
        wal = put("wal", [GR, GK])
        put = over((A_HI + HB, HB), (A_LO + HB, HB))
        lr_w = put("lr_w", [P, KD, GR])
        lr_hi = put("lr_hi", [P, KD, GR], F32R)
        lr_lo = put("lr_lo", [P, KD, GR], F32R)
        put = over((A_HI + HB, HB), (A_LO + HB, HB))
        pool_a = put("pool_a", [P, 8, T])
        pool_b = put("pool_b", [P, 8, T])
        wp = [over((A_HI + HB // 2, HB // 2))("wp0", [P, 2, 2, PD]), over((A_LO + HB // 2, HB // 2))("wp1", [P, 2, 2, PD])]
        rcnt = sb("rcnt", [P, PG, 16])
        gdec = sb("gdec", [P, GHD, LN])

        acc = ctx.enter_context(nc.psum_tensor("acc", [P, 2, M, NW], F32))
        tp = ctx.enter_context(nc.psum_tensor("tp", [P, KW, T], F32))
        side = ctx.enter_context(nc.psum_tensor("side", [P, 2, NW], F32))
        side_T = side[:].rearrange("p b (k t) -> p (b k) t", t=T)

        def dnb(b):
            return tp[:, 2 * b:2 * b + 2].rearrange("p k t -> p (k t)")

        stage_full = [sem(f"stage_full{s}") for s in range(RING)]
        hi_done = sem("hi_done")
        lo_done = sem("lo_done")
        used = sem("used")
        x_full = [sem(f"x_full{c}") for c in range(XC)]
        vec_full = sem("vec_full")
        taps_full = sem("taps_full")
        fnorm_full = sem("fnorm_full")
        consts = sem("consts")
        vec_T = sem("vec_T")
        vec_in = sem("vec_in")
        src = sem("src")
        tp_full = sem("tp_full")
        hi_T = sem("hi_T")
        op_T = sem("op_T")
        gated = sem("gated")
        tap_step = sem("tap_step")
        conved = sem("conved")
        prod = sem("prod")
        x_new = sem("x_new")
        sq = sem("sq")
        sums = sem("sums")
        ms = sem("ms")
        rs = sem("rs")
        blk_ready = sem("blk_ready")
        scaled = sem("scaled")
        rescaled = sem("rescaled")
        out_done = sem("out_done")
        masks = sem("masks")
        left = sem("left")
        copied = sem("copied")
        step_d = sem("step_d")
        step_a = sem("step_a")
        x_again = sem("x_again")
        dtap_full = sem("dtap_full")
        s5_full = sem("s5_full")
        s5_bc_full = sem("s5_bc_full")
        d_full = sem("d_full")
        ba_full = sem("ba_full")
        dnp_full = sem("dnp_full")
        skip_done = sem("skip_done")
        par_dt = sem("par_dt")
        par_th = sem("par_th")
        par_trig = sem("par_trig")
        par_done = sem("par_done")
        par_T = sem("par_T")
        par_in = sem("par_in")
        wide_b = sem("wide_b")
        wide_T = sem("wide_T")
        wide_in = sem("wide_in")
        tok_done = sem("tok_done")
        s5_turn = sem("s5_turn")
        s5_part_turn = sem("s5_part_turn")
        s5_in = sem("s5_in")
        s5_out = sem("s5_out")
        s5_z = sem("s5_z")
        s5_frac = sem("s5_frac")
        s5_sin = sem("s5_sin")
        s5_bu = sem("s5_bu")
        s5_rot = sem("s5_rot")
        s5_x = sem("s5_x")
        s5_y = sem("s5_y")
        s5_res = sem("s5_res")
        s5_gelu = sem("s5_gelu")
        s5_T = sem("s5_T")
        ba_split = sem("ba_split")
        ba_mm = sem("ba_mm")
        ba_in = sem("ba_in")
        ba_neg = sem("ba_neg")
        ba_log = sem("ba_log")
        dn_gate = sem("dn_gate")
        dn_cum = sem("dn_cum")
        dn_tap = sem("dn_tap")
        dn_conved = sem("dn_conved")
        qkv_act = sem("qkv_act")
        qk_sq = sem("qk_sq")
        qk_ss = sem("qk_ss")
        dn_ssin = sem("dn_ssin")
        dn_lns = sem("dn_lns")
        dn_rows = sem("dn_rows")
        dn_fac = sem("dn_fac")
        dn_nwk = sem("dn_nwk")
        dn_expo = sem("dn_expo")
        dn_masked = sem("dn_masked")
        dn_decay = sem("dn_decay")
        dn_kk = sem("dn_kk")
        dn_LA = sem("dn_LA")
        dn_D = sem("dn_D")
        dn_DT = sem("dn_DT")
        dn_lev = sem("dn_lev")
        dn_P = sem("dn_P")
        dn_Pin = sem("dn_Pin")
        dn_X = sem("dn_X")
        dn_vk = sem("dn_vk")
        dn_vb = sem("dn_vb")
        dn_new = sem("dn_new")
        dn_newin = sem("dn_newin")
        dn_St = sem("dn_St")
        dn_Sin = sem("dn_Sin")
        dn_o0 = sem("dn_o0")
        dn_kS = sem("dn_kS")
        dn_rhs = sem("dn_rhs")
        dn_out = sem("dn_out")
        dn_ofull = sem("dn_ofull")
        dn_sq = sem("dn_sq")
        dn_ms = sem("dn_ms")
        dn_rs = sem("dn_rs")
        dn_y = sem("dn_y")
        gate_sig = sem("gate_sig")
        glu_sig = sem("glu_sig")
        glu_a = sem("glu_a")
        s5_part = sem("s5_part")
        merged = sem("merged")
        lr_full = sem("lr_full")
        wal_full = sem("wal_full")
        wp_full = sem("wp_full")
        lr_split = sem("lr_split")
        lr_mm = sem("lr_mm")
        lr_in = sem("lr_in")
        lr_T = sem("lr_T")
        lr_Tin = sem("lr_Tin")
        al_mm = sem("al_mm")
        al_in = sem("al_in")
        al_abs = sem("al_abs")
        al_exp = sem("al_exp")
        al_one = sem("al_one")
        al_ln = sem("al_ln")
        al_cum = sem("al_cum")
        al_dec = sem("al_dec")
        qk_dec = sem("qk_dec")
        gk_T = sem("gk_T")
        gk_in = sem("gk_in")
        g_sc = sem("g_sc")
        g_scin = sem("g_scin")
        g_kv = sem("g_kv")
        g_S = sem("g_S")
        g_o = sem("g_o")
        g_oin = sem("g_oin")
        g_ms = sem("g_ms")
        g_rs = sem("g_rs")
        g_y = sem("g_y")
        pooled = sem("pooled")

        block = ctx.enter_context(nc.Block())

        def weight_of(ph):
            if ph == "ffn2" and two_norms:
                return blk_w[:, :]
            o = vec_at[NORM_W[ph]]
            return vecT[:, o:o + KD]

        first_x = A if phases[1] == "mix1" else B
        left0 = len(W_IN) if "mix1" in phases else 0
        copied0 = NU if "mix1" in phases else 0
        sq_count = {}
        for k, n in enumerate(norm_order):
            sq_count[n] = M * XC * (k + 1)

        @block.sync
        def _(sp):
            def load(g, w, k0, col, i=None, per=0):
                s = g % RING
                if g >= RING or i is not None:
                    sp.wait_ge(lo_done, n_at(g - RING + 1, i, per))
                sp.dma_start(stage[:, s], wview(w)[:, k0:k0 + KG, bass.ds(col, NW)]).then_inc(stage_full[s], 16)

            def ffn(ph, up, down):
                g0, pair0 = at[ph]["g"], 0
                for n in PARTS:
                    for pos in range(2 * GC):
                        load(g0 + pos, up, KG * (pos % GC), pair0 * NW + FF * (pos // GC))
                    if not pair0 and (ph == "ffn1" or ph not in NEXT):
                        v = a["final_norm_2" if ph != "ffn1" and "ffn1" in phases else "final_norm_w"]
                        v = v.rearrange("(o c) -> o c", o=1) if len(v.shape) == 1 else v
                        sp.dma_start(fnorm[:], v[0, :].partition_broadcast(P)).then_inc(fnorm_full, 16)
                    with sp.Fori(1, n) as i:
                        for pos in range(2 * GC):
                            load(g0 + pos, up, KG * (pos % GC), i * NW + (pair0 * NW + FF * (pos // GC)), i, 2 * GC)
                    g0 += 2 * GC * n
                    for c in range(XC):
                        for pos in range(KW * n // KG):
                            load(g0, down, KW * pair0 + KG * pos, c * NW)
                            g0 += 1
                    pair0 += n

            def mix(ph, chunks, w_out):
                g = at[ph]["g"]
                for w, col, n in chunks + [(w_out, c * NW, GC) for c in range(XC)]:
                    for pos in range(n):
                        load(g, w, KG * pos, col)
                        g += 1
                    if ph == "mix1" and w is w_out and col == 0:
                        sp.wait_ge(merged, XC)
                        for m in range(M):
                            sp.dma_start(x[:, m], a["x"][0, m * P:(m + 1) * P, :]).then_inc(x_again, 16)

            for name in VECS:
                v = a[name]
                v = v.rearrange("(r c) -> r c", c=P) if len(v.shape) == 1 else v.rearrange("o (r c) -> (o r) c", c=P)
                sp.dma_start(vecs[vec_at[name]:vec_at[name] + v.shape[0], :], v).then_inc(vec_full, 16)
            sp.dma_start(tap_rows[:], a["ffn_conv_w"].rearrange("o t (r c) -> r (o t) c", c=P)).then_inc(taps_full, 16)
            sp.dma_start(dtap_rows[:], a["dn_conv_w"].rearrange("o t (r c) -> (o t r) c", c=P)).then_inc(dtap_full, 16)
            for c in range(XC):
                sp.dma_start(x[:, :, cols(c)], a["x"][0].rearrange("(m p) d -> p m d", p=P)[:, :, cols(c)]
                             ).then_inc(x_full[c], 16)
            for ph in phases:
                if ph == "mix1":
                    mix(ph, [(a["w_in"], col, GC) for _, col in W_IN]
                        + [(a["s5_glu_w"], half_ * D + c * NW, GH) for c in range(XC) for half_ in range(2)]
                        + [(a["dn_proj_w"], c * NW, GH) for c in range(XC)], a["w_out"])
                elif ph == "mix2":
                    mix(ph, [(a["w_in_mix_2"], col, GC) for _, col in W_IN2], a["w_out_mix_2"])
                elif ph == "ffn1":
                    ffn(ph, a["ffn_up"], a["ffn_down"])
                elif ph == "ffn2":
                    ffn(ph, a["ffn1_w_in_2"], a["ffn1_w_out_2"])
                elif ph == "ffn3":
                    ffn(ph, a["ffn2_w_in_2"], a["ffn2_w_out_2"])
            if two_norms and phases[-1] == "ffn1":
                sp.wait_ge(scaled, M)
            for m in range(M):
                sp.wait_ge(scaled, (M if two_norms else 0) + m + 1)
                sp.dma_start(out[0, m * P:(m + 1) * P, :], x[:, m]).then_inc(out_done, 16)
            sp.wait_ge(out_done, 16 * M)

        counts = {consts: 0, masks: 0}

        @block.gpsimd
        def _(gp):
            def const(op, which):
                op.then_inc(which, 1)
                counts[which] += 1

            def keep(t, which, op, base, pattern, cm, fill):
                gp.wait_ge(which, counts[which])
                const(nc.gpsimd.affine_select(out=t, in_=t, compare_op=op, fill=fill, base=base, pattern=pattern,
                                              channel_multiplier=cm), which)

            const(nc.gpsimd.memset(ident[:], 0.0), consts)
            keep(ident[:], consts, ALU.not_equal, 0, [[-1, P]], 1, 1.0)
            const(nc.gpsimd.memset(half[:], -0.5), consts)
            const(nc.gpsimd.memset(ones[:], 1.0), consts)
            if "mix1" in phases:
                g2 = P // SP_
                for dst, view, full in (
                        (log_dt[:], a["s5_log_dt"].rearrange("o (t g) -> (o t) g", g=g2), s5_full),
                        (row["lr"][:], a["s5_a_re"].rearrange("o (t g) p -> (o t) (g p)", g=g2), s5_full),
                        (row["li"][:], a["s5_a_im"].rearrange("o (t g) p -> (o t) (g p)", g=g2), s5_full),
                        (b_nat[:, 0], a["s5_b_re"].rearrange("o (t g) p h -> (o g p) t h", g=g2), s5_bc_full),
                        (b_nat[:, 1], a["s5_b_im"].rearrange("o (t g) p h -> (o g p) t h", g=g2), s5_bc_full),
                        (c_nat[:, 0], a["s5_c_re"].rearrange("o (c g) h p -> (o g h) c p", c=CT), s5_bc_full),
                        (c_nat[:, 1], a["s5_c_im"].rearrange("o (c g) h p -> (o g h) c p", c=CT), s5_bc_full),
                        (ba_w[:], a["w_in"][:, :, OFF_BA:OFF_BA + 2 * H].rearrange("o (k p) n -> p (o k) n", p=P), ba_full),
                        (d_row[:], a["s5_d"][0, :].partition_broadcast(P), d_full),
                        (dt_row[:], a["dn_dt_bias"][0, :].partition_broadcast(P), dnp_full),
                        (alog_row[:], a["dn_a_log"][0, :].partition_broadcast(P), dnp_full)):
                    gp.dma_start(dst, view).then_inc(full, 16)
                const(nc.gpsimd.memset(b_wide[:], 0.0), consts)
                const(nc.gpsimd.iota(tok_i[:], pattern=[[1, T]], base=0, channel_multiplier=0), consts)
                const(nc.gpsimd.memset(triu[:], 1.0), masks)
                keep(triu[:], masks, ALU.is_ge, 0, [[1, P]], -1, 0.0)
                const(nc.gpsimd.memset(expo_mask[:], 0.0), masks)
                keep(expo_mask[:, 0], masks, ALU.is_gt, 0, [[1, P]], -1, -1e30)
                keep(expo_mask[:, 1], masks, ALU.is_ge, 0, [[1, P]], -1, -1e30)
                for l in range(LEVELS):
                    n = 1 << l
                    odd = lev_mask[:, l].rearrange("p (j h c) -> p j h c", h=2, c=n)[:, :, 1]
                    const(nc.gpsimd.memset(lev_mask[:, l], 0.0), masks)
                    gp.wait_ge(masks, counts[masks])
                    const(nc.gpsimd.memset(odd, 1.0), masks)
                    keep(odd, masks, ALU.is_ge, 0, [[-2 * n, P // (2 * n)], [0, n]], 1, 0.0)
                    keep(odd, masks, ALU.is_ge, n - 1, [[2 * n, P // (2 * n)], [0, n]], -1, 0.0)
            if "mix2" in phases:
                view = score_mask[:].rearrange("p (n i) -> p n i", i=LC)
                const(nc.gpsimd.memset(score_mask[:], 1), masks)
                keep(view, masks, ALU.is_ge, 0, [[LC, P // LC], [1, LC]], -1, 0)
                keep(view, masks, ALU.is_ge, 0, [[-LC, P // LC], [0, LC]], 1, 0)
                for t in range(16):
                    const(nc.gpsimd.memset(rcnt[:, :, t:t + 1], 1.0 / (t + 1)), masks)
                gp.wait_ge(masks, counts[masks])
                for gi in range(PG - 1):
                    w = 2 << gi
                    const(nc.gpsimd.memset(rcnt[:, gi, w:16], 1.0 / w), masks)
            gp.wait_ge(consts, counts[consts])
            for n in norm_order:
                if n == "mix2":
                    gp.wait_ge(x_new, at[n]["x"])
                    gp.dma_start(lr_w[:], a["w_in_mix_2"][:, :, OFF2["lr"]:OFF2["lr"] + GR].rearrange(
                        "o (k p) n -> p (o k) n", p=P)).then_inc(lr_full, 16)
                    gp.dma_start(wal[:], a["w_alpha_2"][0]).then_inc(wal_full, 16)
                    for g2 in range(PG):
                        gp.dma_start(wp[g2 // 2][:, g2 % 2], a["w_pool_2"][0, g2].rearrange("(k p) n -> p k n", p=P)
                                     ).then_inc(wp_full, 16)
                gp.wait_ge(ms, NORM[n] + 1)
                nc.gpsimd.tensor_tensor(rstd[:, NORM[n]], mean[:, NORM[n]], half[:, 0:M], ALU.pow).then_inc(rs, 1)
                if n == "mix1":
                    for b in range(H // 2):
                        gp.wait_ge(dn_ms, b + 1)
                        if b:
                            gp.wait_ge(dn_y, b)
                        nc.gpsimd.tensor_tensor(dn_rstd[:], dn_mean[:], half[:, 0:4], ALU.pow).then_inc(dn_rs, 1)
                if n == "mix2":
                    gp.wait_ge(g_ms, 1)
                    nc.gpsimd.tensor_tensor(g_rstd[:].rearrange("p m h -> p (m h)"), g_mean[:].rearrange("p m h -> p (m h)"),
                                            half[:, 0:M * GHD], ALU.pow).then_inc(g_rs, 1)

        const_total, mask_total = counts[consts], counts[masks]

        @block.scalar
        def _(act):
            def hi(g, i=None, per=0):
                s = g % RING
                act.wait_ge(stage_full[s], n_at(16 * (g // RING + 1), i, 16 * per // RING))
                if g >= RING or i is not None:
                    act.wait_ge(used, n_at(g - RING + 1, i, per))
                nc.scalar.activation(w_hi[:, s], stage[:, s], ACT.Copy).then_inc(hi_done, 1)

            def chunk_hi(ev, dst, k0, weight=None, i=None, w0=None, w_period=KD, chunk=tp):
                act.wait_ge(tp_full, n_at(ev + 1, i, 1))
                if w0 is not None:
                    for k in range(KW):
                        w = w0 + k % w_period
                        op = nc.scalar.activation(dst[:, k0 + k], chunk[:, k], ACT.Copy, scale=vecT[:, w:w + 1])
                    op.then_inc(hi_T, 1)
                elif weight is None:
                    nc.scalar.activation(dst[:, bass.ds(k0, KW)], chunk[:], ACT.Copy).then_inc(hi_T, 1)
                else:
                    for k in range(KW):
                        op = nc.scalar.activation(dst[:, k0 + k], chunk[:, k], ACT.Copy,
                                                  scale=weight[:, k0 + k:k0 + k + 1])
                    op.then_inc(hi_T, 1)

            n_squares = [0]

            def squares(c, halves=range(M)):
                for m in halves:
                    n = n_squares[0]
                    if n >= M:
                        act.wait_ge(sq, n - M + 1)
                    nc.scalar.activation(junk[:, n % M], x[:, m, cols(c)], ACT.Square,
                                         accum_out=ssq[:, m, c:c + 1]).then_inc(sq, 1)
                    n_squares[0] += 1

            def no_tail(pos):
                pass

            def x_tail(ev, xc, c, dst, weight):
                def tail(pos):
                    if pos == EVAC + 1:
                        act.wait_ge(x_new, xc + 1)
                        squares(c)
                    if pos == SPLIT and dst is not None:
                        chunk_hi(ev, dst[0], KW * c, weight)
                return tail

            def block_end_tail(before):
                def tail(pos):
                    before(pos)
                    m = pos - (SPLIT + 3)
                    if m in range(M):
                        act.wait_ge(scaled, m + 1)
                        for c in range(XC):
                            squares(c, [m])
                return tail

            def ffn(ph, conv, xdst, adst, tail):
                at_ph = at[ph]
                g0, ev, sr, xc, q0, cv = (at_ph[k] for k in ("g", "ev", "src", "x", "gate", "conv"))
                weight = weight_of(NEXT[ph]) if ph in NEXT else None
                both = ph == "ffn2" and two_norms
                scale = row_scale[:, :] if both else rstd[:, NORM[ph]]
                per = 2 if conv else 1

                def leave_psum(g, sr, e, s, i=None):
                    act.wait_ge(used, n_at(g, i, 2 * GC))
                    act.wait_ge(tp_full, n_at(e, i, 2))
                    for m in range(M):
                        op = nc.scalar.activation(evac[:, m], acc[:, s, m], ACT.Copy, scale=scale[:, m:m + 1])
                    op.then_inc(src, 1)

                def gate_silu(g, sr, i=None):
                    act.wait_ge(used, n_at(g, i, 2 * GC))
                    act.wait_ge(src, n_at(sr, i, 1))
                    for m in range(M):
                        op = nc.scalar.activation(sgate[:, m], acc[:, 0, m], ACT.Silu, scale=scale[:, m:m + 1])
                    op.then_inc(gated, 1)

                def pair(g, sr, e, cv, before, i=None):
                    for pos in range(2 * GC):
                        hi(g + pos, i, 2 * GC)
                        before(pos)
                        if pos == GC + EVAC and conv:
                            leave_psum(g + GC, sr, e, 0, i)
                        if pos == GC + EVAC and not conv:
                            gate_silu(g + GC, sr, i)
                        if pos == GC + SPLIT + 2 and conv:
                            act.wait_ge(conved, n_at(cv + 1, i, 2))
                            nc.scalar.activation(conv_g[:], conv_g[:], ACT.Silu).then_inc(gated, 1)

                def pair_tail(g, sr, e, pr, k0, i=None):
                    def tail(pos):
                        if pos == EVAC and conv:
                            leave_psum(g, sr, e, 1, i)
                        if pos == SPLIT + 2 and conv:
                            act.wait_ge(prod, n_at(pr + 1, i, 1))
                            nc.scalar.activation(adst[0][:, bass.ds(k0, KW)], conv_v[:], ACT.Copy).then_inc(hi_T, 1)
                        if pos == SPLIT and not conv:
                            chunk_hi(e, adst[0], k0, None, i)
                    return tail

                pr = at_ph["prod"]
                if ph == "ffn1" and two_norms:
                    act.wait_ge(blk_ready, 1)
                for p, n in enumerate(PARTS):
                    if p == 0:
                        x_end = tail

                        def tail(pos):
                            x_end(pos)
                            if pos == GC + EVAC - 1:
                                if both:
                                    act.wait_ge(rescaled, 1)
                                else:
                                    act.wait_ge(rs, NORM[ph] + 1)
                    pair(g0, sr, ev, cv, tail)
                    with act.Fori(1, n) as i:
                        last = pair_tail(g0, sr - 1, ev - 1, pr - 1, i * KW - KW, i)
                        pair(g0, sr, ev, cv, last, i)
                    g0, sr, ev, cv, pr = g0 + 2 * GC * n, sr + per * n, ev + per * n, cv + 2 * n, pr + n
                    tail = pair_tail(g0, sr - 1, ev - 1, pr - 1, KW * (n - 1))
                    older = no_tail
                    for c in range(XC):
                        for pos in range(KW * n // KG):
                            hi(g0)
                            g0 += 1
                            tail(pos)
                            older(pos + KW * n // KG)
                        older, tail = tail if c == 0 else no_tail, no_tail
                        if p == len(PARTS) - 1:
                            tail = x_tail(ev, xc + c, c, xdst, weight)
                            ev += xdst is not None
                    xc += XC
                if ph == "ffn1" and two_norms:
                    tail = block_end_tail(tail)
                return tail

            steps = [0]

            def link(op):
                op.then_inc(step_a, 1)
                steps[0] += 1
                act.wait_ge(step_a, steps[0])

            def s5():
                def turns(t):
                    b = t % 2
                    if t >= 2:
                        act.wait_ge(s5_x, t - 1)
                    link(nc.scalar.activation(angle[:, b], tok[:], ACT.Copy, scale=s5p[:, 1, t:t + 1], bias=MAGIC))
                    nc.scalar.activation(angle[:, b], angle[:, b], ACT.Copy, bias=-MAGIC).then_inc(s5_turn, 1)

                def sines(t):
                    b = t % 2
                    act.wait_ge(s5_frac, t + 1)
                    link(nc.scalar.activation(sn[:, b], angle[:, b], ACT.Sin, scale=TURN))
                    link(nc.scalar.activation(angle[:, b], angle[:, b], ACT.Sin, scale=TURN / 2))
                    link(nc.scalar.activation(angle[:, b], angle[:, b], ACT.Square))
                    nc.scalar.activation(angle[:, b], angle[:, b], ACT.Copy, scale=-2.0, bias=1.0).then_inc(s5_sin, 1)

                act.wait_ge(s5_full, 48)
                nc.scalar.activation(s5_dt[:], log_dt[:], ACT.Exp).then_inc(par_dt, 1)
                yield
                act.wait_ge(par_th, 1)
                nc.scalar.activation(row["mag"][:], row["lrdt"][:], ACT.Exp)
                nc.scalar.activation(row["sn"][:], row["f"][:], ACT.Sin, scale=TURN)
                link(nc.scalar.activation(row["sh"][:], row["f"][:], ACT.Sin, scale=TURN / 2))
                nc.scalar.activation(row["sh"][:], row["sh"][:], ACT.Square).then_inc(par_trig, 1)
                yield
                act.wait_ge(ba_full, 16)
                nc.scalar.activation(ba_hi[:], ba_w[:], ACT.Copy).then_inc(ba_split, 1)
                yield
                yield
                act.wait_ge(par_T, 1)
                nc.scalar.activation(s5p[:], side[:, 0, 0:6 * ST].rearrange("p (n t) -> p n t", t=ST), ACT.Copy).then_inc(par_in, 1)
                yield
                act.wait_ge(ba_mm, 1)
                act.wait_ge(rs, NORM["mix1"] + 1)
                for m in range(M):
                    op = nc.scalar.activation(ba[:, m], side[:, 1, m * 2 * H:(m + 1) * 2 * H], ACT.Copy,
                                              scale=rstd[:, NORM["mix1"], m:m + 1])
                op.then_inc(ba_in, 1)
                yield
                act.wait_ge(ba_neg, 1)
                nc.scalar.activation(ba_ln[:], ba_abs[:], ACT.Exp, scale=-1.0).then_inc(ba_log, 1)
                act.wait_ge(dnp_full, 32)
                nc.scalar.activation(ea_row[:], alog_row[:], ACT.Exp).then_inc(ba_log, 1)
                yield
                act.wait_ge(ba_neg, 2)
                nc.scalar.activation(ba_ln[:], ba_ln[:], ACT.Ln).then_inc(ba_log, 1)
                yield
                yield
                yield
                for q in range(4):
                    for b in range(2):
                        act.wait_ge(wide_T, 2 * q + b + 1)
                        dst = s5_B if q < 2 else s5_C
                        nc.scalar.activation(dst[:, 4 * b:4 * b + 4, q % 2], side[:, b].rearrange("p (c s) -> p c s", s=P),
                                             ACT.Copy, scale=-1.0 if q == 3 else 1.0).then_inc(wide_in, 1)
                    yield
                act.wait_ge(tok_done, 1)
                turns(0)
                sines(0)
                yield
                for n in range(15, S5_SLOT):
                    yield
                for t in range(ST):
                    if t + 1 < ST:
                        turns(t + 1)
                    yield
                    yield
                    if t + 1 < ST:
                        sines(t + 1)
                    yield
                act.wait_ge(s5_res, CT)
                for m in range(M):
                    op = nc.scalar.activation(ud[:, m], ud[:, m], ACT.Gelu)
                op.then_inc(s5_gelu, 1)
                for n in range(S5_REST):
                    yield
                for c in range(NU):
                    act.wait_ge(s5_T, c + 1)
                    nc.scalar.activation(B[0][:, KW * c:KW * (c + 1)], side_T, ACT.Copy).then_inc(hi_T, 1)
                    yield

            def delta(e0):
                for j in range(2 * H // KW):
                    act.wait_ge(qkv_act, j + 1)
                    if j:
                        act.wait_ge(qk_ss, j)
                    nc.scalar.activation(sq4[:], qkvT[:, KW * j:KW * (j + 1)], ACT.Square).then_inc(qk_sq, 1)
                    yield
                act.wait_ge(dn_ssin, 1)
                nc.scalar.activation(dn_ss[:], dn_ss[:], ACT.Ln).then_inc(dn_lns, 1)
                act.wait_ge(dn_rows, 1)
                nc.scalar.activation(dv["wk"][:], dv["colk"][:], ACT.Exp)
                nc.scalar.activation(dv["wq"][:], dv["colq"][:], ACT.Exp)
                nc.scalar.activation(dv["beta"][:], dv["lnb"][:], ACT.Exp)
                nc.scalar.activation(dn_tail[:], dn_tail[:], ACT.Exp).then_inc(dn_fac, 1)
                yield
                for b in range(H // 2):
                    unit = [(h, m) for h in (2 * b, 2 * b + 1) for m in range(M)]
                    act.wait_ge(dn_masked, b + 1)
                    for w in range(2):
                        for u, (h, m) in enumerate(unit):
                            op = nc.scalar.activation(dec[:, w, u], dec[:, w, u], ACT.Exp, bias=dv["rowk"][:, m, h:h + 1])
                    op.then_inc(dn_decay, 1)
                    yield
                    act.wait_ge(dn_vk, b + 1)
                    act.wait_ge(sq, M * XC)
                    for u, (h, m) in enumerate(unit):
                        nc.scalar.activation(vb[:, u], dnb(0)[:, u * P:(u + 1) * P], ACT.Copy, scale=dv["beta"][:, m, h:h + 1])
                    for e in range(2):
                        op = nc.scalar.activation(ktail[:, e], dnb(1)[:, e * P:(e + 1) * P], ACT.Copy,
                                                  scale=dn_tail[:, 2 * b + e:2 * b + e + 1])
                    op.then_inc(dn_vb, 1)
                    yield
                    yield
                    yield
                    for l in range(1, LEVELS):
                        act.wait_ge(dn_P, (LEVELS - 1) * b + l)
                        nc.scalar.activation(PP[:].rearrange("p u c -> p (u c)"), dnb(0), ACT.Copy).then_inc(dn_Pin, 1)
                        yield
                        yield
                    act.wait_ge(dn_new, 2 * b + 1)
                    nc.scalar.activation(vnew[:, 0:2], dnb(0)[:, 0:2 * P].rearrange("p (e c) -> p e c", c=P),
                                         ACT.Copy).then_inc(dn_newin, 1)
                    yield
                    act.wait_ge(dn_St, b + 1)
                    nc.scalar.activation(dn_S[:], dnb(0)[:, 0:2 * P].rearrange("p (e c) -> p e c", c=P),
                                         ACT.Copy).then_inc(dn_Sin, 1)
                    yield
                    yield
                    act.wait_ge(dn_new, 2 * b + 2)
                    nc.scalar.activation(vnew[:, 2:4], dnb(0)[:, 0:2 * P].rearrange("p (e c) -> p e c", c=P),
                                         ACT.Copy).then_inc(dn_newin, 1)
                    yield
                    act.wait_ge(dn_ofull, b + 1)
                    if b:
                        act.wait_ge(dn_ms, b)
                    for u in range(4):
                        if u or b:
                            act.wait_ge(dn_sq, 4 * b + u)
                        nc.scalar.activation(dn_junk[:], dn_o[:, u], ACT.Square,
                                             accum_out=dn_ssq[:, u:u + 1]).then_inc(dn_sq, 1)
                    yield
                yield
                for c in range(NZ):
                    chunk_hi(e0 + c, B[0], KW * (NU + c), None, None, vec_at["dn_norm_w"], 1)
                    yield

            def mix1(xdst, tail):
                g0, e0, xc = (at["mix1"][k] for k in ("g", "ev", "x"))
                g = g0
                scale = rstd[:, NORM["mix1"]]
                e_y = e0 + NU + NQ
                e_m = e_y + NZ
                e_x = e_m + XC
                scan, rule = s5(), delta(e_y)

                def leave(c, kind):
                    def tail(pos):
                        if pos == EVAC:
                            act.wait_ge(used, g0 + GC * (c + 1))
                            dst = {"z": zs, "gs": gs, "gd": gd}.get(kind)
                            if dst is None:
                                act.wait_ge(tp_full, e0 + c)
                                if 1 <= c <= NU:
                                    act.wait_ge(skip_done, c)
                            if kind == "gd":
                                act.wait_ge(s5_res, CT)
                            o = dict(z=NU + NQ, gs=NU + NQ + NZ, gd=NU + NQ + NZ + XC).get(kind, c)
                            for m in range(M):
                                to = evac[:, m] if dst is None else dst[:, m, cols(c - o)]
                                op = nc.scalar.activation(to, acc[:, c % 2, m], ACT.Silu if kind == "z" else ACT.Copy,
                                                          scale=scale[:, m:m + 1])
                            op.then_inc(left, 1)
                        if pos == SPLIT and kind == "u":
                            act.wait_ge(tp_full, e0 + c + 1)
                            nc.scalar.activation(uT[:, KW * c:KW * (c + 1)], tp[:], ACT.Copy).then_inc(copied, 1)
                        if pos == SPLIT - 1 and kind == "qkv":
                            act.wait_ge(tp_full, e0 + c + 1)
                            for k in range(KW):
                                n = KW * (c - NU) + k
                                op = nc.scalar.activation(qkvT[:, n], tp[:, k], ACT.Copy, scale=dtaps[:, DTAPS - 1, n:n + 1])
                            op.then_inc(dn_tap, 1)
                        if pos == GC + 1 and kind == "qkv":
                            act.wait_ge(dn_conved, c - NU + 1)
                            q = qkvT[:, KW * (c - NU):KW * (c - NU + 1)]
                            nc.scalar.activation(q, q, ACT.Silu).then_inc(qkv_act, 1)
                    return tail

                def advance(slot):
                    if slot >= 0:
                        next(scan, None)
                    if slot >= DN_SLOT:
                        next(rule, None)

                older = no_tail
                for c, (kind, _) in enumerate(W_IN):
                    for pos in range(GC):
                        hi(g)
                        if c == 0 and pos == GC - 1:
                            act.wait_ge(rs, NORM["mix1"] + 1)
                        tail(pos)
                        older(pos + GC)
                        advance(g - g0 - LEAD)
                        g += 1
                    older = tail if c else no_tail
                    tail = leave(c, kind)
                for _ in scan:
                    pass
                older = no_tail
                c0 = len(W_IN)

                def glu(j):
                    def tail(pos):
                        if pos == EVAC:
                            act.wait_ge(used, g0 + GC * c0 + GH * (2 * j + 2))
                            if j:
                                act.wait_ge(s5_part, j)
                            op = nc.scalar.activation(evac[:], acc[:, 1], ACT.Sigmoid).then_inc(glu_sig, 1)
                    return tail

                def both(j):
                    def tail(pos):
                        if pos == SPLIT:
                            chunk_hi(e_m + j, A[0], KW * j)
                    return tail

                def sigmoid(t, c, j):
                    act.wait_ge(left, c + 1)
                    nc.scalar.activation(t[:, :, cols(j)], t[:, :, cols(j)], ACT.Sigmoid).then_inc(gate_sig, 1)

                for c in range(3 * XC):
                    if c == 2 * XC:
                        for _ in rule:
                            pass
                    for pos in range(GH):
                        hi(g)
                        tail(pos)
                        older(pos + GH)
                        if pos == 1 and c < 2 * XC and c % 2 == 0:
                            sigmoid(gs, NU + NQ + NZ + c // 2, c // 2)
                        if pos == 1 and c >= 2 * XC:
                            sigmoid(gd, NU + NQ + NZ + XC + c - 2 * XC, c - 2 * XC)
                        if c < 2 * XC:
                            next(rule, None)
                        g += 1
                    older = tail if c else no_tail
                    tail = (glu(c // 2) if c % 2 else no_tail) if c < 2 * XC else both(c - 2 * XC)
                for c in range(XC):
                    for pos in range(GC):
                        hi(g)
                        tail(pos)
                        if c == 0 and pos < GH:
                            older(pos + GH)
                        g += 1
                    tail = x_tail(e_x + c, xc + c, c, xdst, weight_of(NEXT["mix1"]))
                return tail

            def attention():
                n, n_junk = ATT_WARM + 4, False
                for _ in range(ATT_WARM):
                    yield
                act.wait_ge(lr_full, 16)
                nc.scalar.activation(lr_hi[:], lr_w[:], ACT.Copy).then_inc(lr_split, 1)
                yield
                act.wait_ge(lr_mm, 1)
                act.wait_ge(rs, NORM["mix2"] + 1)
                for m in range(M):
                    op = nc.scalar.activation(lr2[:, m], side[:, 0, m * GR:(m + 1) * GR], ACT.Copy,
                                              scale=rstd[:, NORM["mix2"], m:m + 1])
                op.then_inc(lr_in, 1)
                yield
                act.wait_ge(lr_T, 1)
                nc.scalar.activation(lrT[:], side[0:GR, 0, 0:T], ACT.Copy).then_inc(lr_Tin, 1)
                yield
                act.wait_ge(al_mm, 1)
                for h in range(GHD):
                    w = vec_at["b_alpha_2"] + h
                    op = nc.scalar.activation(la[:, h], side[:, h // 2, (h % 2) * T:(h % 2 + 1) * T], ACT.Identity,
                                              bias=vecT[:, w:w + 1])
                op.then_inc(al_in, 1)
                act.wait_ge(al_abs, 1)
                nc.scalar.activation(lt[:], lt[:], ACT.Exp, scale=-1.0).then_inc(al_exp, 1)
                act.wait_ge(al_one, 1)
                nc.scalar.activation(lt[:], lt[:], ACT.Ln).then_inc(al_ln, 1)
                yield
                while n < ATT_SLOT:
                    n += 1
                    yield
                act.wait_ge(al_cum, 1)
                nc.scalar.activation(gdec[:], lt[:].rearrange("p h (n t) -> p h n t", t=LC)[:, :, :, LC - 1], ACT.Exp,
                                     scale=1.0 / GATE_NORM)
                nc.scalar.activation(la[:], lt[:], ACT.Exp, scale=1.0 / GATE_NORM).then_inc(al_dec, 1)
                act.wait_ge(qk_dec, 1)
                nc.scalar.activation(la[:], lt[:], ACT.Exp, scale=-1.0 / GATE_NORM).then_inc(al_dec, 1)
                yield
                act.wait_ge(qk_dec, 3)
                nc.scalar.activation(la[:], la[:], ACT.Exp, scale=1.0 / GATE_NORM).then_inc(al_dec, 1)
                yield
                act.wait_ge(gk_T, 1)
                nc.scalar.activation(ktT[:].rearrange("p m h d -> p m (h d)"), side[:], ACT.Copy).then_inc(gk_in, 1)
                yield
                yield
                for n in range(LN - 1):
                    yield
                for m in range(M):
                    act.wait_ge(g_o, m + 1)
                    for h in range(GHD):
                        o = side[:, h // 2, (h % 2) * GV:(h % 2 + 1) * GV]
                        if n_junk:
                            act.wait_ge(step_a, steps[0])
                        op = nc.scalar.activation(junk[:, 0, 0:GV], o, ACT.Square, accum_out=g_ssq[:, m, h:h + 1])
                        op.then_inc(step_a, 1)
                        steps[0] += 1
                        n_junk = True
                    act.wait_ge(step_a, steps[0])
                    nc.scalar.activation(vv[:, m], side[:].rearrange("p b n -> p (b n)"), ACT.Copy).then_inc(g_oin, 1)
                    yield

            def mix2(xdst, tail):
                g0, e0, xc = (at["mix2"][k] for k in ("g", "ev", "x"))
                g = g0
                scale = rstd[:, NORM["mix2"]]
                event = dict(u0=0, p0=1, u1=2, p1=3, q=4, k=5, y0=6, y1=7)
                e_x = e0 + len(event)
                side_work = attention()

                def leave(c, kind, n):
                    def tail(pos):
                        e = e0 + event.get(kind, event.get(f"{kind}{n}", 0))
                        if pos == EVAC:
                            act.wait_ge(used, g0 + GC * (c + 1))
                            to = evac[:]
                            if kind in ("v", "g"):
                                to = (vv if kind == "v" else sg)[:, :, cols(n)]
                            else:
                                act.wait_ge(tp_full, e)
                            for m in range(M):
                                op = nc.scalar.activation(to[:, m], acc[:, c % 2, m], ACT.Silu if kind == "g" else ACT.Copy,
                                                          scale=scale[:, m:m + 1])
                            op.then_inc(left, 1)
                        if pos == SPLIT and kind in ("u", "q", "k"):
                            act.wait_ge(tp_full, e + 1)
                            to = u2T[:, KW * n:KW * (n + 1)] if kind == "u" else (qd if kind == "q" else kt)[:]
                            nc.scalar.activation(to, tp[:], ACT.Copy, scale=P ** -0.5 if kind == "q" else 1.0).then_inc(copied, 1)
                        if pos == GC + 2 and kind == "u":
                            chunk_hi(e0 + event[f"p{n}"], A[0], KW * n, None, None, vec_at["pool_scale_2"] + KW * n)
                        if pos == SPLIT + 1 and kind == "g":
                            chunk_hi(e0 + event[f"y{n}"], A[0], KW * (VC + n), None, None, vec_at["gla_norm_2"], GV // P)
                    return tail

                older, n = no_tail, {}
                for c, (kind, _) in enumerate(W_IN2):
                    for pos in range(GC):
                        hi(g)
                        if c == 0 and pos == GC - 1:
                            act.wait_ge(rs, NORM["mix2"] + 1)
                        tail(pos)
                        older(pos + GC)
                        if g - g0 >= LEAD:
                            next(side_work, None)
                        g += 1
                    older = tail if c else no_tail
                    tail = leave(c, kind, n.get(kind, 0))
                    n[kind] = n.get(kind, 0) + 1
                for _ in side_work:
                    pass
                for c in range(XC):
                    for pos in range(GC):
                        hi(g)
                        tail(pos)
                        g += 1
                    tail = x_tail(e_x + c, xc + c, c, xdst, weight_of(NEXT["mix2"]))
                return tail

            act.wait_ge(vec_T, 2 + TAPS)
            nc.scalar.activation(vecT[:], side[:, 0, 0:VEC_ROWS], ACT.Copy).then_inc(vec_in, 1)
            for t in range(TAPS):
                nc.scalar.activation(taps[:, t], side[:, 0, P * (t + 1):P * (t + 1) + FT], ACT.Copy).then_inc(vec_in, 1)
            nc.scalar.activation(dtaps[:], side[:, 1, 0:DTAPS * QT].rearrange("p (t r) -> p t r", r=QT), ACT.Copy).then_inc(vec_in, 1)
            act.wait_ge(vec_in, 1)
            for c in range(XC):
                chunk_hi(c, first_x[0], KW * c, weight_of(phases[1]), chunk=(tp, side_T)[c % 2])

            def first_squares(pos):
                if pos < XC:
                    act.wait_ge(x_full[pos], 16)
                    squares(pos)

            tail = first_squares
            for ph in phases[1:]:
                if ph in ("ffn1", "ffn2", "ffn3"):
                    tail = ffn(ph, ph == "ffn1", B if ph in NEXT else None, A, tail)
                elif ph == "mix1":
                    tail = mix1(B if ph in NEXT else None, tail)
                elif ph == "mix2":
                    tail = mix2(B if ph in NEXT else None, tail)
            for pos in range(GC):
                tail(pos)

        @block.vector
        def _(dve):
            def lo(g, i=None, per=0):
                dve.wait_ge(hi_done, n_at(g + 1, i, per))
                s = g % RING
                nc.vector.tensor_tensor(w_lo[:, s], stage[:, s], w_hi[:, s].bitcast(F32), ALU.subtract).then_inc(lo_done, 1)

            def chunk_lo(op, dst, k0, weight=None, i=None, w0=None, w_period=KD, chunk=tp):
                dve.wait_ge(hi_T, n_at(op + 1, i, 1))
                if w0 is not None:
                    for k in range(KW):
                        w = w0 + k % w_period
                        o = nc.vector.scalar_tensor_tensor(
                            out=dst[1][:, k0 + k], in0=chunk[:, k], scalar=vecT[:, w:w + 1],
                            in1=dst[0][:, k0 + k].bitcast(F32), op0=ALU.mult, op1=ALU.subtract)
                    o.then_inc(op_T, 1)
                elif weight is None:
                    k = bass.ds(k0, KW)
                    nc.vector.tensor_tensor(dst[1][:, k], chunk[:], dst[0][:, k].bitcast(F32),
                                            ALU.subtract).then_inc(op_T, 1)
                else:
                    for k in range(k0, k0 + KW):
                        o = nc.vector.scalar_tensor_tensor(
                            out=dst[1][:, k], in0=chunk[:, k - k0], scalar=weight[:, k:k + 1],
                            in1=dst[0][:, k].bitcast(F32), op0=ALU.mult, op1=ALU.subtract)
                    o.then_inc(op_T, 1)

            def norm(n):
                k = NORM[n]
                dve.wait_ge(sq, sq_count[n])
                nc.vector.tensor_reduce(out=sumsq[:, k], in_=ssq[:], axis=AX.X, op=ALU.add).then_inc(sums, 1)
                dve.wait_ge(sums, k + 1)
                nc.vector.tensor_scalar(mean[:, k], sumsq[:, k], 1.0 / D, EPS, ALU.mult, ALU.add).then_inc(ms, 1)

            def no_tail(pos):
                pass

            def x_tail(g, op, xc, c, alpha, dst, weight, after):
                def tail(pos):
                    if pos == EVAC:
                        dve.wait_ge(used, g)
                        dve.wait_ge(*after)
                        nc.vector.scalar_tensor_tensor(out=x[:, :, cols(c)], in0=acc[:, c % 2], scalar=alpha,
                                                       in1=x[:, :, cols(c)], op0=ALU.mult, op1=ALU.add).then_inc(x_new, 1)
                    if pos == SPLIT and dst is not None:
                        chunk_lo(op, dst, KW * c, weight)
                return tail

            def norm_tail(n, before):
                def tail(pos):
                    before(pos)
                    if pos == SPLIT + 1:
                        norm(n)
                return tail

            def apply_norm(n, m):
                nc.vector.scalar_tensor_tensor(out=x[:, m], in0=x[:, m], scalar=rstd[:, NORM[n], m:m + 1],
                                               in1=fnorm[:], op0=ALU.mult, op1=ALU.mult).then_inc(scaled, 1)

            def block_end_tail(nxt, op, before):
                def tail(pos):
                    before(pos)
                    if pos == SPLIT + 1:
                        norm("block end")
                    if pos in (SPLIT + 2, SPLIT + 3):
                        if pos == SPLIT + 2:
                            dve.wait_ge(rs, NORM["block end"] + 1)
                            dve.wait_ge(fnorm_full, 16)
                            dve.wait_ge(op_T, op)
                        apply_norm("block end", pos - SPLIT - 2)
                    if pos == SPLIT + 5:
                        norm(nxt)
                        dve.wait_ge(rs, NORM[nxt] + 1)
                        nc.vector.tensor_tensor(row_scale[:], rstd[:, NORM[nxt]], rstd[:, NORM["block end"]],
                                                ALU.mult).then_inc(rescaled, 1)
                return tail

            def ffn(ph, conv, alpha, xdst, adst, tail, x_after):
                at_ph = at[ph]
                g0, ev, op, sr, xc, q0, cv, pr = (at_ph[k] for k in ("g", "ev", "op", "src", "x", "gate", "conv", "prod"))
                weight = weight_of(NEXT[ph]) if ph in NEXT else None
                both = ph == "ffn2" and two_norms
                scale = row_scale[:, :] if both else rstd[:, NORM[ph]]
                per = 2 if conv else 1

                def convolve(part, cv, e, ft, dst, free, i=None):
                    if part == 0:
                        dve.wait_ge(tp_full, n_at(e + 1, i, 2))
                        dve.wait_ge(*free)
                    n = KW // 2
                    done = 2 * KW * cv + KW * part
                    ks = range(n * part, n * (part + 1))
                    for k in ks:
                        w = taps[:, TAPS - 1, bass.ds(ft + k, 1)]
                        nc.vector.tensor_scalar(dst[:, k], tp[:, k], w, None, ALU.mult).then_inc(tap_step, 1)
                    for back in range(1, TAPS):
                        for k in ks:
                            dve.wait_ge(tap_step, n_at(done + n * (back - 1) + k % n + 1, i, 4 * KW))
                            w = taps[:, TAPS - 1 - back, bass.ds(ft + k, 1)]
                            o = nc.vector.scalar_tensor_tensor(
                                out=dst[:, k, back:T], in0=tp[:, k, 0:T - back], scalar=w, in1=dst[:, k, back:T],
                                op0=ALU.mult, op1=ALU.add)
                            if back < TAPS - 1:
                                o.then_inc(tap_step, 1)
                    if part:
                        o.then_inc(conved, 1)

                def pair(g, e, cv, ft, op, before, i=None):
                    for pos in range(2 * GC):
                        lo(g + pos, i, 2 * GC)
                        before(pos)
                        if pos in (GC + SPLIT, GC + SPLIT + 1) and conv:
                            convolve(pos - GC - SPLIT, cv, e, ft, conv_g, (prod, n_at(op, i, 1)), i)

                def pair_tail(g, e, q, sr, cv, op, pr, ft, k0, i=None):
                    def tail(pos):
                        if pos == EVAC and not conv:
                            dve.wait_ge(used, n_at(g, i, 2 * GC))
                            dve.wait_ge(gated, n_at(q + 1, i, 1))
                            dve.wait_ge(tp_full, n_at(e, i, 1))
                            for m in range(M):
                                o = nc.vector.scalar_tensor_tensor(
                                    out=evac[:, m], in0=acc[:, 1, m], scalar=scale[:, m:m + 1], in1=sgate[:, m],
                                    op0=ALU.mult, op1=ALU.mult)
                            o.then_inc(src, 1)
                        if pos == SPLIT and not conv:
                            chunk_lo(op, adst, k0, None, i)
                        if pos in (SPLIT, SPLIT + 1) and conv:
                            convolve(pos - SPLIT, cv, e, ft, conv_v, (op_T, n_at(op, i, 1)), i)
                        if pos == SPLIT + 1 and conv:
                            dve.wait_ge(gated, n_at(q + 1, i, 1))
                            dve.wait_ge(conved, n_at(cv + 1, i, 2))
                            nc.vector.tensor_tensor(conv_v[:], conv_v[:], conv_g[:], ALU.mult).then_inc(prod, 1)
                        if pos == SPLIT + 2 and conv:
                            dve.wait_ge(hi_T, n_at(op + 1, i, 1))
                            k = bass.ds(k0, KW)
                            nc.vector.tensor_tensor(adst[1][:, k], conv_v[:], adst[0][:, k].bitcast(F32),
                                                    ALU.subtract).then_inc(op_T, 1)
                    return tail

                ft = 0
                for p, n in enumerate(PARTS):
                    pair(g0, ev, cv, ft, pr, tail)
                    with dve.Fori(1, n) as i:
                        last = pair_tail(g0, ev - 1, q0 - 1, sr - 1, cv - 1, op - 1, pr - 1,
                                         i * KW + (FT // 2 + ft - KW), i * KW - KW, i)
                        pair(g0, ev, cv, i * KW + ft, pr, last, i)
                    g0, sr, ev, cv = g0 + 2 * GC * n, sr + per * n, ev + per * n, cv + 2 * n
                    pr, q0, op, ft = pr + n, q0 + n, op + n, ft + KW * n
                    tail = pair_tail(g0, ev - 1, q0 - 1, sr - 1, cv - 1, op - 1, pr - 1, FT // 2 + ft - KW, KW * (n - 1))
                    older = no_tail
                    for c in range(XC):
                        for pos in range(KW * n // KG):
                            lo(g0)
                            g0 += 1
                            tail(pos)
                            older(pos + KW * n // KG)
                        older = tail if c == 0 else no_tail
                        end = p == len(PARTS) - 1 and xdst is not None
                        tail = x_tail(g0, op, xc + c, c, alpha, xdst if end else None, weight, x_after)
                        op += end
                        x_after = (x_new, xc + c + 2 - XC) if p or c == XC - 1 else x_after
                        x_after = (x_new, xc + c + 2 - XC) if xc + c + 2 - XC > at_ph["x"] else x_after
                    xc += XC
                if ph == "ffn1" and two_norms:
                    return block_end_tail(NEXT[ph], op, tail)
                return norm_tail(NEXT.get(ph, "result"), tail)

            if two_norms:
                dve.wait_ge(vec_in, 1)
                f, n1 = vec_at["final_norm_w"], vec_at[NORM_W["ffn2"]]
                nc.vector.tensor_tensor(blk_w[:], vecT[:, f:f + KD], vecT[:, n1:n1 + KD], ALU.mult).then_inc(blk_ready, 1)
            steps = [0]

            def link(op):
                op.then_inc(step_d, 1)
                steps[0] += 1
                dve.wait_ge(step_d, steps[0])

            def free_wide(t, n):
                return t.unsqueeze(len(t.shape)).to_broadcast(list(t.shape) + [n])

            TT, TS, STT = nc.vector.tensor_tensor, nc.vector.tensor_scalar, nc.vector.scalar_tensor_tensor

            def s5(o0):
                def fractions(t):
                    b = t % 2
                    dve.wait_ge(s5_turn, t + 1)
                    n = 2 * t
                    STT(out=angle[:, b], in0=tok[:], scalar=s5p[:, 2, t:t + 1], in1=angle[:, b],
                        op0=ALU.mult, op1=ALU.subtract).then_inc(s5_part_turn, 1)
                    yield
                    dve.wait_ge(s5_part_turn, n + 1)
                    STT(out=angle[:, b], in0=tok[:], scalar=s5p[:, 3, t:t + 1], in1=angle[:, b],
                        op0=ALU.mult, op1=ALU.add).then_inc(s5_part_turn, 1)
                    yield
                    dve.wait_ge(s5_part_turn, n + 2)
                    TS(angle[:, b], angle[:, b], 0.5, -0.5, ALU.min, ALU.max).then_inc(s5_frac, 1)

                r = {n: t[:] for n, t in row.items()}
                g2 = P // SP_
                dve.wait_ge(par_dt, 1)
                dt = free_wide(s5_dt[:], SP_)
                lr, li = (r[n].rearrange("t (g p) -> t g p", g=g2) for n in ("lr", "li"))
                TT(r["lrdt"].rearrange("t (g p) -> t g p", g=g2), lr, dt, ALU.mult)
                link(TT(r["th"].rearrange("t (g p) -> t g p", g=g2), li, dt, ALU.mult))
                link(TS(r["k"], r["th"], IN_TURNS, MAGIC, ALU.mult, ALU.add))
                link(TS(r["k"], r["k"], MAGIC, None, ALU.subtract))
                for c in (TURN_1, TURN_2, TURN_3):
                    link(STT(out=r["th"], in0=r["k"], scalar=-c, in1=r["th"], op0=ALU.mult, op1=ALU.add))
                link(TS(r["f"], r["th"], IN_TURNS, None, ALU.mult))
                TS(r["f"], r["f"], 0.5, -0.5, ALU.min, ALU.max).then_inc(par_th, 1)
                yield
                TT(r["t1"], r["lr"], r["lr"], ALU.mult)
                link(TT(r["t2"], r["li"], r["li"], ALU.mult))
                TT(r["den"], r["t1"], r["t2"], ALU.add)
                dve.wait_ge(par_th, 1)
                link(TS(row_fhi[:], r["f"], 1.0, None, ALU.mult))
                TT(r["flo"], r["f"], row_fhi[:].bitcast(F32), ALU.subtract)
                link(nc.vector.reciprocal(r["den"], r["den"]))
                yield
                dve.wait_ge(par_trig, 1)
                TT(r["ai"], r["mag"], r["sn"], ALU.mult)
                link(TS(r["cs"], r["sh"], -2.0, 1.0, ALU.mult, ALU.add))
                link(TT(r["ar"], r["mag"], r["cs"], ALU.mult))
                link(TS(r["ar"], r["ar"], 1.0, None, ALU.subtract))
                dve.wait_ge(ba_split, 1)
                TT(ba_lo[:], ba_w[:], ba_hi[:].bitcast(F32), ALU.subtract).then_inc(ba_split, 1)
                yield
                TT(r["t1"], r["ar"], r["lr"], ALU.mult)
                link(TT(r["t2"], r["ai"], r["li"], ALU.mult))
                link(TT(r["cr"], r["t1"], r["t2"], ALU.add))
                TT(r["t1"], r["ai"], r["lr"], ALU.mult)
                link(TT(r["t2"], r["ar"], r["li"], ALU.mult))
                link(TT(r["ci"], r["t1"], r["t2"], ALU.subtract))
                TT(r["cr"], r["cr"], r["den"], ALU.mult)
                TT(r["ci"], r["ci"], r["den"], ALU.mult).then_inc(par_done, 1)
                yield
                dve.wait_ge(s5_bc_full, 64)
                dve.wait_ge(consts, const_total)
                nc.vector.tensor_copy(tok[:], tok_i[:]).then_inc(tok_done, 1)
                link(nc.vector.tensor_reduce(out=par[:], in_=ident[:].rearrange("p (j g h) -> p g j h", g=g2, h=SH),
                                             axis=AX.XY, op=ALU.add))
                for n in range(2):
                    for e in range(g2):
                        TS(c_wide[:, n, :, e], c_nat[:, n], par[:, e:e + 1], None, ALU.mult)
                yield
                dve.wait_ge(par_in, 1)
                cr, ci = (free_wide(s5p[:, 4 + n], SH) for n in range(2))
                TT(b_t[:, 0], b_nat[:, 0], cr, ALU.mult)
                link(TT(b_t[:, 1], b_nat[:, 1], ci, ALU.mult))
                yield
                for e in range(g2):
                    g_ = slice(e * SP_, (e + 1) * SP_)
                    o = TT(b_wide[g_, 0, :, e], b_t[g_, 0], b_t[g_, 1], ALU.subtract)
                link(o)
                dve.wait_ge(ba_in, 1)
                dve.wait_ge(dnp_full, 32)
                TS(ba[:, :, 0:H], ba[:, :, 0:H], -1.0, None, ALU.mult)
                link(TT(ba[:, :, H:2 * H], ba[:, :, H:2 * H], dt_row[:].unsqueeze(1).to_broadcast([P, M, H]), ALU.add))
                STT(out=ba_abs[:], in0=ba[:], scalar=-1.0, in1=ba[:], op0=ALU.mult, op1=ALU.max).then_inc(ba_neg, 1)
                yield
                dve.wait_ge(ba_log, 1)
                TS(ba_ln[:], ba_ln[:], 1.0, None, ALU.add).then_inc(ba_neg, 1)
                TT(b_t[:, 0], b_nat[:, 0], ci, ALU.mult)
                link(TT(b_t[:, 1], b_nat[:, 1], cr, ALU.mult))
                yield
                for e in range(g2):
                    g_ = slice(e * SP_, (e + 1) * SP_)
                    o = TT(b_wide[g_, 1, :, e], b_t[g_, 0], b_t[g_, 1], ALU.add)
                o.then_inc(wide_b, 1)
                yield
                dve.wait_ge(ba_log, 3)
                link(STT(out=ba_ln[:], in0=ba[:], scalar=0.0, in1=ba_ln[:], op0=ALU.max, op1=ALU.add))
                TS(dv["lnb"][:], ba_ln[:, :, 0:H], -1.0, None, ALU.mult)
                STT(out=dn_g[:], in0=ba_ln[:, :, H:2 * H], scalar=-1.0,
                    in1=ea_row[:].unsqueeze(1).to_broadcast([P, M, H]), op0=ALU.mult, op1=ALU.mult).then_inc(dn_gate, 1)
                yield
                for q in range(4):
                    yield
                dve.wait_ge(dn_cum, 1)
                nc.vector.tensor_copy(dv["cum"][:], side[:, 0, 0:M * H].rearrange("p (m h) -> p m h", h=H))
                nc.vector.tensor_copy(dn_tail[:], side[:, 0, M * H:M * H + H]).then_inc(dn_gate, 1)
                dve.wait_ge(tok_done, 1)
                for step in fractions(0):
                    pass
                yield
                for n in range(15, S5_SLOT):
                    yield
                for t in range(ST):
                    b, c, j = t % 2, t // SJ, t % SJ
                    two = lambda v: v.unsqueeze(1).to_broadcast([P, 2, T])
                    dve.wait_ge(s5_bu, t + 1)
                    dve.wait_ge(s5_sin, t + 1)
                    if t:
                        dve.wait_ge(s5_x, t)
                    bu = side[:, 0].rearrange("p (n t) -> p n t", t=T)
                    TT(p_c[:], bu, two(angle[:, b]), ALU.mult)
                    TT(p_s[:], bu, two(sn[:, b]), ALU.mult).then_inc(s5_rot, 1)
                    dve.wait_ge(s5_rot, t + 1)
                    TT(rot[:, 0], p_c[:, 0], p_s[:, 1], ALU.add)
                    TT(rot[:, 1], p_c[:, 1], p_s[:, 0], ALU.subtract).then_inc(s5_in, 1)
                    yield
                    step = fractions(t + 1) if t + 1 < ST else iter(())
                    next(step, None)
                    dve.wait_ge(s5_in, t + 1)
                    for n in range(2):
                        o = nc.vector.tensor_tensor_scan(rot[:, n], s5p[:, 0, t:t + 1].to_broadcast([P, T]), rot[:, n],
                                                         0.0, ALU.mult, ALU.add)
                        if n:
                            o.then_inc(s5_z, 1)
                        next(step, None)
                    yield
                    dve.wait_ge(s5_z, t + 1)
                    TT(p_c[:], rot[:], two(angle[:, b]), ALU.mult)
                    TT(p_s[:], rot[:], two(sn[:, b]), ALU.mult).then_inc(s5_out, 1)
                    dve.wait_ge(s5_out, t + 1)
                    if t >= 2:
                        dve.wait_ge(s5_y, t - 1)
                    TT(state[:, b, 0], p_c[:, 0], p_s[:, 1], ALU.subtract)
                    TT(state[:, b, 1], p_c[:, 1], p_s[:, 0], ALU.add).then_inc(s5_x, 1)
                    if t and j == 0:
                        outputs(c - 1)
                    yield
                outputs(CT - 1)
                for n in range(S5_REST):
                    yield
                for c in range(NU):
                    chunk_lo(o0 + c, B, KW * c, None, None, None, KD, side_T)
                    yield

            def delta(o0):
                for j in range(2 * H // KW):
                    yield
                dve.wait_ge(qk_ss, 2 * H // KW)
                TS(dn_ss[:], dnb(0)[:, 0:M * 2 * H].rearrange("p (m n) -> p m n", m=M), EPS, None, ALU.add).then_inc(dn_ssin, 1)
                dve.wait_ge(dn_lns, 1)
                lq, lk = dn_ss[:, :, 0:H], dn_ss[:, :, H:2 * H]
                dve.wait_ge(dn_gate, 2)
                STT(out=dv["colq"][:], in0=lq, scalar=-0.5, in1=dv["cum"][:], op0=ALU.mult, op1=ALU.add)
                STT(out=dv["colk"][:], in0=lk, scalar=-0.5, in1=dv["cum"][:], op0=ALU.mult, op1=ALU.add)
                link(STT(out=dv["rowk"][:], in0=lk, scalar=-0.5, in1=dv["cum"][:], op0=ALU.mult, op1=ALU.subtract))
                TS(dv["colq"][:], dv["colq"][:], Q_LOG, None, ALU.add)
                TT(dv["colk"][:], dv["colk"][:], dv["lnb"][:], ALU.add)
                TT(dn_tail[:], dn_tail[:], dv["rowk"][:, 0], ALU.add).then_inc(dn_rows, 1)
                dve.wait_ge(dn_fac, 1)
                TS(dv["nwk"][:], dv["wk"][:], -1.0, None, ALU.mult).then_inc(dn_nwk, 1)
                yield
                four = lambda v: v.unsqueeze(1).to_broadcast([P, 4, P])
                bank = lambda b: dnb(b).rearrange("p (u c) -> p u c", c=P)

                def results(b):
                    dve.wait_ge(left, NU + NQ + NZ)
                    dve.wait_ge(dn_rs, b + 1)
                    for u in range(4):
                        z = zs[:, u % 2, (2 * b + u // 2) * P:(2 * b + u // 2 + 1) * P]
                        o = STT(out=z, in0=dn_o[:, u], scalar=dn_rstd[:, u:u + 1], in1=z, op0=ALU.mult, op1=ALU.mult)
                    o.then_inc(dn_y, 1)

                dve.wait_ge(masks, mask_total)
                for b in range(H // 2):
                    dve.wait_ge(dn_expo, b + 1)
                    if b:
                        dve.wait_ge(dn_LA, b)
                        results(b - 1)
                        dve.wait_ge(dn_y, b)
                    TT(dec[:, 0], bank(0), four(expo_mask[:, 0]), ALU.add)
                    TT(dec[:, 1], bank(1), four(expo_mask[:, 1]), ALU.add).then_inc(dn_masked, 1)
                    yield
                    yield
                    dve.wait_ge(dn_kk, b + 1)
                    dve.wait_ge(dn_decay, b + 1)
                    TT(LT[:], bank(0), dec[:, 0], ALU.mult)
                    TT(AT[:], bank(1), dec[:, 1], ALU.mult).then_inc(dn_LA, 1)
                    dve.wait_ge(dn_LA, b + 1)
                    link(TT(LK[:], LT[:], four(lev_mask[:, 0]), ALU.mult))
                    TT(DT[:], four(ident[:]), LK[:], ALU.subtract).then_inc(dn_D, 1)
                    yield
                    dve.wait_ge(dn_DT, b + 1)
                    nc.vector.tensor_copy(DD[:], bank(0))
                    TT(LK[:], LT[:], four(lev_mask[:, 1]), ALU.mult).then_inc(dn_lev, 1)
                    yield
                    for l in range(1, LEVELS):
                        yield
                        dve.wait_ge(dn_X, (LEVELS - 1) * b + l)
                        dve.wait_ge(dn_lev, LEVELS * b + l)
                        o = TT(DT[:], DT[:], bank(1), ALU.subtract)
                        if l + 1 < LEVELS:
                            TT(DD[:], DD[:], bank(0), ALU.subtract)
                            o = TT(LK[:], LT[:], four(lev_mask[:, l + 1]), ALU.mult)
                        o.then_inc(dn_lev, 1)
                        yield
                    yield
                    dve.wait_ge(dn_St, b + 1)
                    nc.vector.tensor_copy(dn_o[:].rearrange("p (e m) c -> p m e c", m=M)[:, 0],
                                          dnb(1)[:, 0:2 * P].rearrange("p (e c) -> p e c", c=P)).then_inc(dn_o0, 1)
                    yield
                    dve.wait_ge(dn_nwk, 1)
                    dve.wait_ge(dn_kS, b + 1)
                    for e in range(2):
                        h = 2 * b + e
                        STT(out=rhs1[:, e], in0=dnb(0)[:, e * P:(e + 1) * P], scalar=dv["nwk"][:, 1, h:h + 1],
                            in1=vb[:, 2 * e + 1], op0=ALU.mult, op1=ALU.add)
                        o = TS(qS[:, e], dnb(0)[:, (2 + e) * P:(3 + e) * P], dv["wq"][:, 1, h:h + 1], None, ALU.mult)
                    o.then_inc(dn_rhs, 1)
                    yield
                    yield
                    dve.wait_ge(dn_out, b + 1)
                    dve.wait_ge(dn_rhs, b + 1)
                    TT(dn_o[:].rearrange("p (e m) c -> p m e c", m=M)[:, 1],
                       dnb(1)[:, 0:2 * P].rearrange("p (e c) -> p e c", c=P), qS[:], ALU.add).then_inc(dn_ofull, 1)
                    dve.wait_ge(dn_sq, 4 * (b + 1))
                    if b:
                        dve.wait_ge(dn_rs, b)
                    TS(dn_mean[:], dn_ssq[:], 1.0 / P, EPS, ALU.mult, ALU.add).then_inc(dn_ms, 1)
                    yield
                results(H // 2 - 1)
                yield
                for c in range(NZ):
                    chunk_lo(o0 + NU + c, B, KW * (NU + c), None, None, vec_at["dn_norm_w"], 1)
                    yield

            def outputs(c):
                dve.wait_ge(s5_y, SJ * (c + 1))
                if c % KW == 0:
                    dve.wait_ge(skip_done, c // KW + 1)
                u = ud[:, :, c * P:(c + 1) * P]
                TT(u, side[:, 1, 0:M * P].rearrange("p (m c) -> p m c", m=M), u, ALU.add).then_inc(s5_res, 1)

            def mix1(xdst, tail):
                g0, e0, o0, xc = (at["mix1"][k] for k in ("g", "ev", "op", "x"))
                g = g0
                o_m = o0 + NU + NZ
                scan, rule = s5(o0), delta(o0)

                def convolve(q, k):
                    n = KW * q + k
                    for back in range(1, DTAPS):
                        o = STT(out=qkvT[:, n, back:T], in0=tp[:, k, 0:T - back], scalar=dtaps[:, DTAPS - 1 - back, n:n + 1],
                                in1=qkvT[:, n, back:T], op0=ALU.mult, op1=ALU.add)
                        if back < DTAPS - 1:
                            link(o)
                    return o

                def leave(c, kind):
                    def tail(pos):
                        if pos == EVAC + 1 and kind == "u":
                            dve.wait_ge(left, c + 1)
                            dve.wait_ge(d_full, 16)
                            TT(ud[:, :, cols(c)], evac[:], d_row[:, cols(c)].unsqueeze(1).to_broadcast([P, M, NW]),
                               ALU.mult).then_inc(skip_done, 1)
                        if kind == "qkv" and pos in range(SPLIT, SPLIT + KW):
                            if pos == SPLIT:
                                dve.wait_ge(dn_tap, c - NU + 1)
                            o = convolve(c - NU, pos - SPLIT)
                            if pos == SPLIT + KW - 1:
                                o.then_inc(dn_conved, 1)
                    return tail

                older = no_tail
                for c, (kind, _) in enumerate(W_IN):
                    for pos in range(GC):
                        lo(g)
                        tail(pos)
                        older(pos + GC)
                        if g - g0 >= LEAD:
                            next(scan, None)
                        if g - g0 >= LEAD + DN_SLOT:
                            next(rule, None)
                        g += 1
                    older = tail if c else no_tail
                    tail = leave(c, kind)
                for _ in scan:
                    pass
                older = no_tail
                gg = g0 + GC * len(W_IN)

                def linear(j):
                    def tail(pos):
                        if pos == EVAC:
                            dve.wait_ge(used, gg + GH * (2 * j + 1))
                            dve.wait_ge(gate_sig, j + 1)
                            TT(gs[:, :, cols(j)], acc[:, 0], gs[:, :, cols(j)], ALU.mult).then_inc(glu_a, 1)
                    return tail

                def glu(j):
                    def tail(pos):
                        if pos == EVAC + 1:
                            dve.wait_ge(glu_sig, j + 1)
                            dve.wait_ge(glu_a, j + 1)
                            TT(gs[:, :, cols(j)], gs[:, :, cols(j)], evac[:], ALU.mult).then_inc(s5_part, 1)
                    return tail

                def both(j):
                    def tail(pos):
                        if pos == EVAC:
                            dve.wait_ge(used, gg + GH * (2 * XC + j + 1))
                            dve.wait_ge(gate_sig, XC + j + 1)
                            link(TT(gd[:, :, cols(j)], acc[:, j % 2], gd[:, :, cols(j)], ALU.mult))
                            dve.wait_ge(s5_part, j + 1)
                            TT(gs[:, :, cols(j)], gs[:, :, cols(j)], gd[:, :, cols(j)], ALU.add).then_inc(merged, 1)
                        if pos == SPLIT:
                            chunk_lo(o_m + j, A, KW * j)
                    return tail

                tail = no_tail
                for c in range(3 * XC):
                    if c == 2 * XC:
                        for _ in rule:
                            pass
                    for pos in range(GH):
                        lo(g)
                        tail(pos)
                        older(pos + GH)
                        if c < 2 * XC:
                            next(rule, None)
                        g += 1
                    older = tail
                    tail = both(c - 2 * XC) if c >= 2 * XC else glu(c // 2) if c % 2 else linear(c // 2)
                for c in range(XC):
                    for pos in range(GC):
                        lo(g)
                        tail(pos)
                        if c == 0 and pos < GH:
                            older(pos + GH)
                        g += 1
                    tail = x_tail(g, o_m + XC + c, xc + c, c, 1.0, xdst, weight_of(NEXT["mix1"]), (x_again, 16 * M))
                return norm_tail(NEXT["mix1"], tail)

            def attention():
                for _ in range(ATT_WARM):
                    yield
                dve.wait_ge(lr_split, 1)
                TT(lr_lo[:], lr_w[:], lr_hi[:].bitcast(F32), ALU.subtract).then_inc(lr_split, 1)
                nc.vector.memset(sc[:], 0.0).then_inc(g_scin, 1)
                yield
                yield
                yield
                dve.wait_ge(al_in, 1)
                STT(out=lt[:], in0=la[:], scalar=-1.0, in1=la[:], op0=ALU.mult, op1=ALU.max).then_inc(al_abs, 1)
                dve.wait_ge(al_exp, 1)
                TS(lt[:], lt[:], 1.0, None, ALU.add).then_inc(al_one, 1)
                yield
                dve.wait_ge(al_ln, 1)
                link(STT(out=la[:], in0=la[:], scalar=0.0, in1=lt[:], op0=ALU.min, op1=ALU.subtract))
                for h in range(GHD):
                    for n in range(LN):
                        t = slice(n * LC, (n + 1) * LC)
                        o = nc.vector.tensor_tensor_scan(lt[:, h, t], ones[:, 0:1].to_broadcast([P, LC]), la[:, h, t],
                                                         0.0, ALU.mult, ALU.add)
                o.then_inc(al_cum, 1)
                n = ATT_WARM + 4
                while n < ATT_SLOT:
                    n += 1
                    yield
                dve.wait_ge(al_dec, 1)
                dve.wait_ge(copied, copied0 + 4)
                TT(qd[:], qd[:], la[:], ALU.mult).then_inc(qk_dec, 1)
                dve.wait_ge(al_dec, 2)
                TT(ki[:], kt[:], la[:], ALU.mult).then_inc(qk_dec, 1)
                dve.wait_ge(qk_dec, 2)
                by_chunk = lt[:].rearrange("p h (n t) -> p (h n) t", t=LC)
                dve.wait_ge(al_cum, 1)
                TT(la[:].rearrange("p h (n t) -> p (h n) t", t=LC), by_chunk[:, :, LC - 1:LC].to_broadcast([P, GHD * LN, LC]),
                   by_chunk, ALU.subtract).then_inc(qk_dec, 1)
                yield
                dve.wait_ge(al_dec, 3)
                TT(kt[:], kt[:], la[:], ALU.mult).then_inc(qk_dec, 1)
                yield
                yield
                dve.wait_ge(g_sc, 1)
                dve.wait_ge(g_scin, 1)
                for m in range(M):
                    o = nc.vector.copy_predicated(sc[:, m], score_mask[:].unsqueeze(1).to_broadcast([P, GHD, P]),
                                                  side[:, m].rearrange("p (h i) -> p h i", i=P))
                o.then_inc(g_scin, 1)
                yield
                for n in range(LN - 1):
                    dve.wait_ge(g_kv, n + 1)
                    kv = lambda h: side[:, h // 2, (h % 2) * GV:(h % 2 + 1) * GV]
                    if n:
                        dve.wait_ge(g_S, n)
                    for h in range(GHD):
                        if n:
                            o = STT(out=Sg[:, n, h], in0=Sg[:, n - 1, h], scalar=gdec[:, h, n:n + 1], in1=kv(h),
                                    op0=ALU.mult, op1=ALU.add)
                        else:
                            o = nc.vector.tensor_copy(Sg[:, n, h], kv(h))
                    o.then_inc(g_S, 1)
                    yield
                yield
                dve.wait_ge(g_oin, M)
                TS(g_mean[:], g_ssq[:], 1.0 / GV, EPS, ALU.mult, ALU.add).then_inc(g_ms, 1)
                yield

            def mix2(xdst, tail):
                g0, e0, o0, xc = (at["mix2"][k] for k in ("g", "ev", "op", "x"))
                g = g0
                side_work = attention()

                def pool(n, half_):
                    ks = slice(KW * n, KW * (n + 1))
                    u, s, t = u2T[:, ks], pool_a[:, ks], pool_b[:, ks]
                    src_ = u
                    lv = range(0, 2 * n + 1) if half_ == 0 else range(2 * n + 1, 2 * n + 2)
                    k0 = 0 if half_ == 0 else KW // 2
                    for l in lv:
                        d = 1 << l
                        if l:
                            src_ = (s, t)[(l - 1) % 2]
                        dst = (s, t)[l % 2]
                        nc.vector.tensor_copy(dst[:, k0:, 0:d], src_[:, k0:, 0:d])
                        link(TT(dst[:, k0:, d:T], src_[:, k0:, d:T], src_[:, k0:, 0:T - d], ALU.add))
                    l = lv[-1]
                    w = 2 << l
                    k = slice(k0, k0 + KW // 2)
                    sm, o = (s, t)[l % 2][:, k], (t, s)[l % 2][:, k]
                    link(STT(out=o, in0=sm, scalar=1.0 / w, in1=u[:, k], op0=ALU.mult, op1=ALU.subtract))
                    c = rcnt[:, l].unsqueeze(1).to_broadcast([P, KW // 2, 16])
                    link(TT(o[:, :, 0:16], sm[:, :, 0:16], c, ALU.mult))
                    return TT(o[:, :, 0:16], o[:, :, 0:16], u[:, k, 0:16], ALU.subtract)

                def leave(c, kind, n):
                    def tail(pos):
                        if kind == "u" and pos == SPLIT + 1:
                            dve.wait_ge(copied, copied0 + n + 1)
                            dve.wait_ge(lr_mm, 1)
                            dve.wait_ge(masks, mask_total)
                            link(pool(n, 0))
                        if kind == "u" and pos == SPLIT + 2:
                            pool(n, 1).then_inc(pooled, 1)
                        if kind == "u" and pos == GC + 2:
                            chunk_lo(o0 + n, A, KW * n, None, None, vec_at["pool_scale_2"] + KW * n)
                        if kind == "g" and pos == EVAC + 1:
                            dve.wait_ge(g_rs, 1)
                            dve.wait_ge(left, left0 + c + 1)
                            for m in range(M):
                                for h in range(NW // GV * n, NW // GV * (n + 1)):
                                    v = slice(h * GV, (h + 1) * GV)
                                    o = STT(out=vv[:, m, v], in0=vv[:, m, v], scalar=g_rstd[:, m, h:h + 1], in1=sg[:, m, v],
                                            op0=ALU.mult, op1=ALU.mult)
                            o.then_inc(g_y, 1)
                        if kind == "g" and pos == SPLIT + 1:
                            chunk_lo(o0 + VC + n, A, KW * (VC + n), None, None, vec_at["gla_norm_2"], GV // P)
                    return tail

                older, n = no_tail, {}
                for c, (kind, _) in enumerate(W_IN2):
                    for pos in range(GC):
                        lo(g)
                        tail(pos)
                        older(pos + GC)
                        if g - g0 >= LEAD:
                            next(side_work, None)
                        g += 1
                    older = tail if c else no_tail
                    tail = leave(c, kind, n.get(kind, 0))
                    n[kind] = n.get(kind, 0) + 1
                for _ in side_work:
                    pass
                for c in range(XC):
                    for pos in range(GC):
                        lo(g)
                        tail(pos)
                        g += 1
                    tail = x_tail(g, o0 + 2 * VC + c, xc + c, c, 1.0, xdst, weight_of(NEXT["mix2"]), x_after)
                return norm_tail(NEXT["mix2"], tail)

            dve.wait_ge(vec_in, 2 + TAPS)
            for c in range(XC):
                chunk_lo(c, first_x, KW * c, weight_of(phases[1]), chunk=(tp, side_T)[c % 2])
            tail = norm_tail(phases[1], no_tail)
            x_after = (x_full[XC - 1], 16)
            for ph in phases[1:]:
                if ph in ("ffn1", "ffn2", "ffn3"):
                    tail = ffn(ph, ph == "ffn1", 1.0 if ph == "ffn1" else 0.5, B if ph in NEXT else None, A, tail, x_after)
                elif ph == "mix1":
                    tail = mix1(B if ph in NEXT else None, tail)
                elif ph == "mix2":
                    tail = mix2(B if ph in NEXT else None, tail)
                x_after = (scaled, M) if ph == "ffn1" and two_norms else (x_new, at[ph]["x"] + size[ph]["x"])
            for pos in range(GC):
                tail(pos)
            dve.wait_ge(rs, NORMS)
            dve.wait_ge(fnorm_full, 32 if two_norms and phases[-1] != "ffn1" else 16)
            dve.wait_ge(sq, sq_count["result"])
            for m in range(M):
                apply_norm("result", m)

        @block.tensor
        def _(pe):
            def products(g, xT, k0, s, first, last, i=None, per=0):
                pe.wait_ge(lo_done, n_at(g + 1, i, per))
                r = g % RING
                for kk in range(KG):
                    for m in range(M):
                        xh, xl = (xT[h][:, k0 + kk, m * P:(m + 1) * P] for h in (0, 1))
                        st, en = first and kk == 0, last and kk == KG - 1
                        nc.tensor.matmul(acc[:, s, m], xh, w_hi[:, r, kk], start=st, stop=False)
                        nc.tensor.matmul(acc[:, s, m], xh, w_lo[:, r, kk], start=False, stop=False)
                        op = nc.tensor.matmul(acc[:, s, m], xl, w_hi[:, r, kk], start=False, stop=en)
                op.then_inc(used, 1)

            def transpose_chunk(source, ready, tp_read, dst=tp):
                pe.wait_ge(*ready)
                if tp_read is not None:
                    pe.wait_ge(*tp_read)
                for k in range(KW):
                    for m in range(M):
                        op = nc.tensor.transpose(dst[:, k, m * P:(m + 1) * P], source[:, m, k * P:(k + 1) * P], ident[:])
                op.then_inc(tp_full, 1)

            def no_tail(pos):
                pass

            def x_tail(xc, c, tp_read):
                def tail(pos):
                    if pos == FLIP:
                        transpose_chunk(x[:, :, cols(c)], (x_new, xc + 1), tp_read)
                return tail

            def ffn(ph, conv, end, xT, xdst_op, aT, tail, free, tp_read):
                at_ph = at[ph]
                g0, op, sr, xc, q0, cv = (at_ph[k] for k in ("g", "op", "src", "x", "gate", "conv"))

                def pair(g, free, before, operand=None, gate_step=None, i=None):
                    for pos in range(2 * GC):
                        s, k = pos // GC, pos % GC
                        if k == 0 and free[s] is not None:
                            pe.wait_ge(*free[s])
                        if operand is not None and s == 0 and k % 2 == 0:
                            pe.wait_ge(op_T, operand + k // 2 + 1)
                        products(g + pos, xT, KG * k, s, k == 0, k == GC - 1, i, 2 * GC)
                        before(pos)
                        if pos == GC + FLIP and conv:
                            transpose_chunk(evac[:], *gate_step)

                def pair_tail(sr, op, cv, i=None):
                    def tail(pos):
                        if pos == FLIP:
                            if conv:
                                transpose_chunk(evac[:], (src, n_at(sr, i, 2)), (conved, n_at(cv, i, 2)))
                            else:
                                transpose_chunk(evac[:], (src, n_at(sr, i, 1)), (op_T, n_at(op, i, 1)))
                    return tail

                per = 2 if conv else 1
                for p, n in enumerate(PARTS):
                    gate_step = ((src, sr + 1), tp_read)
                    pair(g0, free, tail, xdst_op if p == 0 else None, gate_step)
                    with pe.Fori(1, n) as i:
                        if conv:
                            busy = [(src, i * 2 + (sr - 1)), (src, i * 2 + sr)]
                            step = ((src, i * 2 + (sr + 1)), (op_T, i + op))
                            last = pair_tail(sr, None, cv - 1, i)
                        else:
                            busy = [(gated, i + q0), (src, i + sr)]
                            step = None
                            last = pair_tail(sr, op - 1, None, i)
                        pair(g0, busy, last, None, step, i)
                    g0, sr, op, q0, cv = g0 + 2 * GC * n, sr + per * n, op + n, q0 + n, cv + 2 * n
                    tail = pair_tail(sr, op - 1, cv - 1)
                    free = [(src, sr - 1) if conv else (gated, q0), (src, sr)]
                    tp_read = (op_T, op)
                    GP = KW * n // KG
                    for c in range(XC):
                        if free[c % 2] is not None:
                            pe.wait_ge(*free[c % 2])
                        for pos in range(GP):
                            if c == 0 and pos % 2 == 0:
                                pe.wait_ge(op_T, op - n + pos // 2 + 1)
                            products(g0, aT, KG * pos, c % 2, pos == 0, pos == GP - 1)
                            g0 += 1
                            tail(pos)
                        free[c % 2] = (x_new, xc + c + 1)
                        tail = no_tail
                        if p == len(PARTS) - 1 and end:
                            tail = x_tail(xc + c, c, tp_read)
                            op += 1
                            tp_read = (op_T, op)
                    xc += XC
                return tail, free, tp_read, op - XC

            MM, TR = nc.tensor.matmul, nc.tensor.transpose

            def small(out_col, bank, xT, hi_, lo_, n):
                for m in range(M):
                    o = side[:, bank, out_col + m * n:out_col + (m + 1) * n]
                    for k in range(KD):
                        xh, xl = (xT[h][:, k, m * P:(m + 1) * P] for h in (0, 1))
                        MM(o, xh, hi_[:, k], start=k == 0, stop=False)
                        MM(o, xh, lo_[:, k], start=False, stop=False)
                        op = MM(o, xl, hi_[:, k], start=False, stop=k == KD - 1)
                return op

            def s5(xT, x_op):
                for n in range(4):
                    yield
                pe.wait_ge(op_T, x_op + XC)
                pe.wait_ge(par_done, 1)
                for i, t in enumerate((row["mag"], row["f"], row_fhi[:].bitcast(F32), row["flo"], row["cr"], row["ci"])):
                    op = TR(side[:, 0, i * ST:(i + 1) * ST], t if i == 2 else t[:], ident[0:ST, 0:ST])
                op.then_inc(par_T, 1)
                yield
                pe.wait_ge(ba_split, 2)
                pe.wait_ge(op_T, x_op + XC)
                small(0, 1, xT, ba_hi, ba_lo, 2 * H).then_inc(ba_mm, 1)
                for n in range(5, 10):
                    yield
                pe.wait_ge(wide_b, 1)
                for q in range(4):
                    for b in range(2):
                        if q:
                            pe.wait_ge(wide_in, 2 * (q - 1) + b + 1)
                        else:
                            pe.wait_ge(*((par_in, 1), (ba_in, 1))[b])
                        for k in range(4):
                            c = 4 * b + k
                            t = (b_wide[:, q, SJ * c:SJ * (c + 1)].rearrange("p t g h -> p (t g h)") if q < 2 else
                                 c_wide[:, q - 2, c].rearrange("p g s -> p (g s)"))
                            op = TR(side[:, b, k * P:(k + 1) * P], t, ident[:])
                        op.then_inc(wide_T, 1)
                    yield
                pe.wait_ge(dn_gate, 1)
                pe.wait_ge(masks, mask_total)
                pe.wait_ge(wide_in, 8)
                for m in range(M):
                    MM(side[:, 0, m * H:(m + 1) * H], triu[:], dn_g[:, m], start=True, stop=True)
                MM(side[:, 0, M * H:(M + 1) * H], ones[:], dn_g[:, 0], start=True, stop=True).then_inc(dn_cum, 1)
                yield
                for n in range(15, S5_SLOT - 1):
                    yield
                pe.wait_ge(dn_gate, 2)

                def y(t):
                    c, j = t // SJ, t % SJ
                    pe.wait_ge(s5_x, t + 1)
                    if c and j == 0:
                        pe.wait_ge(s5_res, c)
                    for m in range(M):
                        for n in range(2):
                            op = MM(side[:, 1, m * P + j * SW:m * P + (j + 1) * SW], state[:, t % 2, n, m * P:(m + 1) * P],
                                    s5_C[:, c, n, j * SW:(j + 1) * SW], start=n == 0, stop=n == 1)
                    op.then_inc(s5_y, 1)

                def inputs(t):
                    c, j = t // SJ, t % SJ
                    if t % (SJ * KW) == 0:
                        pe.wait_ge(copied, c // KW + 1)
                    if t:
                        pe.wait_ge(s5_rot, t)
                    s = slice(j * SW, (j + 1) * SW)
                    for n in range(2):
                        op = MM(side[:, 0, n * T:(n + 1) * T], s5_B[s, c, n], uT[s, c], start=True, stop=True)
                    op.then_inc(s5_bu, 1)

                inputs(0)
                yield
                for t in range(ST):
                    yield
                    if t:
                        y(t - 1)
                    yield
                    if t + 1 < ST:
                        inputs(t + 1)
                    yield
                y(ST - 1)
                for n in range(S5_REST):
                    yield
                for c in range(NU):
                    pe.wait_ge(*((op_T, x_op + XC + c) if c else (s5_gelu, 1)))
                    for k in range(KW):
                        for m in range(M):
                            op = TR(side_T[:, k, m * P:(m + 1) * P], ud[:, m, (KW * c + k) * P:(KW * c + k + 1) * P], ident[:])
                    op.then_inc(s5_T, 1)
                    yield

            def delta(readers, e_y):
                pe.wait_ge(dn_conved, NQ)
                for j in range(2 * H // KW):
                    pe.wait_ge(qk_sq, j + 1)
                    for k in range(KW):
                        for m in range(M):
                            o = m * 2 * H + KW * j + k
                            op = MM(dnb(0)[:, o:o + 1], sq4[:, k, m * P:(m + 1) * P], ones[:, 0:1], start=True, stop=True)
                    op.then_inc(qk_ss, 1)
                    yield
                yield
                pe.wait_ge(dn_rows, 1)
                pe.wait_ge(qkv_act, NQ)
                tok_of = lambda m: slice(m * P, (m + 1) * P)
                unit_of = lambda u: slice(u * P, (u + 1) * P)
                for b in range(H // 2):
                    unit = [(h, m) for h in (2 * b, 2 * b + 1) for m in range(M)]
                    if b:
                        pe.wait_ge(dn_newin, 2 * b)
                        pe.wait_ge(dn_ofull, b)
                    for w, name in enumerate(("colk", "colq")):
                        for u, (h, m) in enumerate(unit):
                            op = MM(dnb(w)[:, unit_of(u)], dv[name][:, m, h:h + 1].to_broadcast([P, P]), ident[:],
                                    start=True, stop=True)
                    op.then_inc(dn_expo, 1)
                    yield
                    pe.wait_ge(dn_masked, b + 1)
                    for u, (h, m) in enumerate(unit):
                        TR(dnb(0)[:, unit_of(u)], qkvT[:, 2 * H + h, tok_of(m)], ident[:])
                    for e in range(2):
                        op = TR(dnb(1)[:, unit_of(e)], qkvT[:, H + 2 * b + e, tok_of(0)], ident[:])
                    op.then_inc(dn_vk, 1)
                    yield
                    pe.wait_ge(dn_vb, b + 1)
                    for w in range(2):
                        for u, (h, m) in enumerate(unit):
                            op = MM(dnb(w)[:, unit_of(u)], qkvT[:, H + h, tok_of(m)], qkvT[:, (1 - w) * H + h, tok_of(m)],
                                    start=True, stop=True)
                    op.then_inc(dn_kk, 1)
                    yield
                    pe.wait_ge(dn_D, b + 1)
                    for u in range(4):
                        op = TR(dnb(0)[:, unit_of(u)], DT[:, u], ident[:])
                    op.then_inc(dn_DT, 1)
                    yield
                    for l in range(1, LEVELS):
                        pe.wait_ge(dn_lev, LEVELS * b + l)
                        for u in range(4):
                            op = MM(dnb(0)[:, unit_of(u)], LK[:, u], DD[:, u], start=True, stop=True)
                        op.then_inc(dn_P, 1)
                        yield
                        pe.wait_ge(dn_Pin, (LEVELS - 1) * b + l)
                        for u in range(4):
                            op = MM(dnb(1)[:, unit_of(u)], PP[:, u], DT[:, u], start=True, stop=True)
                        if l + 1 < LEVELS:
                            for u in range(4):
                                op = MM(dnb(0)[:, unit_of(u)], DT[:, u], PP[:, u], start=True, stop=True)
                        op.then_inc(dn_X, 1)
                        yield
                    pe.wait_ge(dn_lev, LEVELS * (b + 1))
                    for e in range(2):
                        op = MM(dnb(0)[:, unit_of(e)], DT[:, 2 * e], vb[:, 2 * e], start=True, stop=True)
                    op.then_inc(dn_new, 1)
                    yield
                    pe.wait_ge(dn_newin, 2 * b + 1)
                    for e in range(2):
                        MM(dnb(0)[:, unit_of(e)], ktail[:, e], vnew[:, e], start=True, stop=True)
                    for e in range(2):
                        op = MM(dnb(1)[:, unit_of(e)], AT[:, 2 * e], vnew[:, e], start=True, stop=True)
                    op.then_inc(dn_St, 1)
                    yield
                    pe.wait_ge(dn_Sin, b + 1)
                    pe.wait_ge(dn_o0, b + 1)
                    for w in range(2):
                        for e in range(2):
                            op = MM(dnb(0)[:, unit_of(2 * w + e)], qkvT[:, (1 - w) * H + 2 * b + e, tok_of(1)], dn_S[:, e],
                                    start=True, stop=True)
                    op.then_inc(dn_kS, 1)
                    yield
                    pe.wait_ge(dn_rhs, b + 1)
                    for e in range(2):
                        op = MM(dnb(0)[:, unit_of(e)], DT[:, 2 * e + 1], rhs1[:, e], start=True, stop=True)
                    op.then_inc(dn_new, 1)
                    yield
                    pe.wait_ge(dn_newin, 2 * b + 2)
                    for e in range(2):
                        op = MM(dnb(1)[:, unit_of(e)], AT[:, 2 * e + 1], vnew[:, 2 + e], start=True, stop=True)
                    op.then_inc(dn_out, 1)
                    yield
                yield
                for c in range(NZ):
                    transpose_chunk(zs[:, :, cols(c)], (dn_y, H // 2),
                                    readers[e_y + c - 1] if c else (dn_ofull, H // 2))
                    yield

            def mix1(end, xT, x_op, yT, tail, free, tp_read):
                g, o0, xc = (at["mix1"][k] for k in ("g", "op", "x"))
                readers = ([(copied, c + 1) for c in range(NU)] + [(dn_conved, q + 1) for q in range(NQ)]
                           + [(op_T, o0 + NU + i + 1) for i in range(NZ + 2 * XC)])
                e_y = NU + NQ
                e_m = e_y + NZ
                scan, rule = s5(xT, x_op), delta(readers, e_y)
    
                def leave(c, kind):
                    def tail(pos):
                        if pos == FLIP and kind in ("u", "qkv"):
                            transpose_chunk(evac[:], (left, c + 1), readers[c - 1] if c else tp_read)
                    return tail

                for c, (kind, _) in enumerate(W_IN):
                    for pos in range(GC):
                        if pos == 0 and (c >= 2 or free[c % 2] is not None):
                            pe.wait_ge(*((left, c - 1) if c >= 2 else free[c % 2]))
                        if c == 0 and pos % 2 == 0:
                            pe.wait_ge(op_T, x_op + pos // 2 + 1)
                        products(g, xT, KG * pos, c % 2, pos == 0, pos == GC - 1)
                        tail(pos)
                        next(scan, None)
                        if g - at["mix1"]["g"] >= DN_SLOT:
                            next(rule, None)
                        g += 1
                    tail = leave(c, kind)
                for _ in scan:
                    pass
                C = len(W_IN)
                older = no_tail

                def both(j):
                    def tail(pos):
                        if pos == FLIP:
                            transpose_chunk(gs[:, :, cols(j)], (merged, j + 1), readers[e_m + j - 1])
                    return tail

                for c in range(3 * XC):
                    j = c // 2 if c < 2 * XC else c - 2 * XC
                    if c == 2 * XC:
                        for _ in rule:
                            pass
                    if c < 2 * XC:
                        busy = ((glu_a, glu_sig)[c % 2], j) if j else (left, C - 1 + c)
                        k0, op0 = 0, o0
                    else:
                        busy = (merged, j - 1) if j >= 2 else ((glu_a, glu_sig)[j], XC)
                        k0, op0 = KD // 2, o0 + NU
                    pe.wait_ge(*busy)
                    for pos in range(GH):
                        if c in (0, 2 * XC) and pos % 2 == 0:
                            pe.wait_ge(op_T, op0 + pos // 2 + 1)
                        products(g, yT, k0 + KG * pos, c % 2, pos == 0, pos == GH - 1)
                        tail(pos)
                        if c < 2 * XC:
                            next(rule, None)
                        g += 1
                    tail = both(j) if c >= 2 * XC else no_tail
                for c in range(XC):
                    pe.wait_ge(*((merged, XC - 1 + c) if c < 2 else (x_new, xc + c - 1)))
                    for pos in range(GC):
                        if c == 0 and pos % 2 == 0:
                            pe.wait_ge(op_T, o0 + NU + NZ + pos // 2 + 1)
                        products(g, xT, KG * pos, c % 2, pos == 0, pos == GC - 1)
                        tail(pos)
                        g += 1
                    tail = x_tail(xc + c, c, readers[e_m + XC + c - 1])
                return tail, [(x_new, xc + XC - 1), (x_new, xc + XC)], readers[-1], o0 + NU + NZ + XC

            def attention(xT, x_op):
                for _ in range(ATT_WARM):
                    yield
                yield
                pe.wait_ge(lr_split, 2)
                pe.wait_ge(op_T, x_op + XC)
                small(0, 0, xT, lr_hi, lr_lo, GR).then_inc(lr_mm, 1)
                yield
                pe.wait_ge(lr_in, 1)
                for m in range(M):
                    op = TR(side[0:GR, 0, m * P:(m + 1) * P], lr2[:, m], ident[:])
                op.then_inc(lr_T, 1)
                yield
                pe.wait_ge(lr_Tin, 1)
                pe.wait_ge(wal_full, 16)
                for h in range(GHD):
                    op = MM(side[:, h // 2, (h % 2) * T:(h % 2 + 1) * T], wal[:, h * P:(h + 1) * P], lrT[:], start=True, stop=True)
                op.then_inc(al_mm, 1)
                yield
                n = ATT_WARM + 4
                while n < ATT_SLOT:
                    n += 1
                    yield
                yield
                yield
                pe.wait_ge(qk_dec, 4)
                for m in range(M):
                    for h in range(GHD):
                        op = TR(side[:, m, h * P:(h + 1) * P], kt[:, h, m * P:(m + 1) * P], ident[:])
                op.then_inc(gk_T, 1)
                yield
                pe.wait_ge(gk_in, 1)
                for m in range(M):
                    for h in range(GHD):
                        op = MM(side[:, m, h * P:(h + 1) * P], ki[:, h, m * P:(m + 1) * P], qd[:, h, m * P:(m + 1) * P],
                                start=True, stop=True)
                op.then_inc(g_sc, 1)
                yield
                pe.wait_ge(left, left0 + VC + 2 + VC)
                out_of = lambda h: (h // 2, slice((h % 2) * GV, (h % 2 + 1) * GV))
                for n in range(LN - 1):
                    pe.wait_ge(*((g_S, n) if n else (g_scin, 2)))
                    t = slice(n % 2 * LC, (n % 2 + 1) * LC)
                    for h in range(GHD):
                        b, w = out_of(h)
                        op = MM(side[:, b, w], ktT[t, n // 2, h], vv[t, n // 2, h * GV:(h + 1) * GV], start=True, stop=True)
                    op.then_inc(g_kv, 1)
                    yield
                pe.wait_ge(g_S, LN - 1)
                for m in range(M):
                    if m:
                        pe.wait_ge(g_oin, m)
                    for h in range(GHD):
                        b, w = out_of(h)
                        v = vv[:, m, h * GV:(h + 1) * GV]
                        if m:
                            MM(side[:, b, w], sc[:, m, h], v, start=True, stop=False)
                        for e in range(P // LC):
                            n = P // LC * m + e
                            rows = slice(e * LC, (e + 1) * LC)
                            if not m:
                                MM(side[rows, b, w], sc[:, m, h, rows], v, start=True, stop=n == 0)
                            if n:
                                op = MM(side[rows, b, w], qd[:, h, n * LC:(n + 1) * LC], Sg[:, n - 1, h], start=False, stop=True)
                    op.then_inc(g_o, 1)
                    yield

            def mix2(end, xT, x_op, yT, tail, free, tp_read):
                g, o0, xc = (at["mix2"][k] for k in ("g", "op", "x"))
                order = ["u0", "p0", "u1", "p1", "q0", "k0", "y0", "y1"]
                reader = dict(u0=(copied, copied0 + 1), p0=(op_T, o0 + 1), u1=(copied, copied0 + 2), p1=(op_T, o0 + 2),
                              q0=(copied, copied0 + 3), k0=(copied, copied0 + 4), y0=(op_T, o0 + 3), y1=(op_T, o0 + 4))
                before = lambda e: reader[order[order.index(e) - 1]] if e != order[0] else tp_read
                side_work = attention(xT, x_op)

                def leave(c, kind, n):
                    def tail(pos):
                        if pos == FLIP and kind in ("u", "q", "k"):
                            transpose_chunk(evac[:], (left, left0 + c + 1), before(f"{kind}{n}"))
                        if pos == GC and kind == "u":
                            pe.wait_ge(pooled, n + 1)
                            pe.wait_ge(wp_full, 16 * PG)
                            pe.wait_ge(*before(f"p{n}"))
                            for e in range(2):
                                t = (pool_b, pool_a)[e]
                                for d in range(PD // P):
                                    for k in range(PD // P):
                                        op = MM(tp[:, 2 * e + d], wp[n][:, e, k, d * P:(d + 1) * P], t[:, KW * n + 2 * e + k],
                                                start=k == 0, stop=k == PD // P - 1)
                            op.then_inc(tp_full, 1)
                        if pos == FLIP + 1 and kind == "g":
                            transpose_chunk(vv[:, :, cols(n)], (g_y, n + 1), before(f"y{n}"))
                    return tail

                older, n = no_tail, {}
                for c, (kind, _) in enumerate(W_IN2):
                    for pos in range(GC):
                        if pos == 0 and (c >= 2 or free[c % 2] is not None):
                            pe.wait_ge(*((left, left0 + c - 1) if c >= 2 else free[c % 2]))
                        if c == 0 and pos % 2 == 0:
                            pe.wait_ge(op_T, x_op + pos // 2 + 1)
                        products(g, xT, KG * pos, c % 2, pos == 0, pos == GC - 1)
                        tail(pos)
                        older(pos + GC)
                        next(side_work, None)
                        g += 1
                    older = tail if c else no_tail
                    tail = leave(c, kind, n.get(kind, 0))
                    n[kind] = n.get(kind, 0) + 1
                for _ in side_work:
                    pass
                C = len(W_IN2)
                for c in range(XC):
                    pe.wait_ge(*((left, left0 + C - 1 + c) if c < 2 else (x_new, xc + c - 1)))
                    for pos in range(GC):
                        if c == 0 and pos % 2 == 0:
                            pe.wait_ge(op_T, o0 + pos // 2 + 1)
                        products(g, yT, KG * pos, c % 2, pos == 0, pos == GC - 1)
                        tail(pos)
                        g += 1
                    tail = x_tail(xc + c, c, (op_T, o0 + 2 * VC + c))
                return tail, [(x_new, xc + XC - 1), (x_new, xc + XC)], (op_T, o0 + 2 * VC + XC), o0 + 2 * VC

            pe.wait_ge(consts, 2)
            pe.wait_ge(vec_full, 16 * len(VECS))
            nc.tensor.transpose(side[:, 0, 0:VEC_ROWS], vecs[:], ident[0:VEC_ROWS, 0:VEC_ROWS]).then_inc(vec_T, 1)
            pe.wait_ge(taps_full, 16)
            for t in range(TAPS):
                nc.tensor.transpose(side[:, 0, P * (t + 1):P * (t + 1) + FT], tap_rows[:, t], ident[0:FT, 0:FT]).then_inc(vec_T, 1)
            pe.wait_ge(dtap_full, 16)
            nc.tensor.transpose(side[:, 1, 0:DTAPS * QT], dtap_rows[:], ident[0:DTAPS * QT, 0:DTAPS * QT]).then_inc(vec_T, 1)
            pe.wait_ge(vec_in, 2 + TAPS)
            for c in range(XC):
                transpose_chunk(x[:, :, cols(c)], (x_full[c], 16), (op_T, c - 1) if c >= 2 else None, (tp, side_T)[c % 2])
            tail, free, tp_read, operand = no_tail, [None, None], (op_T, XC), 0
            for ph in phases[1:]:
                if ph in ("ffn1", "ffn2", "ffn3"):
                    tail, free, tp_read, operand = ffn(ph, ph == "ffn1", ph in NEXT, B, operand, A, tail, free, tp_read)
                elif ph == "mix1":
                    tail, free, tp_read, operand = mix1(True, A, operand, B, tail, free, tp_read)
                elif ph == "mix2":
                    tail, free, tp_read, operand = mix2(True, B, operand, A, tail, free, tp_read)


_INS = ["x", "mix_norm_w", "w_in", "s5_log_dt", "s5_a_re", "s5_a_im", "s5_b_re", "s5_b_im", "s5_c_re", "s5_c_im", "s5_d",
        "s5_glu_w", "dn_conv_w", "dn_a_log", "dn_dt_bias", "dn_norm_w", "dn_proj_w", "w_out", "ffn_norm_w", "ffn_up",
        "ffn_conv_w", "ffn_down", "final_norm_w", "ffn1_norm_2", "ffn1_w_in_2", "ffn1_w_out_2", "mix_norm_2", "w_in_mix_2",
        "w_pool_2", "pool_scale_2", "w_alpha_2", "b_alpha_2", "gla_norm_2", "w_out_mix_2", "ffn2_norm_2", "ffn2_w_in_2",
        "ffn2_w_out_2", "final_norm_2"]


def kernel(**inputs):
    import numpy as _np
    import concourse.bacc as _bacc
    from concourse import mybir as _mybir
    from concourse.bass_utils import run_bass_kernel_spmd as _run

    nc = _bacc.Bacc("TRN2", target_bir_lowering=False, num_devices=1)
    arrays, aps = {}, {}
    for name in _INS:
        v = _np.ascontiguousarray(inputs[name])
        arrays[f"in_{name}_dram"] = v
        aps[name] = nc.dram_tensor(f"in_{name}_dram", v.shape, _mybir.dt.from_np(v.dtype), kind="ExternalInput").ap()
    out = nc.dram_tensor("out_0_dram", inputs["x"].shape, _mybir.dt.float32, kind="ExternalOutput").ap()
    two_block_kernel(nc, aps, out)
    return _run(nc, [arrays], core_ids=[0]).results[0]["out_0_dram"]
```
